# Optimizing a Trainium2 kernel written in Bass

```python
import numpy as np
import jax, jax.numpy as jnp
from jax import lax

D_MODEL = 1024
BATCH = 1
SEQ = 512
DEPTH = 2

N_A_LAYERS = max(1, DEPTH // 2)
N_B_LAYERS = DEPTH - N_A_LAYERS

D_RNN = 1536
N_RNN_BLOCKS = 16
RNN_BLOCK = D_RNN // N_RNN_BLOCKS
CONV_WIDTH = 4
RGLRU_C = 8.0

D_FF = -(-8 * D_MODEL // (3 * 256)) * 256

N_HEADS = 16
N_KV_GROUPS = 4
HEADS_PER_GROUP = N_HEADS // N_KV_GROUPS
D_QK = 96
D_V = 64
ROPE_DIMS = D_QK // 4
ROPE_THETA = 500000.0
CMP_BLOCK = 32
CMP_STRIDE = 16
CMP_HIDDEN = 256
SEL_BLOCK = 64
SEL_TOPK = 8
WINDOW = 512
Q_BLOCK = 128
N_BRANCH = 3
EPS = 1e-6


def rmsnorm(x, g):
    xf = x.astype(jnp.float32)
    y = xf * lax.rsqrt(jnp.mean(xf * xf, axis=-1, keepdims=True) + EPS)
    return (y * g.astype(jnp.float32)).astype(x.dtype)

def apply_partial_rope(x):
    S = x.shape[1]
    half = ROPE_DIMS // 2
    inv = ROPE_THETA ** (-jnp.arange(half, dtype=jnp.float32) * 2.0 / ROPE_DIMS)
    ang = jnp.arange(S, dtype=jnp.float32)[:, None] * inv[None, :]
    bshape = (1, S) + (1,) * (x.ndim - 3) + (half,)
    cos = jnp.cos(ang).reshape(bshape)
    sin = jnp.sin(ang).reshape(bshape)
    xr = x[..., :ROPE_DIMS].astype(jnp.float32)
    x1, x2 = xr[..., :half], xr[..., half:]
    rot = jnp.concatenate([x1 * cos - x2 * sin, x2 * cos + x1 * sin], axis=-1)
    return jnp.concatenate([rot.astype(x.dtype), x[..., ROPE_DIMS:]], axis=-1)

def masked_softmax(s, mask):
    s = jnp.where(mask, s, -jnp.inf)
    m = jnp.max(s, axis=-1, keepdims=True)
    m = jnp.where(jnp.isfinite(m), m, 0.0)
    e = jnp.where(mask, jnp.exp(s - m), 0.0)
    d = jnp.sum(e, axis=-1, keepdims=True)
    return e / jnp.where(d > 0, d, 1.0)

def swiglu(h, w_gu, w_down):
    u = h @ w_gu
    g, v = u[..., :D_FF], u[..., D_FF:]
    return (jax.nn.silu(g) * v) @ w_down

def rglru_mixer(h, w_in, conv_w, conv_b, w_ra, b_ra, w_ix, b_ix, lam, w_out):
    B, S, _ = h.shape
    u = h @ w_in
    xb, yb = u[..., :D_RNN], u[..., D_RNN:]
    y = jax.nn.gelu(yb)
    xc = lax.conv_general_dilated(
        xb, conv_w[:, None, :], window_strides=(1,), padding=[(CONV_WIDTH - 1, 0)],
        dimension_numbers=('NWC', 'WIO', 'NWC'), feature_group_count=D_RNN) + conv_b
    xg = xc.reshape(B, S, N_RNN_BLOCKS, RNN_BLOCK)
    r = jax.nn.sigmoid(jnp.einsum('bsni,nij->bsnj', xg, w_ra) + b_ra).reshape(B, S, D_RNN)
    i = jax.nn.sigmoid(jnp.einsum('bsni,nij->bsnj', xg, w_ix) + b_ix).reshape(B, S, D_RNN)
    log_a = -RGLRU_C * r.astype(jnp.float32) * jax.nn.softplus(-lam.astype(jnp.float32))
    a = jnp.exp(log_a)
    mult = jnp.sqrt(-jnp.expm1(2.0 * log_a))
    bx = mult * (i * xc).astype(jnp.float32)

    def step(hprev, inp):
        a_t, b_t = inp
        hn = a_t * hprev + b_t
        return hn, hn

    _, hs = lax.scan(step, jnp.zeros((B, D_RNN), jnp.float32),
                     (a.transpose(1, 0, 2), bx.transpose(1, 0, 2)))
    rec = hs.transpose(1, 0, 2).astype(h.dtype)
    return (rec * y) @ w_out

def compress_blocks(raw, pos, w1, w2):
    B, S, G, Dh = raw.shape
    nc = (S - CMP_BLOCK) // CMP_STRIDE + 1
    idx = np.arange(nc)[:, None] * CMP_STRIDE + np.arange(CMP_BLOCK)[None, :]
    blk = raw[:, idx] + pos[None, None, :, None, :]
    blk = blk.transpose(0, 1, 3, 2, 4).reshape(B, nc, G, CMP_BLOCK * Dh)
    return jax.nn.gelu(blk @ w1) @ w2

def shared_kv(h, kv_norm_g, kv_w, cmp_pos_k, cmp_w1_k, cmp_w2_k, cmp_pos_v, cmp_w1_v, cmp_w2_v):
    B, S, _ = h.shape
    hn = rmsnorm(h, kv_norm_g)
    kv = hn @ kv_w
    gk, gv = N_KV_GROUPS * D_QK, N_KV_GROUPS * D_V
    sizes = [gk, gv, gk, gv, gk, gv]
    offs = np.concatenate([[0], np.cumsum(sizes)])
    parts = [kv[..., offs[j]:offs[j + 1]] for j in range(6)]
    k_cmp, v_cmp, k_sel, v_sel, k_win, v_win = [
        p.reshape(B, S, N_KV_GROUPS, -1) for p in parts]
    kc = compress_blocks(k_cmp, cmp_pos_k, cmp_w1_k, cmp_w2_k)
    vc = compress_blocks(v_cmp, cmp_pos_v, cmp_w1_v, cmp_w2_v)
    ks = apply_partial_rope(k_sel)
    kw = apply_partial_rope(k_win)
    pad = ((0, 0), (WINDOW, 0), (0, 0), (0, 0))
    kw_pad = jnp.pad(kw, pad)
    vw_pad = jnp.pad(v_win, pad)
    return (kc, vc, ks, v_sel, kw_pad, vw_pad)

def nsa_mixer(h, w_q, gate_bias, w_o, kc, vc, ks, vs, kw_pad, vw_pad):
    B, S, _ = h.shape
    G, HPG = N_KV_GROUPS, HEADS_PER_GROUP
    nc = kc.shape[1]
    ns = S // SEL_BLOCK
    nq = S // Q_BLOCK
    k_top = min(SEL_TOPK, ns)
    cs = np.arange(nc) * CMP_STRIDE
    ss = np.arange(ns) * SEL_BLOCK
    overlap = jnp.asarray(((cs[:, None] < ss[None, :] + SEL_BLOCK) &
                           (cs[:, None] + CMP_BLOCK > ss[None, :])).astype(np.float32))
    c_end = jnp.arange(nc) * CMP_STRIDE + CMP_BLOCK - 1
    blk_ids = jnp.arange(ns)

    u = h @ w_q
    q = (u[..., :N_HEADS * D_QK] * (D_QK ** -0.5)).reshape(B, S, G, HPG, D_QK)
    gates = jax.nn.sigmoid(u[..., N_HEADS * D_QK:] + gate_bias).reshape(B, S, G, HPG, N_BRANCH)
    q_rope = apply_partial_rope(q)

    def per_seq(args):
        qn, qr, gt, kc_b, vc_b, ks_s, vs_s, kw_b, vw_b = args
        ks_blk = ks_s.reshape(ns, SEL_BLOCK, G, D_QK).transpose(2, 0, 1, 3)
        vs_blk = vs_s.reshape(ns, SEL_BLOCK, G, D_V).transpose(2, 0, 1, 3)
        gidx = jnp.arange(G)[None, :, None]

        def per_block(bargs):
            qn_t, qr_t, g_t, qi = bargs
            s0 = qi * Q_BLOCK
            t = s0 + jnp.arange(Q_BLOCK)
            s_c = jnp.einsum('tghd,cgd->tghc', qn_t, kc_b).astype(jnp.float32)
            mask_c = (c_end[None, :] <= t[:, None])[:, None, None, :]
            p_c = masked_softmax(s_c, mask_c)
            o_c = jnp.einsum('tghc,cgv->tghv', p_c.astype(vc_b.dtype), vc_b)
            imp = jnp.einsum('tghc,cn->tgn', p_c, overlap)
            cur = (t // SEL_BLOCK)[:, None, None]
            visible = (blk_ids * SEL_BLOCK)[None, None, :] <= t[:, None, None]
            forced = (blk_ids == 0) | (blk_ids == cur) | (blk_ids == cur - 1)
            score = jnp.where(forced, jnp.inf, jnp.where(visible, imp, -jnp.inf))
            _, idx = lax.top_k(score, k_top)
            kg = ks_blk[gidx, idx]
            vg = vs_blk[gidx, idx]
            s_s = jnp.einsum('tghd,tgjld->tghjl', qr_t, kg).astype(jnp.float32)
            pos = idx[..., None] * SEL_BLOCK + jnp.arange(SEL_BLOCK)
            mask_s = (pos <= t[:, None, None, None]).reshape(Q_BLOCK, G, 1, k_top * SEL_BLOCK)
            p_s = masked_softmax(s_s.reshape(Q_BLOCK, G, HPG, k_top * SEL_BLOCK), mask_s)
            p_s = p_s.reshape(Q_BLOCK, G, HPG, k_top, SEL_BLOCK)
            o_s = jnp.einsum('tghjl,tgjlv->tghv', p_s.astype(vg.dtype), vg)
            kwin = lax.dynamic_slice_in_dim(kw_b, s0, WINDOW + Q_BLOCK, axis=0)
            vwin = lax.dynamic_slice_in_dim(vw_b, s0, WINDOW + Q_BLOCK, axis=0)
            p_pos = s0 - WINDOW + jnp.arange(WINDOW + Q_BLOCK)
            mask_w = ((p_pos[None, :] >= 0) & (p_pos[None, :] <= t[:, None]) &
                      (p_pos[None, :] > t[:, None] - WINDOW))[:, None, None, :]
            s_w = jnp.einsum('tghd,sgd->tghs', qr_t, kwin).astype(jnp.float32)
            p_w = masked_softmax(s_w, mask_w)
            o_w = jnp.einsum('tghs,sgv->tghv', p_w.astype(vwin.dtype), vwin)
            return g_t[..., 0:1] * o_c + g_t[..., 1:2] * o_s + g_t[..., 2:3] * o_w

        out = lax.map(per_block, (
            qn.reshape(nq, Q_BLOCK, G, HPG, D_QK),
            qr.reshape(nq, Q_BLOCK, G, HPG, D_QK),
            gt.reshape(nq, Q_BLOCK, G, HPG, N_BRANCH),
            jnp.arange(nq)))
        return out.reshape(S, N_HEADS * D_V)

    o = lax.map(per_seq, (q, q_rope, gates, kc, vc, ks, vs, kw_pad, vw_pad))
    return o @ w_o

def first_inputs(seed: int = 0) -> dict:
    key = jax.random.key(seed)
    ks = jax.random.split(key, 32)
    f32 = jnp.float32
    res = (2.0 * DEPTH) ** -0.5

    def nrm(k, shape, scale):
        return jax.random.normal(k, shape, f32) * scale

    kv_cols = N_BRANCH * N_KV_GROUPS * (D_QK + D_V)
    q_cols = N_HEADS * D_QK + N_HEADS * N_BRANCH
    u = jax.random.uniform(ks[9], (N_A_LAYERS, D_RNN), f32, 0.9, 0.999)
    s = u ** (1.0 / RGLRU_C)
    a_lambda = jnp.log(s) - jnp.log1p(-s)
    return {
        'x': nrm(ks[0], (BATCH, SEQ, D_MODEL), 1.0),
        'norm_g': 1.0 + nrm(ks[1], (DEPTH, 2, D_MODEL), 0.02),
        'ffn_w_gu': nrm(ks[2], (DEPTH, D_MODEL, 2 * D_FF), D_MODEL ** -0.5),
        'ffn_w_down': nrm(ks[3], (DEPTH, D_FF, D_MODEL), res * D_FF ** -0.5),
        'a_w_in': nrm(ks[4], (N_A_LAYERS, D_MODEL, 2 * D_RNN), D_MODEL ** -0.5),
        'a_conv_w': nrm(ks[5], (N_A_LAYERS, CONV_WIDTH, D_RNN), CONV_WIDTH ** -0.5),
        'a_conv_b': nrm(ks[6], (N_A_LAYERS, D_RNN), 0.01),
        'a_w_ra': nrm(ks[7], (N_A_LAYERS, N_RNN_BLOCKS, RNN_BLOCK, RNN_BLOCK), RNN_BLOCK ** -0.5),
        'a_b_ra': nrm(ks[8], (N_A_LAYERS, N_RNN_BLOCKS, RNN_BLOCK), 0.01),
        'a_w_ix': nrm(ks[10], (N_A_LAYERS, N_RNN_BLOCKS, RNN_BLOCK, RNN_BLOCK), RNN_BLOCK ** -0.5),
        'a_b_ix': nrm(ks[11], (N_A_LAYERS, N_RNN_BLOCKS, RNN_BLOCK), 0.01),
        'a_lambda': a_lambda,
        'a_w_out': nrm(ks[12], (N_A_LAYERS, D_RNN, D_MODEL), res * D_RNN ** -0.5),
        'kv_norm_g': 1.0 + nrm(ks[13], (D_MODEL,), 0.02),
        'kv_w': nrm(ks[14], (D_MODEL, kv_cols), D_MODEL ** -0.5),
        'cmp_pos_k': nrm(ks[15], (CMP_BLOCK, D_QK), 0.1),
        'cmp_w1_k': nrm(ks[16], (CMP_BLOCK * D_QK, CMP_HIDDEN), (CMP_BLOCK * D_QK) ** -0.5),
        'cmp_w2_k': nrm(ks[17], (CMP_HIDDEN, D_QK), CMP_HIDDEN ** -0.5),
        'cmp_pos_v': nrm(ks[18], (CMP_BLOCK, D_V), 0.1),
        'cmp_w1_v': nrm(ks[19], (CMP_BLOCK * D_V, CMP_HIDDEN), (CMP_BLOCK * D_V) ** -0.5),
        'cmp_w2_v': nrm(ks[20], (CMP_HIDDEN, D_V), CMP_HIDDEN ** -0.5),
        'b_w_q': nrm(ks[21], (N_B_LAYERS, D_MODEL, q_cols), D_MODEL ** -0.5),
        'b_gate_bias': nrm(ks[22], (N_B_LAYERS, N_HEADS * N_BRANCH), 0.01),
        'b_w_o': nrm(ks[23], (N_B_LAYERS, N_HEADS * D_V, D_MODEL), res * (N_HEADS * D_V) ** -0.5),
        'final_g': 1.0 + nrm(ks[24], (D_MODEL,), 0.02),
    }

def first_block(x, norm_g, ffn_w_gu, ffn_w_down, a_w_in, a_conv_w, a_conv_b, a_w_ra, a_b_ra,
              a_w_ix, a_b_ix, a_lambda, a_w_out, kv_norm_g, kv_w, cmp_pos_k, cmp_w1_k, cmp_w2_k,
              cmp_pos_v, cmp_w1_v, cmp_w2_v, b_w_q, b_gate_bias, b_w_o, final_g):
    h = x
    shared = None
    for layer in range(DEPTH):
        hn = rmsnorm(h, norm_g[layer, 0])
        if layer < N_A_LAYERS:
            h = h + rglru_mixer(hn, a_w_in[layer], a_conv_w[layer], a_conv_b[layer],
                                a_w_ra[layer], a_b_ra[layer], a_w_ix[layer], a_b_ix[layer],
                                a_lambda[layer], a_w_out[layer])
        else:
            j = layer - N_A_LAYERS
            kc, vc, ks_, vs_, kw_pad, vw_pad = shared
            h = h + nsa_mixer(hn, b_w_q[j], b_gate_bias[j], b_w_o[j],
                              kc, vc, ks_, vs_, kw_pad, vw_pad)
        h = h + swiglu(rmsnorm(h, norm_g[layer, 1]), ffn_w_gu[layer], ffn_w_down[layer])
        if layer == N_A_LAYERS - 1:
            shared = shared_kv(h, kv_norm_g, kv_w, cmp_pos_k, cmp_w1_k, cmp_w2_k,
                               cmp_pos_v, cmp_w1_v, cmp_w2_v)
    return rmsnorm(h, final_g)


DEPTH_2 = 1

PLE_DIM = 256
RET_HEADS = 4
RET_DK = 128
RET_DV = 128
RET_CHUNK = 128
SWA_HEADS = 8
SWA_KV_HEADS = 2
SWA_GROUP = SWA_HEADS // SWA_KV_HEADS
SWA_HD = 64
WINDOW_2 = 128
N_GROUPS = 4
EXPERTS_PER_GROUP = 8
N_EXPERTS = N_GROUPS * EXPERTS_PER_GROUP
EXPERT_FF = 256
TOP_K = 2

RET_QK = RET_HEADS * RET_DK
RET_V = RET_HEADS * RET_DV
SWA_Q = SWA_HEADS * SWA_HD
SWA_KV = SWA_KV_HEADS * SWA_HD
IN_SPLITS = (RET_QK, RET_QK, RET_V, RET_V, SWA_Q, SWA_KV, SWA_KV, D_MODEL, D_MODEL)
IN_WIDTH = sum(IN_SPLITS)


def rms_norm(x, g):
    xf = x.astype(jnp.float32)
    y = xf * lax.rsqrt(jnp.mean(xf * xf, axis=-1, keepdims=True) + EPS)
    return (y * g.astype(jnp.float32)).astype(x.dtype)

def head_group_norm(y, g, b):
    yf = y.astype(jnp.float32)
    mu = jnp.mean(yf, axis=-1, keepdims=True)
    var = jnp.mean(jnp.square(yf - mu), axis=-1, keepdims=True)
    yn = ((yf - mu) * lax.rsqrt(var + EPS)).reshape(y.shape[0], y.shape[1], -1)
    return (yn * g.astype(jnp.float32) + b.astype(jnp.float32)).astype(y.dtype)

def retention_chunkwise(q, k, v):
    dtype = v.dtype
    q = q.astype(jnp.float32)
    k = k.astype(jnp.float32) * (RET_DK ** -0.5)
    v = v.astype(jnp.float32)
    b, s, h, dk = q.shape
    nc = s // RET_CHUNK
    q = q.reshape(b, nc, RET_CHUNK, h, dk)
    k = k.reshape(b, nc, RET_CHUNK, h, dk)
    v = v.reshape(b, nc, RET_CHUNK, h, RET_DV)
    log_gamma = jnp.log1p(-jnp.exp2(-5.0 - jnp.arange(h, dtype=jnp.float32)))
    pos = jnp.arange(RET_CHUNK, dtype=jnp.float32)
    diff = pos[:, None] - pos[None, :]
    decay_mask = jnp.where(diff[None] >= 0.0,
                           jnp.exp(jnp.maximum(diff, 0.0)[None] * log_gamma[:, None, None]), 0.0)
    scores = jnp.einsum('bnihd,bnjhd->bnhij', q, k) * decay_mask
    inner = jnp.einsum('bnhij,bnjhv->bnihv', scores, v)
    zeta = jnp.exp((RET_CHUNK - 1.0 - pos)[None, :] * log_gamma[:, None])
    chunk_kv = jnp.einsum('bnjhd,bnjhv,hj->nbhdv', k, v, zeta)
    chunk_decay = jnp.exp(RET_CHUNK * log_gamma)[None, :, None, None]

    def step(state, kv):
        return chunk_decay * state + kv, state

    _, prev_states = lax.scan(step, jnp.zeros_like(chunk_kv[0]), chunk_kv)
    xi = jnp.exp((pos + 1.0)[None, :] * log_gamma[:, None])
    cross = jnp.einsum('bnihd,nbhdv,hi->bnihv', q, prev_states, xi)
    return (inner + cross).reshape(b, s, h, RET_DV).astype(dtype)

def sliding_window_gqa(q, k, v, sinks):
    b, s = q.shape[:2]
    nb = s // WINDOW_2
    qb = q.reshape(b, nb, WINDOW_2, SWA_KV_HEADS, SWA_GROUP, SWA_HD)
    kb = k.reshape(b, nb, WINDOW_2, SWA_KV_HEADS, SWA_HD)
    vb = v.reshape(b, nb, WINDOW_2, SWA_KV_HEADS, SWA_HD)
    k_band = jnp.concatenate([jnp.concatenate([jnp.zeros_like(kb[:, :1]), kb[:, :-1]], axis=1), kb], axis=2)
    v_band = jnp.concatenate([jnp.concatenate([jnp.zeros_like(vb[:, :1]), vb[:, :-1]], axis=1), vb], axis=2)
    scores = jnp.einsum('bnqkgd,bnskd->bnkgqs', qb, k_band).astype(jnp.float32) * (SWA_HD ** -0.5)
    qi = jnp.arange(WINDOW_2)
    sj = jnp.arange(2 * WINDOW_2)
    rel = qi[:, None] + WINDOW_2 - sj[None, :]
    in_window = (rel >= 0) & (rel < WINDOW_2)
    key_exists = (jnp.arange(nb)[:, None] * WINDOW_2 - WINDOW_2 + sj[None, :]) >= 0
    mask = in_window[None] & key_exists[:, None, :]
    slopes = jnp.exp2(-8.0 * jnp.arange(1, SWA_HEADS + 1, dtype=jnp.float32) / SWA_HEADS)
    slopes = slopes.reshape(SWA_KV_HEADS, SWA_GROUP)
    alibi = -slopes[:, :, None, None] * rel.astype(jnp.float32)[None, None]
    scores = jnp.where(mask[None, :, None, None], scores + alibi[None, None], -1e30)
    sink = jnp.broadcast_to(sinks.astype(jnp.float32).reshape(1, 1, SWA_KV_HEADS, SWA_GROUP, 1, 1),
                            scores.shape[:-1] + (1,))
    probs = jax.nn.softmax(jnp.concatenate([scores, sink], axis=-1), axis=-1)[..., :-1]
    out = jnp.einsum('bnkgqs,bnskd->bnqkgd', probs.astype(v.dtype), v_band)
    return out.reshape(b, s, SWA_Q)

def hierarchical_moe(h, w_rg, b_rg, w_re, b_re, w_gate, w_up, w_down):
    b, s, d = h.shape
    hf = h.reshape(-1, d)
    g_prob = jax.nn.softmax((hf @ w_rg + b_rg).astype(jnp.float32), axis=-1)
    g_sel = jnp.argmax(g_prob, axis=-1)
    g_w = jnp.take_along_axis(g_prob, g_sel[:, None], axis=-1)
    e_logits = (hf @ w_re + b_re).astype(jnp.float32).reshape(-1, N_GROUPS, EXPERTS_PER_GROUP)
    e_in_group = jnp.take_along_axis(e_logits, g_sel[:, None, None], axis=1)[:, 0]
    top_p, top_i = lax.top_k(jax.nn.softmax(e_in_group, axis=-1), TOP_K)
    top_p = top_p / jnp.sum(top_p, axis=-1, keepdims=True)
    expert_id = g_sel[:, None] * EXPERTS_PER_GROUP + top_i
    combine = jnp.sum(jax.nn.one_hot(expert_id, N_EXPERTS, dtype=jnp.float32)
                      * (g_w * top_p)[..., None], axis=1)
    y = jnp.zeros_like(hf)
    for grp in range(N_GROUPS):
        sl = slice(grp * EXPERTS_PER_GROUP, (grp + 1) * EXPERTS_PER_GROUP)
        hid = jax.nn.silu(jnp.einsum('td,edf->tef', hf, w_gate[sl])) * jnp.einsum('td,edf->tef', hf, w_up[sl])
        y = y + jnp.einsum('tef,efd->td', hid * combine[:, sl, None].astype(hid.dtype), w_down[sl])
    return y.reshape(b, s, d)

def second_inputs(seed: int = 0) -> dict:
    key = jax.random.key(seed)
    ks = jax.random.split(key, 26)
    f32 = jnp.float32
    L = DEPTH_2

    def nrm(k, shape, scale):
        return jax.random.normal(k, shape, f32) * scale

    def gain(k, shape):
        return 1.0 + 0.02 * jax.random.normal(k, shape, f32)

    return dict(
        x=nrm(ks[0], (BATCH, SEQ, D_MODEL), 1.0),
        p=nrm(ks[1], (L, BATCH, SEQ, PLE_DIM), 1.0),
        mix_norm_g=gain(ks[2], (L, D_MODEL)),
        w_in=nrm(ks[3], (L, D_MODEL, IN_WIDTH), D_MODEL ** -0.5),
        ret_gn_g=gain(ks[4], (L, RET_V)),
        ret_gn_b=nrm(ks[5], (L, RET_V), 0.02),
        w_ret_o=nrm(ks[6], (L, RET_V, D_MODEL), RET_V ** -0.5),
        q_norm_g=gain(ks[7], (L, SWA_HD)),
        k_norm_g=gain(ks[8], (L, SWA_HD)),
        attn_sinks=nrm(ks[9], (L, SWA_HEADS), 0.5),
        w_swa_o=nrm(ks[10], (L, SWA_Q, D_MODEL), SWA_Q ** -0.5),
        w_out=nrm(ks[11], (L, D_MODEL, D_MODEL), D_MODEL ** -0.5),
        ffn_norm_g=gain(ks[12], (L, D_MODEL)),
        w_router_group=nrm(ks[13], (L, D_MODEL, N_GROUPS), D_MODEL ** -0.5),
        b_router_group=nrm(ks[14], (L, N_GROUPS), 0.01),
        w_router_expert=nrm(ks[15], (L, D_MODEL, N_EXPERTS), D_MODEL ** -0.5),
        b_router_expert=nrm(ks[16], (L, N_EXPERTS), 0.01),
        w_exp_gate=nrm(ks[17], (L, N_EXPERTS, D_MODEL, EXPERT_FF), D_MODEL ** -0.5),
        w_exp_up=nrm(ks[18], (L, N_EXPERTS, D_MODEL, EXPERT_FF), D_MODEL ** -0.5),
        w_exp_down=nrm(ks[19], (L, N_EXPERTS, EXPERT_FF, D_MODEL), EXPERT_FF ** -0.5),
        ple_gate_norm_g=gain(ks[20], (L, D_MODEL)),
        w_ple_gate=nrm(ks[21], (L, D_MODEL, D_MODEL), D_MODEL ** -0.5),
        w_ple=nrm(ks[22], (L, PLE_DIM, D_MODEL), PLE_DIM ** -0.5),
        ple_norm_g=gain(ks[23], (L, D_MODEL)),
    )

def second_block(x, p, mix_norm_g, w_in, ret_gn_g, ret_gn_b, w_ret_o, q_norm_g, k_norm_g, attn_sinks,
              w_swa_o, w_out, ffn_norm_g, w_router_group, b_router_group, w_router_expert,
              b_router_expert, w_exp_gate, w_exp_up, w_exp_down, ple_gate_norm_g, w_ple_gate,
              w_ple, ple_norm_g):
    b, s, _ = x.shape
    split_at = [int(c) for c in np.cumsum(IN_SPLITS)[:-1]]
    for i in range(DEPTH_2):
        h = rms_norm(x, mix_norm_g[i])
        z = h @ w_in[i]
        rq, rk, rv, rg, sq, sk, sv, gate_r, gate_s = jnp.split(z, split_at, axis=-1)
        y_r = retention_chunkwise(rq.reshape(b, s, RET_HEADS, RET_DK),
                                  rk.reshape(b, s, RET_HEADS, RET_DK),
                                  rv.reshape(b, s, RET_HEADS, RET_DV))
        y_r = (jax.nn.silu(rg) * head_group_norm(y_r, ret_gn_g[i], ret_gn_b[i])) @ w_ret_o[i]
        q = rms_norm(sq.reshape(b, s, SWA_HEADS, SWA_HD), q_norm_g[i])
        k = rms_norm(sk.reshape(b, s, SWA_KV_HEADS, SWA_HD), k_norm_g[i])
        v = sv.reshape(b, s, SWA_KV_HEADS, SWA_HD)
        y_s = sliding_window_gqa(q, k, v, attn_sinks[i]) @ w_swa_o[i]
        merged = jax.nn.sigmoid(gate_r) * y_r + jax.nn.sigmoid(gate_s) * y_s
        x = x + merged @ w_out[i]
        x = x + hierarchical_moe(rms_norm(x, ffn_norm_g[i]), w_router_group[i], b_router_group[i],
                                 w_router_expert[i], b_router_expert[i], w_exp_gate[i],
                                 w_exp_up[i], w_exp_down[i])
        ple = rms_norm(p[i] @ w_ple[i], ple_norm_g[i])
        x = x + jax.nn.sigmoid(rms_norm(x, ple_gate_norm_g[i]) @ w_ple_gate[i]) * ple
    return x


def setup_inputs(seed=0):
    out = dict(first_inputs(seed))
    for name, value in second_inputs(seed + 1).items():
        if name != "x":
            out[name + "_2"] = value
    return out


def reference(
    x, norm_g, ffn_w_gu, ffn_w_down, a_w_in, a_conv_w, a_conv_b, a_w_ra, a_b_ra, a_w_ix, a_b_ix,
    a_lambda, a_w_out, kv_norm_g, kv_w, cmp_pos_k, cmp_w1_k, cmp_w2_k, cmp_pos_v, cmp_w1_v,
    cmp_w2_v, b_w_q, b_gate_bias, b_w_o, final_g, p_2, mix_norm_g_2, w_in_2, ret_gn_g_2,
    ret_gn_b_2, w_ret_o_2, q_norm_g_2, k_norm_g_2, attn_sinks_2, w_swa_o_2, w_out_2,
    ffn_norm_g_2, w_router_group_2, b_router_group_2, w_router_expert_2, b_router_expert_2,
    w_exp_gate_2, w_exp_up_2, w_exp_down_2, ple_gate_norm_g_2, w_ple_gate_2, w_ple_2,
    ple_norm_g_2,
):
    x = first_block(
        x, norm_g, ffn_w_gu, ffn_w_down, a_w_in, a_conv_w, a_conv_b, a_w_ra, a_b_ra, a_w_ix,
        a_b_ix, a_lambda, a_w_out, kv_norm_g, kv_w, cmp_pos_k, cmp_w1_k, cmp_w2_k, cmp_pos_v,
        cmp_w1_v, cmp_w2_v, b_w_q, b_gate_bias, b_w_o, final_g,
    )
    return second_block(
        x, p_2, mix_norm_g_2, w_in_2, ret_gn_g_2, ret_gn_b_2, w_ret_o_2, q_norm_g_2, k_norm_g_2,
        attn_sinks_2, w_swa_o_2, w_out_2, ffn_norm_g_2, w_router_group_2, b_router_group_2,
        w_router_expert_2, b_router_expert_2, w_exp_gate_2, w_exp_up_2, w_exp_down_2,
        ple_gate_norm_g_2, w_ple_gate_2, w_ple_2, ple_norm_g_2,
    )


_drawn_inputs = setup_inputs


def setup_inputs(seed=0):
    import zlib

    import numpy as np

    out = dict(_drawn_inputs(seed))
    spreads = {}
    factors = {'a_b_ra': 8.0,
     'a_b_ix': 7.57,
     'kv_norm_g': 6.335,
     'cmp_pos_k': 7.055,
     'b_gate_bias': 8.0,
     'ret_gn_g_2': 3.393,
     'ret_gn_b_2': 8.392,
     'q_norm_g_2': 5.811,
     'k_norm_g_2': 8.0,
     'b_router_group_2': 28.444,
     'b_router_expert_2': 10.082,
     'ple_gate_norm_g_2': 22.514,
     'ple_norm_g_2': 19.645,
     'attn_sinks_2': 8.0,
     'ffn_norm_g_2': 2.714}
    for name, (base, spread) in spreads.items():
        noise = np.random.default_rng([zlib.crc32(name.encode()), seed]).standard_normal(out[name].shape)
        drawn = base * np.exp(spread * noise) if base else spread * noise
        out[name] = __import__('jax').numpy.asarray(drawn.astype(out[name].dtype))
    for name, factor in factors.items():
        out[name] = (out[name] * factor).astype(out[name].dtype)
    return out
```

```python
from contextlib import ExitStack

import numpy as np

import concourse.bass as bass
from concourse import mybir

F32 = mybir.dt.float32
F32R = mybir.dt.float32r
ALU = mybir.AluOpType
ACT = mybir.ActivationFunctionType
AX_X = mybir.AxisListType.X

P = 128
S = 512
D = 1024
KT = D // P
NT = S // P
EPS = 1e-6
NEG = -1e30

RNN_BLOCKS, RNN_W = 16, 96
FF_TILES = 2816 // P
HEADS, GROUPS, DQK, DV = 16, 4, 96, 64
HPG = HEADS // GROUPS
NCMP, CSTRIDE, CBLOCK = 31, 16, 32
NGATE = 3 * HEADS
RET_H = 4
SWA_H, SWA_HD, SWA_TILES = 8, 64, 4
EXPERTS, EGROUPS, EPG, EFF = 32, 4, 8, 256
NROUTE = EGROUPS + EXPERTS

WA, WB = 2048, 1024

A_RNN = 0
A_FF0 = A_RNN + RNN_BLOCKS
A_KCMP = A_FF0 + FF_TILES
A_VCMP = A_KCMP + 2
A_KSEL = A_VCMP + 1
A_KWIN = A_KSEL + 2
A_VNAT = A_KWIN + 2
A_W1K = A_VNAT + 2
A_W1V = A_W1K + 4
A_GATE = A_W1V + 4
A_Q = A_GATE + 1
A_WO = A_Q + HEADS // 2
A_FF1 = A_WO + 4
A_SKV = A_FF1 + FF_TILES
A_SQ = A_SKV + 1
A_RET = A_SQ + SWA_TILES
A_MRG = A_RET + 2 * RET_H
A_OUT = A_MRG + KT
A_ROUTE = A_OUT + 4
A_MOE = A_ROUTE + 1
A_PLE = A_MOE + 2 * EXPERTS
A_PG = A_PLE + 1
NA = A_PG + 4

B_RNN = 0
B_FF0 = B_RNN + RNN_BLOCKS
B_FF1 = B_FF0 + FF_TILES
B_MRG = B_FF1 + FF_TILES
B_MOE = B_MRG + KT
NB = B_MOE + 2 * EXPERTS

E_RNN = 0
E_FF0 = E_RNN + RNN_BLOCKS // 2
E_FF1 = E_FF0 + FF_TILES // 2
E_MOE = E_FF1 + FF_TILES // 2

(N_MIX0, N_FFN0, N_KV, N_MIX1, N_FFN1, N_FINAL, N_MIX2, N_MOE, N_PLEG, N_PLE) = range(10)

_SMALL = [("gain", 10 * KT), ("conv_w", 4 * RNN_BLOCKS), ("conv_b", RNN_BLOCKS), ("b_ra", RNN_BLOCKS),
          ("b_ix", RNN_BLOCKS), ("lam", RNN_BLOCKS), ("pos_k", CBLOCK), ("pos_v", CBLOCK),
          ("gate_b", NT * NGATE), ("ret_g", RET_H), ("ret_b", RET_H), ("q_g", 1), ("k_g", 1),
          ("sink", SWA_H), ("route_b", NT * NROUTE), ("w2k", 2 * DQK), ("w2v", 2 * DV)]
_CONST = [("eps", 1), ("ident", P), ("ones", P), ("halves", P), ("rot", DQK), ("causal", P),
          ("cmp_mask", NT * NCMP), ("prio_g", NT * EGROUPS), ("prio_e", NT * EPG)]


def _columns(parts):
    at, out = 0, {}
    for name, n in parts:
        out[name] = at
        at += n
    return out, at


SM, N_SMALL = _columns(_SMALL)
CN, N_CONST = _columns(_CONST)


class Steps:

    def __init__(self, eng, sem):
        self.eng, self.sem = eng, sem
        self.base = self.count = self.per = 0
        self.i = 0

    def __call__(self, ins):
        ins.then_inc(self.sem, 1)
        self.count += 1
        self.eng.wait_ge(self.sem, self.base + self.per * self.i + self.count)

    def enter(self, i, per):
        self.base += self.count
        self.i, self.per, self.count = i, per, 0

    def leave(self, trips):
        assert self.count == self.per, f"the loop takes {self.count} steps"
        self.base += self.per * trips
        self.i = self.per = self.count = 0


def build(nc, x_t, p_t, w_a, w_b, small, const, rope, decay, alibi, out_t):
    ctx = ExitStack()
    with ctx:
        def sem(name):
            return ctx.enter_context(nc.semaphore(name))

        def sb(name, shape, dt=F32, stack=None):
            return (stack or ctx).enter_context(nc.sbuf_tensor(name, shape, dt))

        a_raw = [sb(f"a_raw{i}", [P, WA]) for i in range(2)]
        a_hi = [sb(f"a_hi{i}", [P, WA], F32R) for i in range(2)]
        a_lo = [sb(f"a_lo{i}", [P, WA], F32R) for i in range(2)]
        b_raw = [sb(f"b_raw{i}", [P, WB]) for i in range(2)]
        b_hi = [sb(f"b_hi{i}", [P, WB], F32R) for i in range(2)]
        b_lo = [sb(f"b_lo{i}", [P, WB], F32R) for i in range(2)]
        h = sb("h", [P, KT, S])
        hn_hi = sb("hn_hi", [P, KT, S], F32R)
        hn_lo = sb("hn_lo", [P, KT, S], F32R)
        tmp = sb("tmp", [P, 2, S])
        sq = sb("sq", [P, 2, S])
        sd = sb("sd", [P, S])
        rstd = sb("rstd", [P, S])
        sm = sb("sm", [P, N_SMALL])
        cn = sb("cn", [P, N_CONST])
        bank = [ctx.enter_context(nc.psum_tensor(f"bank{i}", [P, S], F32)) for i in range(8)]

        def smc(name, k=0, n=1, rows=P):
            return sm[0:rows, SM[name] + k:SM[name] + k + n]

        def cnc(name, n, rows=P):
            return cn[0:rows, CN[name]:CN[name] + n]

        ident, ones = cnc("ident", P), cnc("ones", P)
        halves, rot = cnc("halves", P), cnc("rot", DQK, DQK)
        eps = cnc("eps", 1)

        with ExitStack() as st:
            rhid_hi = sb("rhid_hi", [P, 2, S], F32R, st)
            rhid_lo = sb("rhid_lo", [P, 2, S], F32R, st)
            xc, ybr, rg, ig, gx, aa, pp, mu, hs, gel = (
                sb(nm, [RNN_W, 2, S], F32, st) for nm in
                ("xc", "ybr", "rg", "ig", "gx", "aa", "pp", "mu", "hs", "gel"))
            xc_hi = sb("xc_hi", [RNN_W, 2, S], F32R, st)
            xc_lo = sb("xc_lo", [RNN_W, 2, S], F32R, st)
            spt = sb("spt", [RNN_W, 8, RNN_BLOCKS], F32, st)
        with ExitStack() as st:
            hid_hi = sb("hid_hi", [P, 2, S], F32R, st)
            hid_lo = sb("hid_lo", [P, 2, S], F32R, st)
            hid = sb("hid", [P, 2, S], F32, st)
            sg = sb("sg", [P, 2, S], F32, st)
            comb = sb("comb", [P, 2, S], F32, st)
            logit = sb("logit", [P, NT, NROUTE], F32, st)
            rt = sb("rt", [P, 24, NT], F32, st)
            rtg = sb("rtg", [P, 4, NT, EGROUPS], F32, st)
            rte = sb("rte", [P, 12, NT, EPG], F32, st)
            cmb = sb("cmb", [P, NT, EXPERTS], F32, st)
            cmbt = sb("cmbt", [EXPERTS, S], F32, st)
        with ExitStack() as st:
            kx = sb("kx", [DQK, 2, GROUPS, S], F32, st)
            vn = sb("vn", [P, 2, NT, GROUPS * DV], F32, st)
            kct = sb("kct", [DQK, GROUPS * NCMP], F32, st)
            vcn = sb("vcn", [NCMP, GROUPS, DV], F32, st)
            cs = sb("cs", [DQK, 2, S], F32, st)
            rtmp = sb("rtmp", [DQK, 2, S], F32, st)
            gates = sb("gates", [P, NT, NGATE], F32, st)
            with ExitStack() as s2:
                kraw = sb("kraw", [DQK, GROUPS, S], F32, s2)
                vraw = sb("vraw", [DV, GROUPS, S], F32, s2)
                xl = sb("xl", [DQK, 8, GROUPS * NCMP], F32, s2)
                xl_hi = sb("xl_hi", [DQK, 8, GROUPS * NCMP], F32R, s2)
                xl_lo = sb("xl_lo", [DQK, 8, GROUPS * NCMP], F32R, s2)
                chid = sb("chid", [P, 2, GROUPS * NCMP], F32, s2)
            with ExitStack() as s2:
                qb = sb("qb", [DQK, 4, 2, S], F32, s2)
            with ExitStack() as s2:
                qs = sb("qs", [DQK, 2, 2, S], F32, s2)
                vs = sb("vs", [P, 2, NT, DV], F32, s2)
                vcs = sb("vcs", [NCMP, DV], F32, s2)
                pm = sb("pm", [P, 2, S], F32, s2)
                pt = sb("pt", [P, 2, NT, S], F32, s2)
                pc = sb("pc", [P, NT, NCMP], F32, s2)
                ptc = sb("ptc", [NCMP, S], F32, s2)
                ast = sb("ast", [P, 2, 4], F32, s2)
                cst = sb("cst", [P, 4, NT], F32, s2)
        with ExitStack() as st:
            ys_hi = sb("ys_hi", [P, SWA_TILES, S], F32R, st)
            ys_lo = sb("ys_lo", [P, SWA_TILES, S], F32R, st)
            yr_hi = sb("yr_hi", [P, RET_H, S], F32R, st)
            yr_lo = sb("yr_lo", [P, RET_H, S], F32R, st)
            with ExitStack() as s2:
                al = sb("al", [P, SWA_H, 2 * P], F32, s2)
                sk = sb("sk", [P, S], F32, s2)
                sv = sb("sv", [P, NT, P], F32, s2)
                qn = sb("qn", [P, S], F32, s2)
                sp_ = sb("sp_", [P, 2, 2 * P], F32, s2)
                spt_ = sb("spt_", [P, 2, 2 * P], F32, s2)
                wst = sb("wst", [P, 2, 8], F32, s2)
            with ExitStack() as s2:
                dk = sb("dk", [P, RET_H, S], F32, s2)
                rq = sb("rq", [P, S], F32, s2)
                rk = sb("rk", [P, S], F32, s2)
                rv = sb("rv", [P, S], F32, s2)
                rgs = sb("rgs", [P, S], F32, s2)
                srt = sb("srt", [P, 2, S], F32, s2)
                ry = sb("ry", [P, S], F32, s2)
                ryc = sb("ryc", [P, S], F32, s2)
            with ExitStack() as s2:
                mg_hi = sb("mg_hi", [P, KT, S], F32R, s2)
                mg_lo = sb("mg_lo", [P, KT, S], F32R, s2)
                sgt = sb("sgt", [P, 2, S], F32, s2)
        with ExitStack() as st:
            ptr = sb("ptr", [P, 2, S], F32, st)
            ptr_hi = sb("ptr_hi", [P, 2, S], F32R, st)
            ptr_lo = sb("ptr_lo", [P, 2, S], F32R, st)
            ple = sb("ple", [P, KT, S], F32, st)
            pgs = sb("pgs", [P, 2, S], F32, st)

        q_dram = nc.dram_tensor("q_scratch", (HEADS, DQK, 2 * S), F32, kind="Internal").ap()
        c_dram = nc.dram_tensor("combine_scratch", (EXPERTS, S), F32, kind="Internal").ap()

        a_loaded = [sem(f"a_loaded{i}") for i in range(2)]
        b_loaded = [sem(f"b_loaded{i}") for i in range(2)]
        a_rounded, a_ready = sem("a_rounded"), sem("a_ready")
        b_rounded, b_ready = sem("b_rounded"), sem("b_ready")
        tile_ready, tile_free = sem("tile_ready"), sem("tile_free")
        y_ready, y_free = sem("y_ready"), sem("y_free")
        gate_done, hid_rounded, hid_ready = sem("gate_done"), sem("hid_rounded"), sem("hid_ready")
        params, consts, x_loaded = sem("params"), sem("consts"), sem("x_loaded")
        sq_ready, stat_mm, sd_ready = sem("sq_ready"), sem("stat_mm"), sem("sd_ready")
        hn_scaled, hn_rounded, hn_ready = sem("hn_scaled"), sem("hn_rounded"), sem("hn_ready")
        dve_step, act_step, dve_rstd, ple_mm = sem("dve_step"), sem("act_step"), sem("rstd_done"), sem("ple_mm")
        sp_exp, sp_one, sp_ln, sp_done = sem("sp_exp"), sem("sp_one"), sem("sp_ln"), sem("sp_done")
        xb_ready, yb_ready, xc_done, xc_rounded = sem("xb_ready"), sem("yb_ready"), sem("xc_done"), sem("xc_rounded")
        xc_ready, yb_copied, gx_done = sem("xc_ready"), sem("yb_copied"), sem("gx_done")
        gelu_done, decay_done, asq_done = sem("gelu_done"), sem("decay_done"), sem("asq_done")
        m2_done, mult_done, bx_done, scan_done, rec_done = (
            sem("m2_done"), sem("mult_done"), sem("bx_done"), sem("scan_done"), sem("rec_done"))
        rope_mm, rope_done = sem("rope_mm"), sem("rope_done")
        xl_done, xl_rounded, xl_ready, cmp_mm, chid_done, cmp_w2, cmp_done = (
            sem("xl_done"), sem("xl_rounded"), sem("xl_ready"), sem("cmp_mm"), sem("chid_done"),
            sem("cmp_w2"), sem("cmp_done"))
        gates_in, gates_done = sem("gates_in"), sem("gates_done")
        q_stored = [sem(f"q_stored{i}") for i in range(2)]
        q_staged = [sem(f"q_staged{i}") for i in range(2)]
        v_staged = sem("v_staged")
        sc_ready, mx_done, exp_done, pm_ready, tr_ready, pt_ready = (
            sem("sc_ready"), sem("mx_done"), sem("exp_done"), sem("pm_ready"), sem("tr_ready"), sem("pt_ready"))
        csc_ready, csub_done, cexp_done, cpm_ready, ctr_ready, cpt_ready = (
            sem("csc_ready"), sem("csub_done"), sem("cexp_done"), sem("cpm_ready"), sem("ctr_ready"), sem("cpt_ready"))
        o_ready, o_rounded, o_split = sem("o_ready"), sem("o_rounded"), sem("o_split")
        rope_loaded, alibi_loaded, decay_loaded, p_loaded = (
            sem("rope_loaded"), sem("alibi_loaded"), sem("decay_loaded"), sem("p_loaded"))
        qk_raw, qk_sq, qk_mm, qk_sd, qk_norm = (
            sem("qk_raw"), sem("qk_sq"), sem("qk_mm"), sem("qk_sd"), sem("qk_norm"))
        w_sc, w_mx, w_exp, w_pm, w_tr, w_pt, w_o, w_or, w_os = (
            sem("w_sc"), sem("w_mx"), sem("w_exp"), sem("w_pm"), sem("w_tr"), sem("w_pt"), sem("w_o"),
            sem("w_o_rounded"), sem("w_o_split"))
        r_in, r_gate, r_sc, r_dec, r_o, r_y, r_mean, r_c, r_sq, r_var, r_sd, r_g, r_rounded, r_split = (
            sem("r_in"), sem("r_gate"), sem("r_sc"), sem("r_dec"), sem("r_o"), sem("r_y"), sem("r_mean"),
            sem("r_c"), sem("r_sq"), sem("r_var"), sem("r_sd"), sem("r_g"), sem("r_rounded"), sem("r_split"))
        mg_gate, mg_sum, mg_rounded, mg_ready = sem("mg_gate"), sem("mg_sum"), sem("mg_rounded"), sem("mg_ready")
        rt_exp, rt_in, rt_done, cmbt_mm, cmbt_done, comb_stored = (
            sem("rt_exp"), sem("rt_in"), sem("rt_done"), sem("cmbt_mm"), sem("cmbt_done"), sem("comb_stored"))
        comb_loaded = [sem(f"comb_loaded{i}") for i in range(1)]
        p_rounded, p_ready, pg_done, out_done, stored = (
            sem("p_rounded"), sem("p_ready"), sem("pg_done"), sem("out_done"), sem("stored"))

        block = ctx.enter_context(nc.Block())
        ds = bass.ds

        @block.sync
        def _(sp):
            def load_a(s, i=0):
                n = s + 2 * i
                if s >= 2:
                    sp.wait_ge(a_ready, n - 1)
                sp.dma_start(a_raw[s % 2][:, :], w_a[ds(n, 1)].rearrange("a p n -> p (a n)")) \
                  .then_inc(a_loaded[s % 2], 16)

            def load_b(s, i=0):
                n = s + 2 * i
                if s >= 2:
                    sp.wait_ge(b_ready, n - 1)
                sp.dma_start(b_raw[s % 2][:, :], w_b[ds(n, 1)].rearrange("a p n -> p (a n)")) \
                  .then_inc(b_loaded[s % 2], 16)

            def stream(a, b, trips):
                with sp.Fori(0, trips) as i:
                    for u in range(2):
                        if a is not None:
                            load_a(a + u, i)
                        if b is not None:
                            load_b(b + u, i)

            for u in range(2):
                load_a(u)
                load_b(u)
            stream(A_RNN + 2, B_RNN + 2, RNN_BLOCKS // 2 - 1)
            stream(A_FF0, B_FF0, FF_TILES // 2)
            stream(A_KCMP, None, (A_FF1 - A_KCMP) // 2)
            stream(A_FF1, B_FF1, FF_TILES // 2)
            load_a(A_SKV)
            stream(A_SQ, None, (A_MRG - A_SQ) // 2)
            stream(A_MRG, B_MRG, KT // 2)
            stream(A_OUT, None, 2)
            load_a(A_ROUTE)
            stream(A_MOE, B_MOE, EXPERTS)
            load_a(A_PLE)
            stream(A_PG, None, 2)

        @block.tensor
        def _(pe):
            def three(out, w_hi, w_lo, x_hi, x_lo, first, last):
                pe.matmul(out, w_hi, x_hi, start=first, stop=False)
                pe.matmul(out, w_hi, x_lo, start=False, stop=False)
                return pe.matmul(out, w_lo, x_hi, start=False, stop=last)

            def product(out, s, col, pitch, width, x_hi, x_lo, kt=KT, k0=0, rows=P, first=True, last=True):
                for k in range(kt):
                    c = col + k * pitch
                    m = three(out, a_hi[s % 2][0:rows, c:c + width], a_lo[s % 2][0:rows, c:c + width],
                              x_hi(k), x_lo(k), first and k == 0, last and k == kt - 1)
                return m

            def hh(k):
                return hn_hi[:, k, :]

            def hl(k):
                return hn_lo[:, k, :]

            def tile_bank(s, j, n):
                if s >= 2 or s + j >= 2:
                    pe.wait_ge(tile_free, 2 * n - 3 + j)
                return bank[2 * (s % 2) + j]

            def linear(s, i=0, width=P):
                n = s + 2 * i
                pe.wait_ge(a_ready, n + 1)
                for j in range(2):
                    b = tile_bank(s, j, n)
                    product(b[0:width, :], s, j * width, 2 * width, width, hh, hl).then_inc(tile_ready, 1)

            def natural(s, j, col, pitch, width, i=0, inc=1):
                n = s + 2 * i
                b = tile_bank(s, j, n)
                for t in range(NT):
                    c = slice(t * P, (t + 1) * P)
                    for k in range(KT):
                        w = slice(col + k * pitch, col + k * pitch + width)
                        m = three(b[:, t * width:(t + 1) * width], hn_hi[:, k, c], hn_lo[:, k, c],
                                  a_hi[s % 2][:, w], a_lo[s % 2][:, w], k == 0, k == KT - 1)
                m.then_inc(tile_ready, inc)

            def norm_stats(q, ready, width=KT):
                ready(pe)
                for m in range(width):
                    pe.wait_ge(sq_ready, KT * q + m + 1)
                    pe.matmul(bank[4][:, :], ones, sq[:, m % 2, :], start=m == 0, stop=m == width - 1) \
                      .then_inc(stat_mm, 1)

            def down(sb_, e, i, x_hi, x_lo, rows):
                for hb in range(2):
                    s = sb_ + hb
                    n = s + 2 * i
                    pe.wait_ge(b_ready, n + 1)
                    for f in range(2):
                        if hb == 0:
                            pe.wait_ge(hid_ready, 2 * (e + i) + f + 1)
                        for m in range(4):
                            if f == 0:
                                pe.wait_ge(y_free, 4 * n + m - 3)
                            c = slice(f * 512 + m * P, f * 512 + (m + 1) * P)
                            mm = three(bank[4 + m][:, :], b_hi[s % 2][0:rows, c], b_lo[s % 2][0:rows, c],
                                       x_hi[0:rows, f, :], x_lo[0:rows, f, :], f == 0, f == 1)
                            if f == 1:
                                mm.then_inc(y_ready, 1)

            def rnn_pair(i, peeled):
                for u in range(2):
                    n = 2 * i + u
                    pe.wait_ge(a_ready, n + 1)
                    for j, done in ((0, xb_ready), (1, yb_ready)):
                        if not peeled:
                            pe.wait_ge(tile_free, 2 * n - 3 + j)
                        product(bank[2 * u + j][0:RNN_W, :], u, j * RNN_W, 2 * RNN_W, RNN_W, hh, hl) \
                            .then_inc(done, 1)
                    for j in range(2):
                        pe.wait_ge(xc_ready if j == 0 else yb_copied, n + 1)
                        product(bank[2 * u + j][0:RNN_W, :], u, 8 * 192 + j * RNN_W, 0, RNN_W,
                                lambda k: xc_hi[:, u, :], lambda k: xc_lo[:, u, :], kt=1, rows=RNN_W) \
                            .then_inc(tile_ready, 1)
                    if u == 0 and not peeled:
                        rnn_down(i)

            def rnn_down(i):
                for hb in range(2):
                    n = 2 * i - 2 + hb
                    pe.wait_ge(b_ready, n + 1)
                    for f in range(2):
                        if hb == 0:
                            pe.wait_ge(hid_ready, 2 * i - 2 + f + 1)
                        for m in range(4):
                            if f == 0:
                                pe.wait_ge(y_free, 4 * (2 * i - 2) + m - 3 + 4 * hb if hb else 8 * i - 8)
                            c = slice(f * 512 + m * P, f * 512 + (m + 1) * P)
                            mm = three(bank[4 + m][:, :], b_hi[hb][0:RNN_W, c], b_lo[hb][0:RNN_W, c],
                                       rhid_hi[0:RNN_W, f, :], rhid_lo[0:RNN_W, f, :], f == 0, f == 1)
                            if f == 1:
                                mm.then_inc(y_ready, 1)

            pe.wait_ge(consts, 16)
            norm_stats(N_MIX0, lambda e: None)
            pe.wait_ge(hn_ready, KT * (N_MIX0 + 1))
            rnn_pair(0, True)
            with pe.Fori(1, RNN_BLOCKS // 2) as i:
                rnn_pair(i, False)
            rnn_down(RNN_BLOCKS // 2)

            def ffn(sa, sb_, e, trips):
                with pe.Fori(0, trips) as i:
                    for f in range(2):
                        linear(sa + f, i)
                    down(sb_, e, i, hid_hi, hid_lo, P)

            def y_all(n_b):
                return lambda e: e.wait_ge(y_free, 4 * n_b)

            norm_stats(N_FFN0, y_all(B_FF0))
            pe.wait_ge(hn_ready, KT * (N_FFN0 + 1))
            ffn(A_FF0, B_FF0, E_FF0, FF_TILES // 2)

            norm_stats(N_KV, y_all(B_FF1))
            pe.wait_ge(hn_ready, KT * (N_KV + 1))
            linear(A_KCMP, width=DQK)
            linear(A_KCMP + 1, width=DQK)
            linear(A_VCMP)

            def rope_mm_(r, src):
                if r >= 2:
                    pe.wait_ge(rope_done, r - 1)
                pe.matmul(bank[4 + r % 2][0:DQK, :], rot, src, start=True, stop=True).then_inc(rope_mm, 1)

            for b in range(2):
                for p in range(2):
                    s = A_KSEL + 2 * b + p
                    linear(s, width=DQK)
                    for j in range(2):
                        pe.wait_ge(tile_free, 2 * s + j + 1)
                        rope_mm_(4 * b + 2 * p + j, kx[:, b, 2 * p + j, :])
            for b in range(2):
                s = A_VNAT + b
                pe.wait_ge(a_ready, s + 1)
                for j in range(2):
                    bk = tile_bank(s, j, s)
                    for t in range(2):
                        c = slice((2 * j + t) * P, (2 * j + t + 1) * P)
                        for k in range(KT):
                            w = slice(k * 256, (k + 1) * 256)
                            m = three(bk[:, t * 256:(t + 1) * 256], hn_hi[:, k, c], hn_lo[:, k, c],
                                      a_hi[s % 2][:, w], a_lo[s % 2][:, w], k == 0, k == KT - 1)
                    m.then_inc(tile_ready, 1)
            for b, (s0, rows) in enumerate(((A_W1K, DQK), (A_W1V, DV))):
                for p in range(4):
                    s = s0 + p
                    pe.wait_ge(a_ready, s + 1)
                    pe.wait_ge(xl_ready, 4 * b + p + 1)
                    if b == 1 and p == 0:
                        pe.wait_ge(chid_done, 1)
                    for m in range(2):
                        for l in range(8):
                            c = slice(l * 256 + m * P, l * 256 + (m + 1) * P)
                            mm = three(bank[6 + m][:, 0:124], a_hi[s % 2][0:rows, c], a_lo[s % 2][0:rows, c],
                                       xl_hi[0:rows, l, :], xl_lo[0:rows, l, :],
                                       p == 0 and l == 0, p == 3 and l == 7)
                    mm.then_inc(tile_ready, 2)
                pe.wait_ge(chid_done, b + 1)
                if b == 0:
                    for m in range(2):
                        mm = pe.matmul(bank[5][0:DQK, 0:124], smc("w2k", m * DQK, DQK), chid[:, m, :],
                                       start=m == 0, stop=m == 1)
                else:
                    pe.wait_ge(cmp_done, 1)
                    for g in range(GROUPS):
                        for m in range(2):
                            mm = pe.matmul(bank[5][0:NCMP, g * DV:(g + 1) * DV],
                                           chid[:, m, g * NCMP:(g + 1) * NCMP], smc("w2v", m * DV, DV),
                                           start=m == 0, stop=m == 1)
                mm.then_inc(cmp_w2, 1)

            norm_stats(N_MIX1, lambda e: e.wait_ge(cmp_done, 2))
            pe.wait_ge(hn_ready, KT * (N_MIX1 + 1))
            pe.wait_ge(a_ready, A_GATE + 1)
            natural(A_GATE, 0, 0, NGATE, NGATE, inc=2)
            with pe.Fori(0, HEADS // 4) as i:
                for u in range(2):
                    s = A_Q + u
                    linear(s, i, width=DQK)
                    for j in range(2):
                        v = 2 * u + j
                        pe.wait_ge(tile_free, 2 * (s + 2 * i) + j + 1)
                        pe.wait_ge(rope_done, 8 + 4 * i + v - 1)
                        pe.matmul(bank[4 + v % 2][0:DQK, :], rot, qb[:, v, 0, :], start=True, stop=True) \
                          .then_inc(rope_mm, 1)

            pe.wait_ge(rope_done, 8 + HEADS)
            pe.wait_ge(tile_free, 2 * A_WO)
            with pe.Fori(0, GROUPS) as g:
                pe.wait_ge(v_staged, 3 * g + 3)
                for u in range(HPG):
                    hd = HPG * g + u
                    q = u % 2
                    pe.wait_ge(q_staged[q], 32 * g + 16 * (u // 2) + 16)
                    pe.wait_ge(cpt_ready, hd)
                    for t in range(NT):
                        mm = pe.matmul(bank[6][:, t * NCMP:(t + 1) * NCMP], qs[:, q, 0, t * P:(t + 1) * P],
                                       kct[:, ds(g * NCMP, NCMP)], start=True, stop=True)
                    mm.then_inc(csc_ready, 1)

                    def scores(x):
                        t, b = x // 2, x % 2
                        n = (t + 1) * P
                        bk = bank[x % 4]
                        if x >= 4:
                            pe.wait_ge(exp_done, 8 * hd + x - 3)
                        else:
                            pe.wait_ge(exp_done, 8 * hd)
                        pe.matmul(bk[:, 0:n], qs[:, q, 1, t * P:(t + 1) * P], kx[:, b, ds(g, 1), 0:n].rearrange("p a s -> p (a s)"),
                                  start=True, stop=False)
                        pe.matmul(bk[:, t * P:n], ident, cnc("causal", P), start=False, stop=True) \
                          .then_inc(sc_ready, 1)

                    def turn(x):
                        t = x // 2
                        pe.wait_ge(pm_ready, 8 * hd + x + 1)
                        pe.wait_ge(pt_ready, 8 * hd + x - 1 if x >= 2 else 8 * hd)
                        for j in range(t + 1):
                            mm = pe.transpose(bank[4 + x % 2][:, j * P:(j + 1) * P],
                                              pm[:, x % 2, j * P:(j + 1) * P], ident)
                        mm.then_inc(tr_ready, 1)

                    scores(0)
                    scores(1)
                    pe.wait_ge(cpm_ready, hd + 1)
                    for t in range(NT):
                        mm = pe.transpose(bank[6][0:NCMP, t * P:(t + 1) * P], pc[:, t, :], ident)
                    mm.then_inc(ctr_ready, 1)
                    for x in range(2, 8):
                        scores(x)
                        turn(x - 2)
                    turn(6)
                    turn(7)
                    r0 = DV * (u % 2)
                    if u % 2 == 0:
                        pe.wait_ge(o_split, 2 * g + u // 2)
                    for b in range(2):
                        for j in range(NT):
                            if b == 0 and j == 0:
                                pe.wait_ge(pt_ready, 8 * hd + 8)
                                pe.wait_ge(cpt_ready, hd + 1)
                            pe.matmul(bank[7][r0:r0 + DV, j * P:S], vs[:, b, j, :], pt[:, b, j, j * P:S],
                                      start=b == 0 and j == 0, stop=False)
                    pe.matmul(bank[7][r0:r0 + DV, :], vcs[:, :], ptc[:, :], start=False, stop=True) \
                      .then_inc(o_ready, 1)

            pe.wait_ge(o_split, HEADS // 2)
            with pe.Fori(0, 2) as i:
                linear(A_WO, i)
                linear(A_WO + 1, i)

            norm_stats(N_FFN1, lambda e: None)
            pe.wait_ge(hn_ready, KT * (N_FFN1 + 1))
            ffn(A_FF1, B_FF1, E_FF1, FF_TILES // 2)
            norm_stats(N_FINAL, y_all(B_MRG))
            norm_stats(N_MIX2, lambda e: None)
            pe.wait_ge(hn_ready, KT * (N_MIX2 + 1))

            s = A_SKV
            pe.wait_ge(a_ready, s + 1)
            b = tile_bank(s, 0, s)
            product(b[:, :], s, 0, 2 * P, P, hh, hl).then_inc(tile_ready, 1)
            natural(s, 1, P, 2 * P, P)
            pe.wait_ge(qk_sq, 1)
            pe.matmul(bank[4][:, :], halves, sq[:, 0, :], start=True, stop=True).then_inc(qk_mm, 1)
            with pe.Fori(0, 2) as i:
                for u in range(2):
                    m = 2 * i + u
                    s = A_SQ + u
                    n = s + 2 * i
                    pe.wait_ge(a_ready, n + 1)
                    b = tile_bank(s, 0, n)
                    product(b[:, :], s, 0, 2 * P, P, hh, hl).then_inc(tile_ready, 2)
                    pe.wait_ge(qk_sq, m + 2)
                    pe.wait_ge(w_exp, 8 * m)
                    pe.matmul(bank[4][:, :], halves, sq[:, 0, :], start=True, stop=True).then_inc(qk_mm, 1)
                    pe.wait_ge(qk_norm, m + 2)

                    def scores_w(x):
                        t, half = x // 2, x % 2
                        r = slice(64 * half, 64 * half + 64)
                        pe.wait_ge(w_exp, 8 * m + x - 1 if x >= 2 else 8 * m)
                        k0 = max(t - 1, 0) * P
                        pe.matmul(bank[4 + half][:, 0:(t + 1) * P - k0], qn[r, t * P:(t + 1) * P],
                                  sk[r, k0:(t + 1) * P], start=True, stop=True).then_inc(w_sc, 1)

                    def out_w(x):
                        t, half = x // 2, x % 2
                        nb = 1 if t == 0 else 2
                        pe.wait_ge(w_pm, 8 * m + x + 1)
                        pe.wait_ge(w_pt, 8 * m + x)
                        for j in range(nb):
                            mm = pe.transpose(bank[6][:, j * P:(j + 1) * P], sp_[:, half, j * P:(j + 1) * P], ident)
                        mm.then_inc(w_tr, 1)
                        pe.wait_ge(w_pt, 8 * m + x + 1)
                        if x == 0:
                            pe.wait_ge(w_os, m)
                        for j in range(nb):
                            mm = pe.matmul(bank[7][64 * half:64 * half + 64, t * P:(t + 1) * P],
                                           sv[:, t - nb + 1 + j, 64 * half:64 * half + 64],
                                           spt_[:, half, j * P:(j + 1) * P], start=j == 0, stop=j == nb - 1)
                        if x == 7:
                            mm.then_inc(w_o, 1)

                    scores_w(0)
                    for x in range(1, 8):
                        scores_w(x)
                        out_w(x - 1)
                    out_w(7)

            pe.wait_ge(w_os, SWA_TILES)
            with pe.Fori(0, RET_H) as i:
                pe.wait_ge(a_ready, A_RET + 2 * i + 1)
                for j in range(2):
                    b = tile_bank(A_RET, j, A_RET + 2 * i)
                    product(b[:, :], A_RET, j * P, 2 * P, P, hh, hl).then_inc(tile_ready, 1)
                pe.wait_ge(a_ready, A_RET + 2 * i + 2)
                b = tile_bank(A_RET + 1, 0, A_RET + 1 + 2 * i)
                product(b[:, :], A_RET + 1, 0, 2 * P, P, hh, hl).then_inc(tile_ready, 1)
                natural(A_RET + 1, 1, P, 2 * P, P, i=i)
                pe.wait_ge(tile_free, 2 * (A_RET + 2 + 2 * i))

                def scores_r(j):
                    pe.wait_ge(r_dec, 4 * i + j - 1 if j >= 2 else 4 * i)
                    pe.matmul(bank[4 + j % 2][:, 0:S - j * P], rk[:, j * P:(j + 1) * P], rq[:, j * P:S],
                              start=True, stop=True).then_inc(r_sc, 1)

                def out_r(j):
                    pe.wait_ge(r_dec, 4 * i + j + 1)
                    if j == 0:
                        pe.wait_ge(r_y, i)
                    mm = pe.matmul(bank[6][:, j * P:S], rv[:, j * P:(j + 1) * P], srt[:, j % 2, 0:S - j * P],
                                   start=j == 0, stop=j == 3)
                    mm.then_inc(r_o, 1)

                scores_r(0)
                scores_r(1)
                out_r(0)
                scores_r(2)
                out_r(1)
                scores_r(3)
                out_r(2)
                out_r(3)
                pe.wait_ge(r_y, i + 1)
                pe.matmul(bank[7][:, :], ones, ry[:, :], start=True, stop=True).then_inc(r_mean, 1)
                pe.wait_ge(r_sq, i + 1)
                pe.matmul(bank[7][:, :], ones, sq[:, 0, :], start=True, stop=True).then_inc(r_var, 1)

            pe.wait_ge(r_split, RET_H)
            with pe.Fori(0, KT // 2) as i:
                for u in range(2):
                    linear(A_MRG + u, i)
                    s = B_MRG + u
                    n = s + 2 * i
                    pe.wait_ge(b_ready, n + 1)
                    pe.wait_ge(y_free, 4 * n - 4)
                    for j, (yh, yl) in enumerate(((yr_hi, yr_lo), (ys_hi, ys_lo))):
                        for k in range(4):
                            c = slice(j * 512 + k * P, j * 512 + (k + 1) * P)
                            mm = three(bank[4 + 2 * u + j][:, :], b_hi[s % 2][:, c], b_lo[s % 2][:, c],
                                       yh[:, k, :], yl[:, k, :], k == 0, k == 3)
                        mm.then_inc(y_ready, 2)

            pe.wait_ge(mg_ready, KT)
            with pe.Fori(0, 2) as i:
                for u in range(2):
                    s = A_OUT + u
                    n = s + 2 * i
                    pe.wait_ge(a_ready, n + 1)
                    for j in range(2):
                        b = tile_bank(s, j, n)
                        product(b[:, :], s, j * P, 2 * P, P, lambda k: mg_hi[:, k, :], lambda k: mg_lo[:, k, :]) \
                            .then_inc(tile_ready, 1)

            norm_stats(N_MOE, y_all(B_MOE))
            pe.wait_ge(hn_ready, KT * (N_MOE + 1))
            pe.wait_ge(a_ready, A_ROUTE + 1)
            natural(A_ROUTE, 0, 0, NROUTE, NROUTE, inc=2)
            pe.wait_ge(rt_done, 1)
            for t in range(NT):
                mm = pe.transpose(bank[4][0:EXPERTS, t * P:(t + 1) * P], cmb[:, t, :], ident)
            mm.then_inc(cmbt_mm, 1)
            pe.wait_ge(cmbt_done, 1)
            ffn(A_MOE, B_MOE, E_MOE, EXPERTS)

            norm_stats(N_PLEG, y_all(NB))
            s = A_PLE
            pe.wait_ge(a_ready, s + 1)
            pe.wait_ge(p_ready, 1)
            for m in range(KT):
                b = bank[m % 2 + 2 * (s % 2)]
                if m >= 2:
                    pe.wait_ge(pg_done, m - 1)
                else:
                    tile_bank(s, m, s)
                mm = product(b[:, :], s, m * P, D, P, lambda k: ptr_hi[:, k, :], lambda k: ptr_lo[:, k, :], kt=2)
                mm.then_inc(ple_mm, 1)
            pe.wait_ge(pg_done, KT)
            pe.sem_inc(tile_ready, 2)
            norm_stats(N_PLE, lambda e: e.wait_ge(sd_ready, N_PLEG + 1))
            pe.wait_ge(hn_ready, KT * (N_PLEG + 1))
            for p in range(4):
                linear(A_PG + p)

        @block.scalar
        def _(act):
            step = Steps(act, act_step)

            def high_a(s, i=0):
                n = s + 2 * i
                act.wait_ge(a_loaded[s % 2], 16 * (s // 2 + i) + 16)
                if s >= 1:
                    act.wait_ge(tile_ready, 2 * n - 2)
                act.activation(a_hi[s % 2][:, :], a_raw[s % 2][:, :], ACT.Copy).then_inc(a_rounded, 1)

            def high_b(s, i=0):
                n = s + 2 * i
                act.wait_ge(b_loaded[s % 2], 16 * (s // 2 + i) + 16)
                if s >= 1:
                    act.wait_ge(y_ready, 4 * n - 4)
                act.activation(b_hi[s % 2][:, :], b_raw[s % 2][:, :], ACT.Copy).then_inc(b_rounded, 1)

            def squares(q, ready):
                for m in range(KT):
                    ready(act, m)
                    if m >= 2:
                        act.wait_ge(stat_mm, KT * q + m - 1)
                    act.activation(sq[:, m % 2, :], h[:, m, :], ACT.Square).then_inc(sq_ready, 1)

            def root(q, n=KT):
                act.wait_ge(stat_mm, KT * (q + 1))
                if q:
                    act.wait_ge(dve_rstd, q)
                act.activation(sd[:, :], bank[4][:, :], ACT.Sqrt, bias=eps, scale=1.0 / D).then_inc(sd_ready, 1)

            def high_hn(q):
                for m in range(KT):
                    act.wait_ge(hn_scaled, KT * q + m + 1)
                    act.activation(hn_hi[:, m, :], tmp[:, m % 2, :], ACT.Copy).then_inc(hn_rounded, 1)

            act.dma_start(cn[:, :], const).then_inc(consts, 16)
            act.dma_start(h[:, :, :], x_t.rearrange("(k p) s -> p k s", p=P)).then_inc(x_loaded, 16)
            act.dma_start(sm[:, :], small).then_inc(params, 16)
            act.wait_ge(consts, 16)
            squares(N_MIX0, lambda e, m: e.wait_ge(x_loaded, 16))
            root(N_MIX0)
            high_a(A_RNN)
            high_hn(N_MIX0)

            act.wait_ge(params, 16)
            lam = smc("lam", 0, RNN_BLOCKS, RNN_W)
            step(act.activation(spt[:, 0, :], lam, ACT.Abs))
            act.activation(spt[:, 1, :], spt[:, 0, :], ACT.Exp, scale=-1.0).then_inc(sp_exp, 1)
            act.wait_ge(sp_one, 1)
            act.activation(spt[:, 3, :], spt[:, 2, :], ACT.Ln).then_inc(sp_ln, 1)
            act.wait_ge(sp_done, 1)

            def rnn_pair(i, peeled):
                for u in range(2):
                    n = 2 * i + u
                    high_a(A_RNN + 1 + u, i)
                    act.wait_ge(xc_done, n + 1)
                    act.activation(xc_hi[:, u, :], xc[:, u, :], ACT.Copy).then_inc(xc_rounded, 1)
                    for j, (dst, bias) in enumerate(((rg, "b_ra"), (ig, "b_ix"))):
                        act.wait_ge(tile_ready, 2 * n + j + 1)
                        act.activation(dst[:, u, :], bank[2 * u + j][0:RNN_W, :], ACT.Sigmoid,
                                       bias=sm[0:RNN_W, ds(SM[bias] + n, 1)]).then_inc(tile_free, 1)
                for u in range(2):
                    act.wait_ge(b_loaded[u], 16 * i + 16)
                    if not peeled:
                        act.wait_ge(y_ready, 8 * i - 4 + 4 * u)
                    act.activation(b_hi[u][:, :], b_raw[u][:, :], ACT.Copy).then_inc(b_rounded, 1)
                for u in range(2):
                    n = 2 * i + u
                    act.wait_ge(yb_copied, n + 1)
                    act.activation(gel[:, u, :], ybr[:, u, :], ACT.Gelu_apprx_tanh).then_inc(gelu_done, 1)
                act.wait_ge(tile_free, 4 * i + 4)
                for u in range(2):
                    n = 2 * i + u
                    act.activation(aa[:, u, :], rg[:, u, :], ACT.Exp, scale=spt[:, 7, ds(n, 1)]) \
                       .then_inc(decay_done, 1)
                    act.activation(pp[:, u, :], rg[:, u, :], ACT.Tanh, scale=spt[:, 6, ds(n, 1)]) \
                       .then_inc(decay_done, 1)
                for u in range(2):
                    n = 2 * i + u
                    act.wait_ge(m2_done, n + 1)
                    act.activation(mu[:, u, :], pp[:, u, :], ACT.Sqrt).then_inc(mult_done, 1)
                for u in range(2):
                    n = 2 * i + u
                    act.wait_ge(rec_done, n + 1)
                    if not peeled:
                        act.wait_ge(y_ready, 8 * i)
                    act.activation(rhid_hi[0:RNN_W, u, :], hs[:, u, :], ACT.Copy).then_inc(hid_rounded, 1)

            rnn_pair(0, True)
            with act.Fori(1, RNN_BLOCKS // 2) as i:
                rnn_pair(i, False)

            def ffn_pair(sa, sb_, e, i):
                for f in range(2):
                    n = sa + f + 2 * i
                    high_a(sa + f + 1, i)
                    high_b(sb_ + f, i)
                    act.wait_ge(tile_ready, 2 * n + 1)
                    act.activation(sg[:, f, :], bank[2 * ((sa + f) % 2)][:, :], ACT.Silu).then_inc(gate_done, 1)
                    act.wait_ge(tile_free, 2 * n + 2)
                    act.activation(hid_hi[:, f, :], hid[:, f, :], ACT.Copy).then_inc(hid_rounded, 1)

            def ffn(sa, sb_, e, trips):
                with act.Fori(0, trips) as i:
                    ffn_pair(sa, sb_, e, i)

            def y_is(nb):
                return lambda e, m: e.wait_ge(y_free, 4 * nb - KT + m + 1)

            squares(N_FFN0, y_is(B_FF0))
            root(N_FFN0)
            high_hn(N_FFN0)
            ffn(A_FF0, B_FF0, E_FF0, FF_TILES // 2)

            squares(N_KV, y_is(B_FF1))
            root(N_KV)
            high_hn(N_KV)
            for s in range(A_KCMP, A_W1K):
                high_a(s + 1)
            for b, rows in enumerate((DQK, DV)):
                for p in range(4):
                    high_a(A_W1K + 4 * b + p + 1)
                    act.wait_ge(xl_done, 4 * b + p + 1)
                    act.wait_ge(tile_ready, 2 * (A_W1K + 4 * b + p))
                    act.activation(xl_hi[0:rows, :, :], xl[0:rows, :, :], ACT.Copy).then_inc(xl_rounded, 1)
                act.wait_ge(tile_ready, 2 * (A_W1K + 4 * b + 4))
                if b == 1:
                    act.wait_ge(cmp_w2, 1)
                for m in range(2):
                    mm = act.activation(chid[:, m, :], bank[6 + m][:, 0:124], ACT.Gelu_apprx_tanh)
                mm.then_inc(chid_done, 1)

            squares(N_MIX1, lambda e, m: None)
            root(N_MIX1)
            high_hn(N_MIX1)
            high_a(A_GATE + 1)
            act.wait_ge(gates_in, 1)
            act.activation(gates[:, :, :], gates[:, :, :], ACT.Sigmoid).then_inc(gates_done, 1)
            with act.Fori(0, HEADS // 4) as i:
                for u in range(2):
                    high_a(A_Q + u + 1, i)

            with act.Fori(0, GROUPS) as g:
                for u in range(HPG):
                    hd = HPG * g + u

                    def expo(x):
                        n = (x // 2 + 1) * P
                        act.wait_ge(mx_done, 8 * hd + x + 1)
                        act.wait_ge(tr_ready, 8 * hd + x - 1 if x >= 2 else 8 * hd)
                        act.activation(pm[:, x % 2, 0:n], bank[x % 4][:, 0:n], ACT.Exp,
                                       bias=ast[:, x % 2, 0:1], accum_out=ast[:, x % 2, 1:2]).then_inc(exp_done, 1)

                    act.wait_ge(csub_done, hd + 1)
                    act.activation(pc[:, :, :], pc[:, :, :], ACT.Exp).then_inc(cexp_done, 1)
                    expo(0)
                    expo(1)
                    act.wait_ge(ctr_ready, hd + 1)
                    act.wait_ge(o_ready, hd)
                    act.activation(ptc[:, :], bank[6][0:NCMP, :], ACT.Copy).then_inc(cpt_ready, 1)
                    for x in range(8):
                        t = x // 2
                        if x + 2 < 8:
                            expo(x + 2)
                        act.wait_ge(tr_ready, 8 * hd + x + 1)
                        act.activation(pt[:, x % 2, 0:t + 1, t * P:(t + 1) * P],
                                       bank[4 + x % 2][:, 0:(t + 1) * P].rearrange("p (j c) -> p j c", c=P),
                                       ACT.Copy).then_inc(pt_ready, 1)
                    if u % 2:
                        act.wait_ge(o_ready, hd + 1)
                        act.activation(hn_hi[:, ds(2 * g + u // 2, 1), :].rearrange("p a s -> p (a s)"),
                                       bank[7][:, :], ACT.Copy).then_inc(o_rounded, 1)

            for p in range(4):
                high_a(A_WO + p + 1)

            def tile_is(s):
                return lambda e, m: e.wait_ge(tile_free, 2 * s + m + 1)

            squares(N_FFN1, tile_is(A_WO))
            root(N_FFN1)
            high_hn(N_FFN1)
            ffn(A_FF1, B_FF1, E_FF1, FF_TILES // 2)
            squares(N_FINAL, y_is(B_MRG))
            root(N_FINAL)
            squares(N_MIX2, lambda e, m: e.wait_ge(hn_scaled, KT * N_FINAL + m + 1))
            root(N_MIX2)
            act.wait_ge(hn_rounded, KT * N_FINAL)
            act.sem_inc(hn_rounded, KT)
            high_hn(N_MIX2)

            high_a(A_SKV + 1)
            act.wait_ge(qk_raw, 1)
            act.activation(sq[:, 0, :], sk[:, :], ACT.Square).then_inc(qk_sq, 1)
            act.wait_ge(qk_mm, 1)
            act.activation(sd[:, :], bank[4][:, :], ACT.Sqrt, bias=eps, scale=1.0 / SWA_HD).then_inc(qk_sd, 1)
            with act.Fori(0, 2) as i:
                for u in range(2):
                    m = 2 * i + u
                    high_a(A_SQ + u + 1, i)
                    act.wait_ge(qk_raw, m + 2)
                    act.activation(sq[:, 0, :], tmp[:, 0, :], ACT.Square).then_inc(qk_sq, 1)
                    act.wait_ge(qk_mm, m + 2)
                    act.wait_ge(qk_norm, m + 1)
                    act.activation(sd[:, :], bank[4][:, :], ACT.Sqrt, bias=eps, scale=1.0 / SWA_HD).then_inc(qk_sd, 1)
                    for x in range(8):
                        t, half = x // 2, x % 2
                        n = P if t == 0 else 2 * P
                        act.wait_ge(w_mx, 8 * m + x + 1)
                        act.activation(sp_[:, half, 0:n], sp_[:, half, 0:n], ACT.Exp, bias=wst[:, half, 1:2],
                                       accum_out=wst[:, half, 2:3])
                        act.activation(wst[:, half, 3:4], sm[:, ds(SM["sink"] + 2 * m + half, 1)], ACT.Exp,
                                       bias=wst[:, half, 1:2]).then_inc(w_exp, 1)
                        act.wait_ge(w_tr, 8 * m + x + 1)
                        act.activation(spt_[:, half, 0:n], bank[6][:, 0:n], ACT.Copy).then_inc(w_pt, 1)
                    act.wait_ge(w_o, m + 1)
                    act.activation(ys_hi[:, ds(m, 1), :].rearrange("p a s -> p (a s)"), bank[7][:, :], ACT.Copy) \
                       .then_inc(w_or, 1)

            with act.Fori(0, RET_H) as i:
                high_a(A_RET + 1, i)
                act.wait_ge(tile_ready, 2 * (A_RET + 1 + 2 * i) + 1)
                act.wait_ge(r_g, i)
                act.activation(rgs[:, :], bank[2 * ((A_RET + 1) % 2)][:, :], ACT.Silu).then_inc(r_gate, 1)
                high_a(A_RET + 2, i)
                act.wait_ge(r_c, i + 1)
                act.activation(sq[:, 0, :], ryc[:, :], ACT.Square).then_inc(r_sq, 1)
                act.wait_ge(r_var, i + 1)
                act.activation(sd[:, :], bank[7][:, :], ACT.Sqrt, bias=eps, scale=1.0 / P).then_inc(r_sd, 1)
                act.wait_ge(r_g, i + 1)
                act.activation(yr_hi[:, ds(i, 1), :].rearrange("p a s -> p (a s)"), ryc[:, :], ACT.Copy) \
                   .then_inc(r_rounded, 1)

            act.wait_ge(r_split, RET_H)
            with act.Fori(0, KT // 2) as i:
                for u in range(2):
                    s = A_MRG + u
                    n = s + 2 * i
                    high_a(s + 1, i)
                    high_b(B_MRG + u, i)
                    act.wait_ge(mg_sum, 2 * i + u)
                    for j in range(2):
                        act.wait_ge(tile_ready, 2 * n + j + 1)
                        act.activation(sgt[:, j, :], bank[2 * (s % 2) + j][:, :], ACT.Sigmoid).then_inc(mg_gate, 1)
                    act.wait_ge(mg_sum, 2 * i + u + 1)
                    act.activation(mg_hi[:, ds(2 * i + u, 1), :].rearrange("p a s -> p (a s)"), tmp[:, 0, :],
                                   ACT.Copy).then_inc(mg_rounded, 1)
            for p in range(4):
                high_a(A_OUT + p + 1)
            squares(N_MOE, tile_is(A_OUT))
            root(N_MOE)
            high_hn(N_MOE)

            high_a(A_ROUTE + 1)
            act.wait_ge(rt_in, 1)
            act.activation(rtg[:, 1, :, :], rtg[:, 0, :, :], ACT.Exp)
            act.activation(rt[:, 5, :], rt[:, 4, :], ACT.Exp).then_inc(rt_exp, 1)
            ffn(A_MOE, B_MOE, E_MOE, EXPERTS)

            squares(N_PLEG, y_is(NB))
            root(N_PLEG)
            act.wait_ge(p_loaded, 16)
            act.activation(ptr_hi[:, :, :], ptr[:, :, :], ACT.Copy).then_inc(p_rounded, 1)
            high_a(A_PLE + 1)
            high_hn(N_PLEG)
            for m in range(KT):
                act.wait_ge(pg_done, m + 1)
                if m >= 2:
                    act.wait_ge(stat_mm, KT * N_PLE + m - 1)
                act.activation(sq[:, m % 2, :], ple[:, m, :], ACT.Square).then_inc(sq_ready, 1)
            root(N_PLE)
            for p in range(4):
                s = A_PG + p
                if p < 3:
                    high_a(s + 1)
                for j in range(2):
                    m = 2 * p + j
                    act.wait_ge(tile_ready, 2 * s + j + 1)
                    act.wait_ge(tile_free, 2 * s + j - 1)
                    act.activation(pgs[:, j, :], bank[2 * (s % 2) + j][:, :], ACT.Sigmoid).then_inc(out_done, 1)

        @block.vector
        def _(dve):
            step = Steps(dve, dve_step)
            V = dve

            def low_a(s, i=0):
                n = s + 2 * i
                V.wait_ge(a_rounded, n + 1)
                V.tensor_tensor(a_lo[s % 2][:, :], a_raw[s % 2][:, :], a_hi[s % 2][:, :], ALU.subtract) \
                 .then_inc(a_ready, 1)

            def low_b(s, i=0):
                n = s + 2 * i
                V.wait_ge(b_rounded, n + 1)
                V.tensor_tensor(b_lo[s % 2][:, :], b_raw[s % 2][:, :], b_hi[s % 2][:, :], ALU.subtract) \
                 .then_inc(b_ready, 1)

            def inverse_root(q):
                V.wait_ge(sd_ready, q + 1)
                V.reciprocal(rstd[:, :], sd[:, :]).then_inc(dve_rstd, 1)
                V.wait_ge(dve_rstd, q + 1)

            def normalise(q, gain, ready=None):
                inverse_root(q)
                if ready:
                    ready(V)

                def low(m):
                    V.wait_ge(hn_rounded, KT * q + m + 1)
                    V.tensor_tensor(hn_lo[:, m, :], tmp[:, m % 2, :], hn_hi[:, m, :], ALU.subtract) \
                     .then_inc(hn_ready, 1)

                for m in range(KT):
                    if m >= 2:
                        V.wait_ge(hn_ready, KT * q + m - 1)
                    V.scalar_tensor_tensor(tmp[:, m % 2, :], h[:, m, :], smc("gain", KT * gain + m), rstd[:, :],
                                           ALU.mult, ALU.mult).then_inc(hn_scaled, 1)
                    if m:
                        low(m - 1)
                low(KT - 1)

            low_a(A_RNN)
            V.wait_ge(params, 16)
            V.wait_ge(x_loaded, 16)
            normalise(N_MIX0, 0)

            V.wait_ge(sp_exp, 1)
            one, dif, zero = spt[:, 2, :], spt[:, 4, :], spt[:, 5, :]
            V.tensor_scalar(one, spt[:, 1, :], 1.0, None, ALU.add).then_inc(sp_one, 1)
            V.wait_ge(sp_one, 1)
            step(V.tensor_scalar(dif, one, -1.0, None, ALU.add))
            step(V.tensor_scalar(zero, dif, 0.0, None, ALU.is_equal))
            step(V.tensor_tensor(dif, dif, zero, ALU.add))
            step(V.reciprocal(dif, dif))
            V.wait_ge(sp_ln, 1)
            step(V.tensor_tensor(zero, zero, spt[:, 3, :], ALU.add))
            step(V.tensor_tensor(zero, zero, dif, ALU.mult))
            step(V.tensor_tensor(zero, zero, spt[:, 1, :], ALU.mult))
            step(V.tensor_scalar(dif, smc("lam", 0, RNN_BLOCKS, RNN_W), -1.0, 0.0, ALU.mult, ALU.max))
            step(V.tensor_tensor(dif, dif, zero, ALU.add))
            V.tensor_scalar(spt[:, 6, :], dif, 8.0, None, ALU.mult)
            V.tensor_scalar(spt[:, 7, :], dif, -8.0, None, ALU.mult).then_inc(sp_done, 1)

            def add_y(nb0):
                for m in range(KT):
                    V.wait_ge(y_ready, 4 * nb0 + m + 1)
                    V.tensor_tensor(h[:, m, :], h[:, m, :], bank[4 + m % 4][:, :], ALU.add).then_inc(y_free, 1)

            def rnn_pair(i, peeled):
                for u in range(2):
                    n = 2 * i + u
                    low_a(A_RNN + 1 + u, i)
                    V.wait_ge(xb_ready, n + 1)
                    if not peeled:
                        V.wait_ge(gx_done, n - 1)
                    ps = bank[2 * u][0:RNN_W, :]

                    def tap(k):
                        return sm[0:RNN_W, ds(SM["conv_w"] + 4 * n + k, 1)]

                    step(V.tensor_scalar(xc[:, u, :], ps, tap(3), sm[0:RNN_W, ds(SM["conv_b"] + n, 1)],
                                         ALU.mult, ALU.add))
                    for k in (2, 1, 0):
                        d = 3 - k
                        ins = V.scalar_tensor_tensor(xc[:, u, d:S], ps[:, 0:S - d], tap(k), xc[:, u, d:S],
                                                     ALU.mult, ALU.add)
                        if k:
                            step(ins)
                    ins.then_inc(xc_done, 1)
                    V.wait_ge(xc_rounded, n + 1)
                    V.tensor_tensor(xc_lo[:, u, :], xc[:, u, :], xc_hi[:, u, :], ALU.subtract).then_inc(xc_ready, 1)
                    V.wait_ge(yb_ready, n + 1)
                    if not peeled:
                        V.wait_ge(gelu_done, n - 1)
                    V.tensor_copy(ybr[:, u, :], bank[2 * u + 1][0:RNN_W, :]).then_inc(yb_copied, 1)
                    if u == 0 and not peeled:
                        add_y(2 * i - 2)
                for u in range(2):
                    V.wait_ge(b_rounded, 2 * i + u + 1)
                    V.tensor_tensor(b_lo[u][:, :], b_raw[u][:, :], b_hi[u][:, :], ALU.subtract).then_inc(b_ready, 1)
                for u in range(2):
                    n = 2 * i + u
                    V.wait_ge(asq_done, n + 1)
                    V.scalar_tensor_tensor(pp[:, u, :], mu[:, u, :], 1.0, pp[:, u, :], ALU.add, ALU.mult) \
                     .then_inc(m2_done, 1)
                for u in range(2):
                    n = 2 * i + u
                    V.wait_ge(bx_done, n + 1)
                    V.tensor_tensor_scan(hs[:, u, :], aa[:, u, :], gx[:, u, :], 0.0, ALU.mult, ALU.add) \
                     .then_inc(scan_done, 1)
                for u in range(2):
                    n = 2 * i + u
                    V.wait_ge(hid_rounded, n + 1)
                    V.tensor_tensor(rhid_lo[0:RNN_W, u, :], hs[:, u, :], rhid_hi[0:RNN_W, u, :], ALU.subtract) \
                     .then_inc(hid_ready, 1)

            rnn_pair(0, True)
            step.enter(0, 6)
            with V.Fori(1, RNN_BLOCKS // 2) as i:
                step.i = i - 1
                rnn_pair(i, False)
            step.leave(RNN_BLOCKS // 2 - 1)
            add_y(RNN_BLOCKS - 2)

            def ffn(sa, sb_, e, trips, weighted=False):
                per = 2 if weighted else 0
                step.enter(0, per)
                with V.Fori(0, trips) as i:
                    step.i = i
                    for f in range(2):
                        n = sa + f + 2 * i
                        low_a(sa + f + 1, i)
                        low_b(sb_ + f, i)
                        V.wait_ge(gate_done, 2 * (e - E_FF0 + i) + f + 1)
                        if weighted:
                            if f == 0:
                                V.wait_ge(comb_loaded[0], 16 * i + 16)
                            step(V.tensor_tensor(sg[:, f, :], sg[:, f, :], comb[:, 0, :], ALU.mult))
                        V.wait_ge(tile_ready, 2 * n + 2)
                        V.tensor_tensor(hid[:, f, :], sg[:, f, :], bank[2 * ((sa + f) % 2) + 1][:, :], ALU.mult) \
                         .then_inc(tile_free, 2)
                        V.wait_ge(hid_rounded, 2 * (e + i) + f + 1)
                        V.tensor_tensor(hid_lo[:, f, :], hid[:, f, :], hid_hi[:, f, :], ALU.subtract) \
                         .then_inc(hid_ready, 1)
                    add_y(sb_ + 2 * i)
                step.leave(trips)

            normalise(N_FFN0, 1)
            ffn(A_FF0, B_FF0, E_FF0, FF_TILES // 2)

            normalise(N_KV, 2)

            def tile(s, j, n=None):
                V.wait_ge(tile_ready, 2 * (s if n is None else n) + j + 1)
                return bank[2 * (s % 2) + j]

            for p in range(2):
                low_a(A_KCMP + p + 1)
                for j in range(2):
                    b = tile(A_KCMP + p, j)
                    V.tensor_copy(kraw[:, 2 * p + j, :], b[0:DQK, :]).then_inc(tile_free, 1)
            low_a(A_VCMP + 1)
            for j in range(2):
                b = tile(A_VCMP, j)
                V.tensor_copy(vraw[:, 2 * j, :], b[0:DV, :])
                V.tensor_copy(vraw[:, 2 * j + 1, :], b[DV:P, :]).then_inc(tile_free, 1)
            V.wait_ge(rope_loaded, 16)

            def rotate(r, bk, x, out):
                V.wait_ge(rope_mm, r + 1)
                V.wait_ge(rope_done, r)
                step(V.tensor_tensor(rtmp[:, 0, :], bank[bk][0:DQK, :], cs[:, 1, :], ALU.mult))
                step(V.tensor_tensor(rtmp[:, 1, :], x, cs[:, 0, :], ALU.mult))
                V.tensor_tensor(out, rtmp[:, 0, :], rtmp[:, 1, :], ALU.add).then_inc(rope_done, 1)

            for b in range(2):
                for p in range(2):
                    s = A_KSEL + 2 * b + p
                    low_a(s + 1)
                    for j in range(2):
                        V.tensor_copy(kx[:, b, 2 * p + j, :], tile(s, j)[0:DQK, :]).then_inc(tile_free, 1)
                    for j in range(2):
                        r = 4 * b + 2 * p + j
                        rotate(r, 4 + r % 2, kx[:, b, 2 * p + j, :], kx[:, b, 2 * p + j, :])
            for b in range(2):
                s = A_VNAT + b
                low_a(s + 1)
                for j in range(2):
                    V.tensor_copy(vn[:, b, 2 * j:2 * j + 2, :],
                                  tile(s, j)[:, :].rearrange("p (t c) -> p t c", t=2)).then_inc(tile_free, 1)
            for b, (src, pos, rows) in enumerate(((kraw, "pos_k", DQK), (vraw, "pos_v", DV))):
                for p in range(4):
                    s = A_W1K + 4 * b + p
                    low_a(s + 1)
                    for l in range(8):
                        tap = 8 * p + l
                        ins = V.tensor_scalar(
                            xl[0:rows, l, :].rearrange("p (g c) -> p g c", g=GROUPS),
                            src[:, :, tap:tap + CSTRIDE * (NCMP - 1) + 1:CSTRIDE],
                            smc(pos, tap, 1, rows), None, ALU.add)
                    ins.then_inc(xl_done, 1)
                    V.wait_ge(xl_rounded, 4 * b + p + 1)
                    V.tensor_tensor(xl_lo[0:rows, :, :], xl[0:rows, :, :], xl_hi[0:rows, :, :], ALU.subtract) \
                     .then_inc(xl_ready, 1)
                    V.wait_ge(xl_ready, 4 * b + p + 1)
                    V.sem_inc(tile_free, 2)
                V.wait_ge(cmp_w2, b + 1)
                if b == 0:
                    V.tensor_copy(kct[:, :], bank[5][0:DQK, 0:124]).then_inc(cmp_done, 1)
                else:
                    V.tensor_copy(vcn[:, :, :], bank[5][0:NCMP, 0:GROUPS * DV]
                                  .rearrange("p (g c) -> p g c", g=GROUPS)).then_inc(cmp_done, 1)

            normalise(N_MIX1, 3)
            low_a(A_GATE + 1)
            V.wait_ge(tile_ready, 2 * A_GATE + 2)
            step(V.tensor_tensor(gates[:, :, :], bank[2 * (A_GATE % 2)][:, 0:NT * NGATE]
                                 .rearrange("p (t c) -> p t c", t=NT),
                                 smc("gate_b", 0, NT * NGATE).rearrange("p (t c) -> p t c", t=NT), ALU.add))
            V.sem_inc(gates_in, 1)
            V.sem_inc(tile_free, 2)
            step.enter(0, 8)
            with V.Fori(0, HEADS // 4) as i:
                step.i = i
                for u in range(2):
                    s = A_Q + u
                    n = s + 2 * i
                    low_a(s + 1, i)
                    for j in range(2):
                        v = 2 * u + j
                        b = tile(s, j, n)
                        V.wait_ge(q_stored[u], 16 * i)
                        V.tensor_scalar(qb[:, v, 0, :], b[0:DQK, :], DQK ** -0.5, None, ALU.mult) \
                         .then_inc(tile_free, 1)
                    V.wait_ge(tile_free, 2 * n + 2)
                    for j in range(2):
                        v = 2 * u + j
                        V.wait_ge(rope_mm, 8 + 4 * i + v + 1)
                        V.wait_ge(rope_done, 8 + 4 * i + v)
                        step(V.tensor_tensor(rtmp[:, 0, :], bank[4 + v % 2][0:DQK, :], cs[:, 1, :], ALU.mult))
                        step(V.tensor_tensor(rtmp[:, 1, :], qb[:, v, 0, :], cs[:, 0, :], ALU.mult))
                        V.tensor_tensor(qb[:, v, 1, :], rtmp[:, 0, :], rtmp[:, 1, :], ALU.add).then_inc(rope_done, 1)
            step.leave(HEADS // 4)

            V.wait_ge(gates_done, 1)
            step.enter(0, HPG * (8 + 16))
            with V.Fori(0, GROUPS) as g:
                step.i = g
                for u in range(HPG):
                    hd = HPG * g + u

                    def gate(t, b, n=1):
                        return gates[:, t:t + n, ds(3 * hd + b, 1)]

                    V.wait_ge(csc_ready, hd + 1)
                    V.wait_ge(ctr_ready, hd)
                    step(V.tensor_tensor(pc[:, :, :], bank[6][:, 0:124].rearrange("p (t c) -> p t c", t=NT),
                                         cnc("cmp_mask", 124).rearrange("p (t c) -> p t c", t=NT), ALU.add))
                    step(V.tensor_reduce(cst[:, 0, :], pc[:, :, :], AX_X, ALU.max))
                    step(V.tensor_scalar(cst[:, 1, :], cst[:, 0, :], -1e20, None, ALU.max))
                    V.tensor_tensor(pc[:, :, :], pc[:, :, :],
                                    cst[:, 1, :].rearrange("p (t o) -> p t o", o=1).to_broadcast([P, NT, NCMP]),
                                    ALU.subtract).then_inc(csub_done, 1)

                    def peak(x):
                        n = (x // 2 + 1) * P
                        V.wait_ge(sc_ready, 8 * hd + x + 1)
                        V.wait_ge(pm_ready, 8 * hd + x - 1 if x >= 2 else 8 * hd)
                        V.tensor_reduce(ast[:, x % 2, 0:1], bank[x % 4][:, 0:n], AX_X, ALU.max, negate=True) \
                         .then_inc(mx_done, 1)

                    def weigh(x):
                        t, b = x // 2, x % 2
                        n = (t + 1) * P
                        V.wait_ge(exp_done, 8 * hd + x + 1)
                        step(V.reciprocal(ast[:, x % 2, 2:3], ast[:, x % 2, 1:2]))
                        step(V.tensor_tensor(ast[:, x % 2, 3:4], ast[:, x % 2, 2:3],
                                             gate(t, 1 + b).rearrange("p a o -> p (a o)"), ALU.mult))
                        V.tensor_scalar(pm[:, x % 2, 0:n], pm[:, x % 2, 0:n], ast[:, x % 2, 3:4], None, ALU.mult) \
                         .then_inc(pm_ready, 1)

                    peak(0)
                    peak(1)
                    V.wait_ge(cexp_done, hd + 1)
                    step(V.tensor_reduce(cst[:, 2, :], pc[:, :, :], AX_X, ALU.add))
                    step(V.tensor_scalar(cst[:, 2, :], cst[:, 2, :], 1e-30, None, ALU.max))
                    step(V.reciprocal(cst[:, 3, :], cst[:, 2, :]))
                    step(V.tensor_tensor(cst[:, 3, :], cst[:, 3, :],
                                         gate(0, 0, NT).rearrange("p a o -> p (a o)"), ALU.mult))
                    step(V.tensor_tensor(pc[:, :, :], pc[:, :, :],
                                    cst[:, 3, :].rearrange("p (t o) -> p t o", o=1).to_broadcast([P, NT, NCMP]),
                                    ALU.mult))
                    V.sem_inc(cpm_ready, 1)
                    for x in range(8):
                        weigh(x)
                        if x + 2 < 8:
                            peak(x + 2)
                    if u % 2:
                        V.wait_ge(o_rounded, 2 * g + u // 2 + 1)
                        m = ds(2 * g + u // 2, 1)
                        V.tensor_tensor(hn_lo[:, m, :].rearrange("p a s -> p (a s)"), bank[7][:, :],
                                        hn_hi[:, m, :].rearrange("p a s -> p (a s)"), ALU.subtract) \
                         .then_inc(o_split, 1)
            step.leave(GROUPS)

            def add_tiles(s0):
                for p in range(4):
                    s = s0 + p
                    low_a(s + 1)
                    for j in range(2):
                        m = 2 * p + j
                        V.tensor_tensor(h[:, m, :], h[:, m, :], tile(s, j)[:, :], ALU.add).then_inc(tile_free, 1)

            add_tiles(A_WO)
            normalise(N_FFN1, 4)
            ffn(A_FF1, B_FF1, E_FF1, FF_TILES // 2)

            inverse_root(N_FINAL)
            for m in range(KT):
                V.scalar_tensor_tensor(h[:, m, :], h[:, m, :], smc("gain", KT * 5 + m), rstd[:, :],
                                       ALU.mult, ALU.mult).then_inc(hn_scaled, 1)
            V.wait_ge(hn_scaled, KT * (N_FINAL + 1))
            V.sem_inc(hn_ready, KT)
            normalise(N_MIX2, 6)

            low_a(A_SKV + 1)
            V.tensor_copy(sk[:, :], tile(A_SKV, 0)[:, :]).then_inc(qk_raw, 1)
            V.tensor_copy(sv[:, :, :], tile(A_SKV, 1)[:, :].rearrange("p (t c) -> p t c", t=NT)) \
             .then_inc(tile_free, 2)

            def qk_scale(dst, src, gain, k):
                V.wait_ge(qk_sd, k)
                step(V.reciprocal(rstd[:, :], sd[:, :]))
                V.scalar_tensor_tensor(dst, src, smc(gain), rstd[:, :], ALU.mult, ALU.mult).then_inc(qk_norm, 1)

            qk_scale(sk[:, :], sk[:, :], "k_g", 1)
            V.wait_ge(alibi_loaded, 16)
            step.enter(0, 2 * (1 + 8 * 5))
            with V.Fori(0, 2) as i:
                step.i = i
                for u in range(2):
                    m = 2 * i + u
                    s = A_SQ + u
                    n = s + 2 * i
                    low_a(s + 1, i)
                    V.wait_ge(tile_ready, 2 * n + 2)
                    V.tensor_copy(tmp[:, 0, :], bank[2 * (s % 2)][:, :]).then_inc(tile_free, 2)
                    V.wait_ge(tile_free, 2 * n + 2)
                    V.sem_inc(qk_raw, 1)
                    qk_scale(qn[:, :], tmp[:, 0, :], "q_g", m + 2)

                    def peak_w(x):
                        t, half = x // 2, x % 2
                        w = P if t == 0 else 2 * P
                        V.wait_ge(w_sc, 8 * m + x + 1)
                        V.wait_ge(w_tr, 8 * m + x - 1 if x >= 2 else 8 * m)
                        step(V.scalar_tensor_tensor(
                            sp_[:, half, 0:w], bank[4 + half][:, 0:w], SWA_HD ** -0.5,
                            al[:, ds(2 * m + half, 1), 2 * P - w:2 * P].rearrange("p a s -> p (a s)"),
                            ALU.mult, ALU.add))
                        step(V.tensor_reduce(wst[:, half, 0:1], sp_[:, half, 0:w], AX_X, ALU.max))
                        V.tensor_scalar(wst[:, half, 1:2], wst[:, half, 0:1],
                                        sm[:, ds(SM["sink"] + 2 * m + half, 1)], -1.0, ALU.max, ALU.mult) \
                         .then_inc(w_mx, 1)

                    def weigh_w(x):
                        t, half = x // 2, x % 2
                        w = P if t == 0 else 2 * P
                        V.wait_ge(w_exp, 8 * m + x + 1)
                        step(V.tensor_tensor(wst[:, half, 4:5], wst[:, half, 2:3], wst[:, half, 3:4], ALU.add))
                        step(V.reciprocal(wst[:, half, 5:6], wst[:, half, 4:5]))
                        step(V.tensor_scalar(sp_[:, half, 0:w], sp_[:, half, 0:w], wst[:, half, 5:6], None,
                                             ALU.mult))
                        V.sem_inc(w_pm, 1)

                    peak_w(0)
                    for x in range(8):
                        if x < 7:
                            peak_w(x + 1)
                        weigh_w(x)
                    V.wait_ge(w_or, m + 1)
                    V.tensor_tensor(ys_lo[:, ds(m, 1), :].rearrange("p a s -> p (a s)"), bank[7][:, :],
                                    ys_hi[:, ds(m, 1), :].rearrange("p a s -> p (a s)"), ALU.subtract) \
                     .then_inc(w_os, 1)
            step.leave(2)

            V.wait_ge(decay_loaded, 16)
            step.enter(0, 3)
            with V.Fori(0, RET_H) as i:
                step.i = i
                low_a(A_RET + 1, i)
                V.tensor_copy(rq[:, :], tile(A_RET, 0, A_RET + 2 * i)[:, :]).then_inc(tile_free, 1)
                V.tensor_copy(rk[:, :], tile(A_RET, 1, A_RET + 2 * i)[:, :]).then_inc(tile_free, 1)
                low_a(A_RET + 2, i)
                b = tile(A_RET + 1, 1, A_RET + 1 + 2 * i)
                V.wait_ge(r_gate, i + 1)
                V.tensor_copy(rv[:, :], b[:, :]).then_inc(tile_free, 2)
                for j in range(4):
                    V.wait_ge(r_sc, 4 * i + j + 1)
                    V.wait_ge(r_o, 4 * i + j - 1 if j >= 2 else 4 * i)
                    V.tensor_tensor(srt[:, j % 2, 0:S - j * P], bank[4 + j % 2][:, 0:S - j * P],
                                    dk[:, ds(i, 1), 0:S - j * P].rearrange("p a s -> p (a s)"), ALU.mult) \
                     .then_inc(r_dec, 1)
                V.wait_ge(r_o, 4 * i + 4)
                V.tensor_copy(ry[:, :], bank[6][:, :]).then_inc(r_y, 1)
                V.wait_ge(r_mean, i + 1)
                V.wait_ge(r_rounded, i)
                V.scalar_tensor_tensor(ryc[:, :], bank[7][:, :], -1.0 / P, ry[:, :], ALU.mult, ALU.add) \
                 .then_inc(r_c, 1)
                V.wait_ge(r_sd, i + 1)
                step(V.reciprocal(rstd[:, :], sd[:, :]))
                step(V.scalar_tensor_tensor(ryc[:, :], ryc[:, :], sm[:, ds(SM["ret_g"] + i, 1)], rstd[:, :],
                                            ALU.mult, ALU.mult))
                V.scalar_tensor_tensor(ryc[:, :], ryc[:, :], sm[:, ds(SM["ret_b"] + i, 1)], rgs[:, :],
                                       ALU.add, ALU.mult).then_inc(r_g, 1)
                V.wait_ge(r_rounded, i + 1)
                step(V.tensor_tensor(yr_lo[:, ds(i, 1), :].rearrange("p a s -> p (a s)"), ryc[:, :],
                                     yr_hi[:, ds(i, 1), :].rearrange("p a s -> p (a s)"), ALU.subtract))
                V.sem_inc(r_split, 1)
            step.leave(RET_H)

            step.enter(0, 4)
            with V.Fori(0, KT // 2) as i:
                step.i = i
                for u in range(2):
                    s = A_MRG + u
                    n = s + 2 * i
                    nb = B_MRG + u + 2 * i
                    low_a(s + 1, i)
                    low_b(B_MRG + u, i)
                    V.wait_ge(mg_gate, 2 * (2 * i + u) + 2)
                    V.wait_ge(y_ready, 4 * nb + 2)
                    V.wait_ge(mg_ready, 2 * i + u)
                    step(V.tensor_tensor(tmp[:, 1, :], bank[4 + 2 * u][:, :], sgt[:, 0, :], ALU.mult))
                    V.wait_ge(y_ready, 4 * nb + 4)
                    step(V.tensor_tensor(tmp[:, 0, :], bank[5 + 2 * u][:, :], sgt[:, 1, :], ALU.mult))
                    V.sem_inc(tile_free, 2)
                    V.sem_inc(y_free, 4)
                    V.tensor_tensor(tmp[:, 0, :], tmp[:, 0, :], tmp[:, 1, :], ALU.add).then_inc(mg_sum, 1)
                    V.wait_ge(mg_rounded, 2 * i + u + 1)
                    V.tensor_tensor(mg_lo[:, ds(2 * i + u, 1), :].rearrange("p a s -> p (a s)"), tmp[:, 0, :],
                                    mg_hi[:, ds(2 * i + u, 1), :].rearrange("p a s -> p (a s)"), ALU.subtract) \
                     .then_inc(mg_ready, 1)
            step.leave(KT // 2)
            add_tiles(A_OUT)
            normalise(N_MOE, 7)

            low_a(A_ROUTE + 1)
            V.wait_ge(tile_ready, 2 * A_ROUTE + 2)
            step(V.tensor_tensor(logit[:, :, :], bank[2 * (A_ROUTE % 2)][:, 0:NT * NROUTE]
                                 .rearrange("p (t c) -> p t c", t=NT),
                                 smc("route_b", 0, NT * NROUTE).rearrange("p (t c) -> p t c", t=NT), ALU.add))
            V.sem_inc(tile_free, 2)

            def wide(x, n):
                return x.rearrange("p (t o) -> p t o", o=1).to_broadcast([P, NT, n])

            def best(dst, mark, x, prio, n, top):
                step(V.tensor_reduce(top, x, AX_X, ALU.max))
                step(V.tensor_tensor(mark, x, wide(top, n), ALU.is_ge))
                step(V.tensor_tensor(mark, mark, prio, ALU.mult))
                step(V.tensor_reduce(rt[:, 0, :], mark, AX_X, ALU.max))
                step(V.tensor_tensor(dst, mark, wide(rt[:, 0, :], n), ALU.is_equal))

            gl = logit[:, :, 0:EGROUPS]
            pg = cnc("prio_g", NT * EGROUPS).rearrange("p (t c) -> p t c", t=NT)
            pe_ = cnc("prio_e", NT * EPG).rearrange("p (t c) -> p t c", t=NT)
            best(rtg[:, 2, :, :], rtg[:, 3, :, :], gl, pg, EGROUPS, rt[:, 1, :])
            step(V.tensor_tensor(rtg[:, 0, :, :], gl, wide(rt[:, 1, :], EGROUPS), ALU.subtract))
            for g in range(EGROUPS):
                lg = logit[:, :, EGROUPS + g * EPG:EGROUPS + (g + 1) * EPG]
                mark = rtg[:, 2, :, g:g + 1].to_broadcast([P, NT, EPG])
                dst = rte[:, 0, :, :] if g == 0 else rte[:, 1, :, :]
                step(V.tensor_tensor(dst, lg, mark, ALU.mult))
                if g:
                    step(V.tensor_tensor(rte[:, 0, :, :], rte[:, 0, :, :], rte[:, 1, :, :], ALU.add))
            best(rte[:, 2, :, :], rte[:, 3, :, :], rte[:, 0, :, :], pe_, EPG, rt[:, 2, :])
            step(V.tensor_scalar(rte[:, 4, :, :], rte[:, 2, :, :], 2 * NEG, None, ALU.mult))
            step(V.tensor_tensor(rte[:, 4, :, :], rte[:, 4, :, :], rte[:, 0, :, :], ALU.add))
            best(rte[:, 5, :, :], rte[:, 6, :, :], rte[:, 4, :, :], pe_, EPG, rt[:, 3, :])
            step(V.tensor_tensor(rt[:, 4, :], rt[:, 3, :], rt[:, 2, :], ALU.subtract))
            V.sem_inc(rt_in, 1)
            V.wait_ge(rt_exp, 1)
            step(V.tensor_reduce(rt[:, 6, :], rtg[:, 1, :, :], AX_X, ALU.add))
            step(V.tensor_scalar(rt[:, 7, :], rt[:, 5, :], 1.0, None, ALU.add))
            step(V.tensor_tensor(rt[:, 8, :], rt[:, 6, :], rt[:, 7, :], ALU.mult))
            step(V.reciprocal(rt[:, 9, :], rt[:, 8, :]))
            step(V.tensor_tensor(rt[:, 10, :], rt[:, 9, :], rt[:, 5, :], ALU.mult))
            step(V.tensor_tensor(rte[:, 7, :, :], rte[:, 2, :, :], wide(rt[:, 9, :], EPG), ALU.mult))
            step(V.tensor_tensor(rte[:, 8, :, :], rte[:, 5, :, :], wide(rt[:, 10, :], EPG), ALU.mult))
            step(V.tensor_tensor(rte[:, 9, :, :], rte[:, 7, :, :], rte[:, 8, :, :], ALU.add))
            for g in range(EGROUPS):
                step(V.tensor_tensor(cmb[:, :, g * EPG:(g + 1) * EPG], rte[:, 9, :, :],
                                     rtg[:, 2, :, g:g + 1].to_broadcast([P, NT, EPG]), ALU.mult))
            V.sem_inc(rt_done, 1)
            V.wait_ge(cmbt_mm, 1)
            V.tensor_copy(cmbt[:, :], bank[4][0:EXPERTS, :]).then_inc(cmbt_done, 1)
            ffn(A_MOE, B_MOE, E_MOE, EXPERTS, weighted=True)

            V.wait_ge(p_rounded, 1)
            V.tensor_tensor(ptr_lo[:, :, :], ptr[:, :, :], ptr_hi[:, :, :], ALU.subtract).then_inc(p_ready, 1)
            low_a(A_PLE + 1)
            normalise(N_PLEG, 8)
            for m in range(KT):
                V.wait_ge(ple_mm, m + 1)
                V.tensor_copy(ple[:, m, :], bank[m % 2 + 2 * (A_PLE % 2)][:, :]).then_inc(pg_done, 1)
            V.wait_ge(pg_done, KT)
            V.sem_inc(tile_free, 2)
            inverse_root(N_PLE)
            for m in range(KT):
                ins = V.scalar_tensor_tensor(ple[:, m, :], ple[:, m, :], smc("gain", KT * 9 + m), rstd[:, :],
                                             ALU.mult, ALU.mult)
            step(ins)
            for p in range(4):
                s = A_PG + p
                if p < 3:
                    low_a(s + 1)
                for j in range(2):
                    m = 2 * p + j
                    V.wait_ge(out_done, m + 1)
                    step(V.tensor_tensor(ple[:, m, :], ple[:, m, :], pgs[:, j, :], ALU.mult))
                    V.tensor_tensor(h[:, m, :], h[:, m, :], ple[:, m, :], ALU.add).then_inc(tile_free, 1)

        @block.gpsimd
        def _(pool):
            def rnn_pair(i):
                for u in range(2):
                    n = 2 * i + u
                    pool.wait_ge(xc_done, n + 1)
                    pool.wait_ge(tile_free, 2 * n + 2)
                    pool.tensor_tensor(gx[:, u, :], ig[:, u, :], xc[:, u, :], ALU.mult).then_inc(gx_done, 1)
                for u in range(2):
                    n = 2 * i + u
                    pool.wait_ge(decay_done, 2 * n + 2)
                    pool.tensor_tensor(mu[:, u, :], aa[:, u, :], aa[:, u, :], ALU.mult).then_inc(asq_done, 1)
                for u in range(2):
                    n = 2 * i + u
                    pool.wait_ge(mult_done, n + 1)
                    pool.wait_ge(gx_done, n + 1)
                    pool.tensor_tensor(gx[:, u, :], gx[:, u, :], mu[:, u, :], ALU.mult).then_inc(bx_done, 1)
                for u in range(2):
                    n = 2 * i + u
                    pool.wait_ge(scan_done, n + 1)
                    pool.wait_ge(gelu_done, n + 1)
                    pool.tensor_tensor(hs[:, u, :], hs[:, u, :], gel[:, u, :], ALU.mult).then_inc(rec_done, 1)

            with pool.Fori(0, RNN_BLOCKS // 2) as i:
                rnn_pair(i)

            pool.wait_ge(hn_ready, KT * (N_KV + 1))
            pool.dma_start(cs[:, :, :], rope).then_inc(rope_loaded, 16)
            with pool.Fori(0, HEADS // 4) as i:
                for u in range(2):
                    pool.wait_ge(rope_done, 8 + 4 * i + 2 * u + 2)
                    pool.dma_start(q_dram[ds(4 * i + 2 * u, 2)].rearrange("a p n -> p a n"),
                                   qb[:, 2 * u:2 * u + 2, :, :].rearrange("p a b n -> p a (b n)")) \
                        .then_inc(q_stored[u], 16)
            for u in range(2):
                pool.wait_ge(q_stored[u], 16 * (HEADS // 4))
            with pool.Fori(0, GROUPS) as g:
                pool.wait_ge(o_ready, HPG * g)
                for b in range(2):
                    pool.tensor_copy(vs[:, b, :, :], vn[:, b, :, ds(g * DV, DV)]).then_inc(v_staged, 1)
                pool.tensor_copy(vcs[:, :], vcn[:, ds(g, 1), :].rearrange("p a c -> p (a c)")).then_inc(v_staged, 1)
                for u in range(HPG):
                    if u >= 2:
                        pool.wait_ge(sc_ready, 8 * (HPG * g + u - 1))
                    pool.dma_start(qs[:, u % 2, :, :].rearrange("p b n -> p (b n)"),
                                   q_dram[ds(HPG * g + u, 1)].rearrange("a p n -> p (a n)")) \
                        .then_inc(q_staged[u % 2], 16)

            pool.wait_ge(hn_ready, KT * (N_MIX2 + 1))
            pool.dma_start(al[:, :, :], alibi).then_inc(alibi_loaded, 16)
            pool.wait_ge(w_os, SWA_TILES)
            pool.dma_start(dk[:, :, :], decay).then_inc(decay_loaded, 16)

            pool.wait_ge(cmbt_done, 1)
            pool.dma_start(c_dram, cmbt[:, :]).then_inc(comb_stored, 16)
            pool.wait_ge(comb_stored, 16)
            pool.dma_start(comb[:, 0, :], c_dram[0:1, :].to_broadcast([P, S])).then_inc(comb_loaded[0], 16)
            with pool.Fori(1, EXPERTS) as i:
                pool.wait_ge(tile_free, 2 * (A_MOE + 2 * i))
                pool.dma_start(comb[:, 0, :], c_dram[ds(i, 1), :].to_broadcast([P, S])) \
                    .then_inc(comb_loaded[0], 16)

            pool.wait_ge(y_free, 4 * NB)
            pool.dma_start(ptr[:, :, :], p_t.rearrange("(k p) s -> p k s", p=P)).then_inc(p_loaded, 16)
            out_v = out_t.rearrange("(k p) s -> p k s", p=P)
            for m in range(KT):
                pool.wait_ge(tile_free, 2 * A_PG + m + 1)
                pool.dma_start(out_v[:, m, :], h[:, m, :]).then_inc(stored, 16)
            pool.wait_ge(stored, 16 * KT)


def _pack_a(v):
    out = np.zeros((v.shape[0], P, WA), np.float32)
    out[:, :v.shape[1], :v.shape[2]] = v
    return out


def _cols(w, groups):
    k = w.shape[0] // P
    t = w.reshape(k, P, -1)
    return _pack_a(np.stack([np.concatenate([t[:, :, c] for c in g], 2).transpose(1, 0, 2).reshape(P, -1)
                             for g in groups]))


def _pairs(w, width, step=2):
    n = w.shape[1] // width
    return _cols(w, [[slice(i * width, (i + step) * width)] for i in range(0, n, step)])


def _down(w, rows):
    v = w.reshape(-1, 2, rows, 2, 512).transpose(0, 3, 2, 1, 4).reshape(-1, rows, WB)
    out = np.zeros((v.shape[0], P, WB), np.float32)
    out[:, :rows] = v
    return out


def _panels(x):
    a = []
    w_in = x["a_w_in"][0]
    gates = np.concatenate([x["a_w_ra"][0], x["a_w_ix"][0]], 2)
    rnn = _cols(w_in, [[slice(c * RNN_W, (c + 1) * RNN_W), slice(1536 + c * RNN_W, 1536 + (c + 1) * RNN_W)]
                       for c in range(RNN_BLOCKS)])
    rnn[:, :RNN_W, 1536:1728] = gates
    a.append(rnn)

    def ff(w):
        n = w.shape[1] // 2
        return _cols(w, [[slice(f * P, (f + 1) * P), slice(n + f * P, n + (f + 1) * P)] for f in range(n // P)])

    a.append(ff(x["ffn_w_gu"][0]))
    kc, vc, ks, vs, kw, vw = np.split(x["kv_w"], np.cumsum([384, 256, 384, 256, 384])[:5], 1)
    a += [_pairs(kc, DQK), _pairs(vc, P), _pairs(ks, DQK), _pairs(kw, DQK), _cols(vs, [[slice(0, 256)]]),
          _cols(vw, [[slice(0, 256)]])]
    for w, d in ((x["cmp_w1_k"], DQK), (x["cmp_w1_v"], DV)):
        a.append(_pack_a(w.reshape(4, 8, d, 256).transpose(0, 2, 1, 3).reshape(4, d, 2048)))
    w_q = x["b_w_q"][0]
    a += [_cols(w_q, [[slice(HEADS * DQK, HEADS * DQK + NGATE)]]), _pairs(w_q[:, :HEADS * DQK], DQK)]
    a.append(_pairs(x["b_w_o"][0], P))
    a.append(ff(x["ffn_w_gu"][1]))
    rq, rk, rv, rg, sq, sk, sv, gr, gs = np.split(
        x["w_in_2"][0], np.cumsum([512, 512, 512, 512, 512, 128, 128, 1024]), 1)
    order = np.concatenate([np.arange(64 * q, 64 * q + 64) for m in range(4) for q in (m, m + 4)])
    a.append(_cols(np.concatenate([sk, sv], 1), [[slice(0, 256)]]))
    sqp = np.zeros((D, 1024), np.float32)
    for m in range(4):
        sqp[:, m * 256:m * 256 + 128] = sq[:, order[m * 128:(m + 1) * 128]]
    a.append(_pairs(sqp, P))
    ret = np.concatenate([rq, rk, rg, rv], 1)
    a.append(_cols(ret, [[slice(o + i * P, o + (i + 1) * P), slice(o + 512 + i * P, o + 512 + (i + 1) * P)]
                         for i in range(RET_H) for o in (0, 1024)]))
    a.append(_cols(np.concatenate([gr, gs], 1), [[slice(m * P, (m + 1) * P), slice(D + m * P, D + (m + 1) * P)]
                                                 for m in range(KT)]))
    a.append(_pairs(x["w_out_2"][0], P))
    a.append(_cols(np.concatenate([x["w_router_group_2"][0], x["w_router_expert_2"][0]], 1),
                   [[slice(0, NROUTE)]]))
    eg, eu = x["w_exp_gate_2"][0], x["w_exp_up_2"][0]
    v = np.stack([eg.reshape(EXPERTS, KT, P, 2, P), eu.reshape(EXPERTS, KT, P, 2, P)], 4)
    a.append(v.transpose(0, 3, 2, 1, 4, 5).reshape(2 * EXPERTS, P, WA))
    a.append(_cols(x["w_ple_2"][0], [[slice(0, D)]]))
    a.append(_pairs(x["w_ple_gate_2"][0], P))
    w_a = np.concatenate(a)
    assert w_a.shape == (NA, P, WA), w_a.shape
    ret_o = x["w_ret_o_2"][0].reshape(4, P, KT, P).transpose(2, 1, 0, 3).reshape(KT, P, 512)
    swa_o = x["w_swa_o_2"][0][order].reshape(4, P, KT, P).transpose(2, 1, 0, 3).reshape(KT, P, 512)
    b = [_down(x["a_w_out"][0], RNN_W), _down(x["ffn_w_down"][0], P), _down(x["ffn_w_down"][1], P),
         np.concatenate([ret_o, swa_o], 2), _down(x["w_exp_down_2"][0].reshape(EXPERTS * EFF, D), P)]
    w_b = np.concatenate(b)
    assert w_b.shape == (NB, P, WB), w_b.shape
    return w_a, w_b


def _small(x):
    out = np.zeros((P, N_SMALL), np.float32)

    def put(name, v):
        out[:v.shape[0], SM[name]:SM[name] + v.shape[1]] = v

    gains = [x["norm_g"][0, 0], x["norm_g"][0, 1], x["kv_norm_g"], x["norm_g"][1, 0], x["norm_g"][1, 1],
             x["final_g"], x["mix_norm_g_2"][0], x["ffn_norm_g_2"][0], x["ple_gate_norm_g_2"][0],
             x["ple_norm_g_2"][0]]
    put("gain", np.concatenate([g.reshape(KT, P).T for g in gains], 1))
    put("conv_w", x["a_conv_w"][0].reshape(4, RNN_BLOCKS, RNN_W).transpose(2, 1, 0).reshape(RNN_W, -1))
    put("conv_b", x["a_conv_b"][0].reshape(RNN_BLOCKS, RNN_W).T)
    put("b_ra", x["a_b_ra"][0].T)
    put("b_ix", x["a_b_ix"][0].T)
    put("lam", x["a_lambda"][0].reshape(RNN_BLOCKS, RNN_W).T)
    put("pos_k", x["cmp_pos_k"].T)
    put("pos_v", x["cmp_pos_v"].T)
    put("gate_b", np.broadcast_to(np.tile(x["b_gate_bias"][0], NT), (P, NT * NGATE)))
    put("ret_g", x["ret_gn_g_2"][0].reshape(RET_H, P).T)
    put("ret_b", x["ret_gn_b_2"][0].reshape(RET_H, P).T)
    put("q_g", np.tile(x["q_norm_g_2"][0], 2)[:, None])
    put("k_g", np.tile(x["k_norm_g_2"][0], 2)[:, None])
    put("sink", np.broadcast_to(x["attn_sinks_2"][0].reshape(2, 4).T.reshape(-1), (P, SWA_H)))
    put("route_b", np.broadcast_to(np.tile(np.concatenate(
        [x["b_router_group_2"][0], x["b_router_expert_2"][0]]), NT), (P, NT * NROUTE)))
    put("w2k", x["cmp_w2_k"].reshape(2, P, DQK).transpose(1, 0, 2).reshape(P, -1))
    put("w2v", x["cmp_w2_v"].reshape(2, P, DV).transpose(1, 0, 2).reshape(P, -1))
    return out


def _constants():
    out = np.zeros((P, N_CONST), np.float32)

    def put(name, v):
        out[:v.shape[0], CN[name]:CN[name] + v.shape[1]] = v

    r = np.arange(P)
    put("eps", np.full((P, 1), EPS))
    put("ident", np.eye(P))
    put("ones", np.ones((P, P)))
    put("halves", (r[:, None] // 64 == r[None, :] // 64).astype(np.float32))
    rot = np.zeros((DQK, DQK))
    for k in range(12):
        rot[k + 12, k] = 1.0
        rot[k, k + 12] = 1.0
    put("rot", rot)
    put("causal", np.where(r[None, :] <= r[:, None], 0.0, NEG))
    t = np.arange(S).reshape(NT, P)
    c_end = np.arange(NCMP) * CSTRIDE + CBLOCK - 1
    put("cmp_mask", np.where(c_end[None, None, :] <= t[:, :, None], 0.0, NEG)
        .transpose(1, 0, 2).reshape(P, -1))
    put("prio_g", np.tile(EGROUPS - np.arange(EGROUPS), (P, NT)))
    put("prio_e", np.tile(EPG - np.arange(EPG), (P, NT)))

    inv = np.float32(500000.0) ** (-np.arange(12, dtype=np.float32) * np.float32(2.0) / np.float32(24))
    ang = (np.arange(S, dtype=np.float32)[:, None] * inv[None, :].astype(np.float32)).astype(np.float64)
    rope = np.zeros((DQK, 2, S), np.float32)
    rope[:, 0] = 1.0
    rope[:12, 0] = rope[12:24, 0] = np.cos(ang).T
    rope[:12, 1] = -np.sin(ang).T
    rope[12:24, 1] = np.sin(ang).T

    c = np.arange(S)
    decay = np.zeros((P, RET_H, S))
    for i in range(RET_H):
        lg = np.log1p(-2.0 ** (-5.0 - i))
        d = c[None, :] - r[:, None]
        decay[:, i] = np.where(d >= 0, np.exp(np.maximum(d, 0) * lg), 0.0) * 128 ** -0.5
    alibi = np.zeros((P, SWA_H, 2 * P))
    rel = r[:, None] + P - np.arange(2 * P)[None, :]
    for m in range(4):
        for half in range(2):
            slope = 2.0 ** (-(m + 4 * half + 1.0))
            alibi[:, 2 * m + half] = np.where((rel >= 0) & (rel < P), -slope * rel, NEG)
    return out, rope, decay.astype(np.float32), alibi.astype(np.float32)


def kernel(**inputs):
    import concourse.bacc as bacc
    from concourse.bass_utils import run_bass_kernel_spmd

    x = {k: np.asarray(v) for k, v in inputs.items()}
    w_a, w_b = _panels(x)
    const, rope, decay, alibi = _constants()
    arrays = {
        "x_t": np.ascontiguousarray(x["x"][0].T), "p_t": np.ascontiguousarray(x["p_2"][0, 0].T),
        "w_a": w_a, "w_b": w_b, "small": _small(x), "const": const, "rope": rope, "decay": decay, "alibi": alibi,
    }
    nc = bacc.Bacc("TRN2", target_bir_lowering=False, num_devices=1)
    aps = [nc.dram_tensor(k, v.shape, F32, kind="ExternalInput").ap() for k, v in arrays.items()]
    out = nc.dram_tensor("out_t", (D, S), F32, kind="ExternalOutput").ap()
    build(nc, *aps, out)
    r = run_bass_kernel_spmd(nc, [arrays], core_ids=[0])
    return r.results[0]["out_t"].T[None]
```

```python
from contextlib import ExitStack

import numpy as np

import concourse.bass as bass
from concourse import mybir

F32 = mybir.dt.float32
F32R = mybir.dt.float32r
I32 = mybir.dt.int32
ALU = mybir.AluOpType
ACT = mybir.ActivationFunctionType
AX_X = mybir.AxisListType.X

P = 128
S = 512
D = 1024
KT = D // P
NT = S // P
EPS = 1e-6
NEG = -1e30

RNN_BLOCKS, RNN_W = 16, 96
FF_TILES = 2816 // P
HEADS, GROUPS, DQK, DV = 16, 4, 96, 64
HPG = HEADS // GROUPS
NCMP, CSTRIDE, CBLOCK = 31, 16, 32
NGATE = 3 * HEADS
RET_H = 4
SWA_H, SWA_HD, SWA_TILES = 8, 64, 4
EXPERTS, EGROUPS, EPG, EFF = 32, 4, 8, 256
NROUTE = EGROUPS + EXPERTS
XB = 256
XITEMS = S // XB + EGROUPS - 1
XSUB = XB // P

WA, WB = 2048, 1024

A_RNN = 0
A_FF0 = A_RNN + RNN_BLOCKS
A_KCMP = A_FF0 + FF_TILES
A_VCMP = A_KCMP + 2
A_KSEL = A_VCMP + 1
A_KWIN = A_KSEL + 2
A_VNAT = A_KWIN + 2
A_W1K = A_VNAT + 2
A_W1V = A_W1K + 4
A_GATE = A_W1V + 4
A_Q = A_GATE + 1
A_WO = A_Q + HEADS // 2
A_FF1 = A_WO + 4
A_SKV = A_FF1 + FF_TILES
A_SQ = A_SKV + 1
A_RET = A_SQ + SWA_TILES
A_MRG = A_RET + 2 * RET_H
A_OUT = A_MRG + KT
A_ROUTE = A_OUT + 4
A_MOE = A_ROUTE + 1
A_PLE = A_MOE + 2 * XITEMS * EPG
A_PG = A_PLE + 1
NA = A_PG + 4

B_RNN = 0
B_FF0 = B_RNN + RNN_BLOCKS
B_FF1 = B_FF0 + FF_TILES
B_MRG = B_FF1 + FF_TILES
B_MOE = B_MRG + KT
NB = B_MOE + 2 * XITEMS * EPG
REPEATED = 2 * (XITEMS * EPG - EXPERTS)

E_RNN = 0
E_FF0 = E_RNN + RNN_BLOCKS // 2
E_FF1 = E_FF0 + FF_TILES // 2
E_MOE = E_FF1 + FF_TILES // 2

(N_MIX0, N_FFN0, N_KV, N_MIX1, N_FFN1, N_FINAL, N_MIX2, N_MOE, N_PLEG, N_PLE) = range(10)

_SMALL = [("gain", 10 * KT), ("conv_w", 4 * RNN_BLOCKS), ("conv_b", RNN_BLOCKS), ("b_ra", RNN_BLOCKS),
          ("b_ix", RNN_BLOCKS), ("lam", RNN_BLOCKS), ("pos_k", CBLOCK), ("pos_v", CBLOCK),
          ("gate_b", NT * NGATE), ("ret_g", RET_H), ("ret_b", RET_H), ("q_g", 1), ("k_g", 1),
          ("sink", SWA_H), ("route_b", NT * NROUTE), ("w2k", 2 * DQK), ("w2v", 2 * DV)]
_CONST = [("eps", 1), ("ident", P), ("ones", P), ("halves", P), ("rot", DQK), ("causal", P),
          ("cmp_mask", NT * NCMP), ("prio_g", NT * EGROUPS), ("prio_e", NT * EPG),
          ("upto", P), ("iota", XB), ("slot_id", XITEMS * XSUB)]


def _columns(parts):
    at, out = 0, {}
    for name, n in parts:
        out[name] = at
        at += n
    return out, at


SM, N_SMALL = _columns(_SMALL)
CN, N_CONST = _columns(_CONST)


WIN = [(1, 0, 2 * P, 0), (2, P, 2 * P, 2 * P), (3, 2 * P, 2 * P, 4 * P), (0, 0, P, 6 * P)]


class Steps:

    def __init__(self, eng, sem):
        self.eng, self.sem = eng, sem
        self.base = self.count = self.per = 0
        self.i = 0

    def __call__(self, ins):
        ins.then_inc(self.sem, 1)
        self.count += 1
        self.eng.wait_ge(self.sem, self.base + self.per * self.i + self.count)

    def enter(self, i, per):
        self.base += self.count
        self.i, self.per, self.count = i, per, 0

    def leave(self, trips):
        assert self.count == self.per, f"the loop takes {self.count} steps"
        self.base += self.per * trips
        self.i = self.per = self.count = 0


def build(nc, x_t, p_t, w_a, w_b, small, const, rope, decay, alibi, out_t):
    ctx = ExitStack()
    with ctx:
        def sem(name):
            return ctx.enter_context(nc.semaphore(name))

        def sb(name, shape, dt=F32, stack=None):
            return (stack or ctx).enter_context(nc.sbuf_tensor(name, shape, dt))

        a_raw = [sb(f"a_raw{i}", [P, WA]) for i in range(2)]
        a_hi = [sb(f"a_hi{i}", [P, WA], F32R) for i in range(2)]
        a_lo = [sb(f"a_lo{i}", [P, WA], F32R) for i in range(2)]
        b_raw = [sb(f"b_raw{i}", [P, WB]) for i in range(2)]
        b_hi = [sb(f"b_hi{i}", [P, WB], F32R) for i in range(2)]
        b_lo = [sb(f"b_lo{i}", [P, WB], F32R) for i in range(2)]
        h = sb("h", [P, KT, S])
        hn_hi = sb("hn_hi", [P, KT, S], F32R)
        hn_lo = sb("hn_lo", [P, KT, S], F32R)
        tmp = sb("tmp", [P, 2, S])
        sq = sb("sq", [P, 2, S])
        sd = sb("sd", [P, S])
        rstd = sb("rstd", [P, S])
        sm = sb("sm", [P, N_SMALL])
        cn = sb("cn", [P, N_CONST])
        psum = ctx.enter_context(nc.psum_tensor("psum", [P, 8, S], F32))
        bank = [psum[:, i, :] for i in range(8)]
        masks = sb("masks", [P, 2, P], mybir.dt.bfloat16)
        xsg, xhid, xcomb = tmp[:, :, 0:XB], tmp[:, :, XB:2 * XB], sq[:, 0, 0:XB]
        slot_row, slot_wide = sd, rstd

        def smc(name, k=0, n=1, rows=P):
            return sm[0:rows, SM[name] + k:SM[name] + k + n]

        def cnc(name, n, rows=P):
            return cn[0:rows, CN[name]:CN[name] + n]

        ident, ones = cnc("ident", P), cnc("ones", P)
        halves, rot = cnc("halves", P), cnc("rot", DQK, DQK)
        eps = cnc("eps", 1)

        with ExitStack() as st:
            rhid_hi = sb("rhid_hi", [P, 2, S], F32R, st)
            rhid_lo = sb("rhid_lo", [P, 2, S], F32R, st)
            xc, ybr, rg, ig, gx, aa, pp, mu, hs, gel = (
                sb(nm, [RNN_W, 2, S], F32, st) for nm in
                ("xc", "ybr", "rg", "ig", "gx", "aa", "pp", "mu", "hs", "gel"))
            xc_hi = sb("xc_hi", [RNN_W, 2, S], F32R, st)
            xc_lo = sb("xc_lo", [RNN_W, 2, S], F32R, st)
            spt = sb("spt", [RNN_W, 8, RNN_BLOCKS], F32, st)
        with ExitStack() as st:
            hid_hi = sb("hid_hi", [P, 2, S], F32R, st)
            hid_lo = sb("hid_lo", [P, 2, S], F32R, st)
            hid = sb("hid", [P, 2, S], F32, st)
            sg = sb("sg", [P, 2, S], F32, st)
        with ExitStack() as st:
            xhid_hi = sb("xhid_hi", [P, 2, XB], F32R, st)
            xhid_lo = sb("xhid_lo", [P, 2, XB], F32R, st)
            nat_hi = sb("nat_hi", [P, NT, D], F32R, st)
            nat_lo = sb("nat_lo", [P, NT, D], F32R, st)
            xy_hi = sb("xy_hi", [P, XSUB, D], F32R, st)
            xy_lo = sb("xy_lo", [P, XSUB, D], F32R, st)
            sel = sb("sel", [P, NT, XB], F32R, st)
            sel_t = sb("sel_t", [P, XSUB, S], F32R, st)
            ident_r = sb("ident_r", [P, P], F32R, st)
            w_hi = sb("w_hi", [P, NT, EPG], F32R, st)
            w_lo = sb("w_lo", [P, NT, EPG], F32R, st)
            grp = sb("grp", [P, 8, EGROUPS], F32, st)
            rank = sb("rank", [P, NT, EGROUPS], F32, st)
            slot = sb("slot", [P, NT], F32, st)
            item = sb("item", [P, 3, 8], F32, st)
            item_group = sb("item_group", [P, 8], I32, st)
            logit = sb("logit", [P, NT, NROUTE], F32, st)
            rt = sb("rt", [P, 24, NT], F32, st)
            rtg = sb("rtg", [P, 4, NT, EGROUPS], F32, st)
            rte = sb("rte", [P, 12, NT, EPG], F32, st)
            wslot = sb("wslot", [EPG, XB], F32, st)
        with ExitStack() as st:
            kx = sb("kx", [DQK, 2, GROUPS, S], F32, st)
            vn = sb("vn", [P, 2, NT, GROUPS * DV], F32, st)
            kct = sb("kct", [DQK, GROUPS * NCMP], F32, st)
            vcn = sb("vcn", [NCMP, GROUPS, DV], F32, st)
            gates = sb("gates", [P, NT, NGATE], F32, st)
            s1 = st.enter_context(ExitStack())
            cs = sb("cs", [DQK, 2, S], F32, s1)
            rtmp = sb("rtmp", [DQK, 2, S], F32, s1)
            with ExitStack() as s2:
                kraw = sb("kraw", [DQK, GROUPS, S], F32, s2)
                vraw = sb("vraw", [DV, GROUPS, S], F32, s2)
                xl = sb("xl", [DQK, 8, GROUPS * NCMP], F32, s2)
                xl_hi = sb("xl_hi", [DQK, 8, GROUPS * NCMP], F32R, s2)
                xl_lo = sb("xl_lo", [DQK, 8, GROUPS * NCMP], F32R, s2)
                chid = sb("chid", [P, 2, GROUPS * NCMP], F32, s2)
            with ExitStack() as s2:
                qb = sb("qb", [DQK, 4, 2, S], F32, s2)
            s1.close()
            with ExitStack() as s2:
                qs = sb("qs", [DQK, 2, 2, S], F32, s2)
                vs = sb("vs", [P, 2, NT, DV], F32, s2)
                vcs = sb("vcs", [NCMP, DV], F32, s2)
                pm = sb("pm", [P, 2, 2, S], F32, s2)
                pt = sb("pt", [P, 2, NT, S], F32, s2)
                pc = sb("pc", [P, NT, NCMP], F32, s2)
                ptc = sb("ptc", [NCMP, S], F32, s2)
                ast = sb("ast", [P, 2, 8], F32, s2)
                cst = sb("cst", [P, 4, NT], F32, s2)
        with ExitStack() as st:
            ys_hi = sb("ys_hi", [P, SWA_TILES, S], F32R, st)
            ys_lo = sb("ys_lo", [P, SWA_TILES, S], F32R, st)
            yr_hi = sb("yr_hi", [P, RET_H, S], F32R, st)
            yr_lo = sb("yr_lo", [P, RET_H, S], F32R, st)
            with ExitStack() as s2:
                al = sb("al", [P, SWA_H, 2 * P], F32, s2)
                sk = sb("sk", [P, S], F32, s2)
                sv = sb("sv", [P, NT, P], F32, s2)
                qn = sb("qn", [P, S], F32, s2)
                wp = sb("wp", [P, 2, 7 * P], F32, s2)
                wpt = sb("wpt", [P, 2, 7 * P], F32, s2)
                wst = sb("wst", [P, 2, 20], F32, s2)
            with ExitStack() as s2:
                dk = sb("dk", [P, RET_H, S], F32, s2)
                rq = sb("rq", [P, S], F32, s2)
                rk = sb("rk", [P, S], F32, s2)
                rv = sb("rv", [P, S], F32, s2)
                rgs = sb("rgs", [P, S], F32, s2)
                srt = sb("srt", [P, 2, S], F32, s2)
                ry = sb("ry", [P, S], F32, s2)
                ryc = sb("ryc", [P, S], F32, s2)
            with ExitStack() as s2:
                mg_hi = sb("mg_hi", [P, KT, S], F32R, s2)
                mg_lo = sb("mg_lo", [P, KT, S], F32R, s2)
        with ExitStack() as st:
            ptr = sb("ptr", [P, 2, S], F32, st)
            ptr_hi = sb("ptr_hi", [P, 2, S], F32R, st)
            ptr_lo = sb("ptr_lo", [P, 2, S], F32R, st)
            ple = sb("ple", [P, KT, S], F32, st)
            pgs = sb("pgs", [P, 2, S], F32, st)

        q_dram = nc.dram_tensor("q_scratch", (HEADS, DQK, 2 * S), F32, kind="Internal").ap()
        c_dram = nc.dram_tensor("combine_scratch", (XITEMS * EPG, XB), F32, kind="Internal").ap()

        a_loaded = [sem(f"a_loaded{i}") for i in range(2)]
        b_loaded = [sem(f"b_loaded{i}") for i in range(2)]
        a_rounded, a_ready = sem("a_rounded"), sem("a_ready")
        b_rounded, b_ready = sem("b_rounded"), sem("b_ready")
        tile_ready, tile_free = sem("tile_ready"), sem("tile_free")
        y_ready, y_free = sem("y_ready"), sem("y_free")
        gate_done, hid_rounded, hid_ready = sem("gate_done"), sem("hid_rounded"), sem("hid_ready")
        params, consts, x_loaded = sem("params"), sem("consts"), sem("x_loaded")
        sq_ready, stat_mm, sd_ready = sem("sq_ready"), sem("stat_mm"), sem("sd_ready")
        hn_scaled, hn_rounded, hn_ready = sem("hn_scaled"), sem("hn_rounded"), sem("hn_ready")
        dve_step, act_step, dve_rstd, ple_mm = sem("dve_step"), sem("act_step"), sem("rstd_done"), sem("ple_mm")
        sp_exp, sp_one, sp_ln, sp_done = sem("sp_exp"), sem("sp_one"), sem("sp_ln"), sem("sp_done")
        xb_ready, yb_ready, xc_done, xc_rounded = sem("xb_ready"), sem("yb_ready"), sem("xc_done"), sem("xc_rounded")
        xc_ready, yb_copied, gx_done = sem("xc_ready"), sem("yb_copied"), sem("gx_done")
        gelu_done, decay_done, asq_done = sem("gelu_done"), sem("decay_done"), sem("asq_done")
        m2_done, mult_done, bx_done, scan_done, rec_done = (
            sem("m2_done"), sem("mult_done"), sem("bx_done"), sem("scan_done"), sem("rec_done"))
        rope_mm, rope_done = sem("rope_mm"), sem("rope_done")
        xl_done, xl_rounded, xl_ready, cmp_mm, chid_done, cmp_w2, cmp_done = (
            sem("xl_done"), sem("xl_rounded"), sem("xl_ready"), sem("cmp_mm"), sem("chid_done"),
            sem("cmp_w2"), sem("cmp_done"))
        gates_in, gates_done = sem("gates_in"), sem("gates_done")
        q_stored = [sem(f"q_stored{i}") for i in range(2)]
        q_staged = [sem(f"q_staged{i}") for i in range(2)]
        v_staged, q_free = sem("v_staged"), sem("q_free")
        sc_ready, mx_done, exp_done, pm_ready, tr_ready, pt_ready = (
            sem("sc_ready"), sem("mx_done"), sem("exp_done"), sem("pm_ready"), sem("tr_ready"), sem("pt_ready"))
        csc_ready, csub_done, cexp_done, cpm_ready, ctr_ready, cpt_ready = (
            sem("csc_ready"), sem("csub_done"), sem("cexp_done"), sem("cpm_ready"), sem("ctr_ready"), sem("cpt_ready"))
        o_ready, o_rounded, o_split = sem("o_ready"), sem("o_rounded"), sem("o_split")
        rope_loaded, alibi_loaded, decay_loaded, p_loaded = (
            sem("rope_loaded"), sem("alibi_loaded"), sem("decay_loaded"), sem("p_loaded"))
        qk_raw, qk_sq, qk_mm, qk_sd, qk_norm = (
            sem("qk_raw"), sem("qk_sq"), sem("qk_mm"), sem("qk_sd"), sem("qk_norm"))
        w_sc, w_mx, w_exp, w_pm, w_tr, w_pt, w_o, w_or, w_os = (
            sem("w_sc"), sem("w_mx"), sem("w_exp"), sem("w_pm"), sem("w_tr"), sem("w_pt"), sem("w_o"),
            sem("w_o_rounded"), sem("w_o_split"))
        r_in, r_gate, r_sc, r_dec, r_o, r_y, r_mean, r_c, r_sq, r_var, r_sd, r_g, r_rounded, r_split = (
            sem("r_in"), sem("r_gate"), sem("r_sc"), sem("r_dec"), sem("r_o"), sem("r_y"), sem("r_mean"),
            sem("r_c"), sem("r_sq"), sem("r_var"), sem("r_sd"), sem("r_g"), sem("r_rounded"), sem("r_split"))
        mg_gate, mg_sum, mg_rounded, mg_ready = sem("mg_gate"), sem("mg_sum"), sem("mg_rounded"), sem("mg_ready")
        rt_exp, rt_in, wslot_done, wslot_stored, comb_loaded = (
            sem("rt_exp"), sem("rt_in"), sem("wslot_done"), sem("wslot_stored"), sem("comb_loaded"))
        ident_ready, marks_ready, rank_mm, groups_ready, nat_mm, nat_rounded, nat_ready = (
            sem("ident_ready"), sem("marks_ready"), sem("rank_mm"), sem("groups_ready"), sem("nat_mm"),
            sem("nat_rounded"), sem("nat_ready"))
        sel_ready, sel_t_ready, wide_ready, side_mm, side_free, x_rounded, xy_rounded, xy_ready, h_added = (
            sem("sel_ready"), sem("sel_t_ready"), sem("wide_ready"), sem("side_mm"), sem("side_free"),
            sem("x_rounded"), sem("xy_rounded"), sem("xy_ready"), sem("h_added"))
        p_rounded, p_ready, pg_done, out_done, stored = (
            sem("p_rounded"), sem("p_ready"), sem("pg_done"), sem("out_done"), sem("stored"))

        EARLY = [mg_sum, o_ready, r_g,
                 tr_ready, ctr_ready, mg_ready, pm_ready, r_o, r_rounded, w_tr, cpt_ready,
                 exp_done, o_split, pt_ready, r_dec, r_y, w_exp, w_os, w_pt, q_free, q_free]
        GATHER, SCATTER, side = {}, {}, 0
        for it in range(-1, XITEMS + 1):
            if it >= 1:
                SCATTER[it - 1] = side
                side += KT
            if it + 1 < XITEMS:
                GATHER[it + 1] = side
                side += KT // 2 + 1
        block = ctx.enter_context(nc.Block())
        ds = bass.ds

        @block.sync
        def _(sp):
            for x in EARLY:
                sp.sem_inc(x, 1)

            def load_a(s, i=0, panel=None):
                n = s + 2 * i
                panel = n if panel is None else panel
                if s >= 2:
                    sp.wait_ge(a_ready, n - 1)
                sp.dma_start(a_raw[s % 2][:, :], w_a[ds(panel, 1)].rearrange("a p n -> p (a n)")) \
                  .then_inc(a_loaded[s % 2], 16)

            def load_b(s, i=0, panel=None):
                n = s + 2 * i
                panel = n if panel is None else panel
                if s >= 2:
                    sp.wait_ge(b_ready, n - 1)
                sp.dma_start(b_raw[s % 2][:, :], w_b[ds(panel, 1)].rearrange("a p n -> p (a n)")) \
                  .then_inc(b_loaded[s % 2], 16)

            def stream(a, b, trips):
                with sp.Fori(0, trips) as i:
                    for u in range(2):
                        if a is not None:
                            load_a(a + u, i)
                        if b is not None:
                            load_b(b + u, i)

            for u in range(2):
                load_a(u)
                load_b(u)
            stream(A_RNN + 2, B_RNN + 2, RNN_BLOCKS // 2 - 1)
            stream(A_FF0, B_FF0, FF_TILES // 2)
            stream(A_KCMP, None, (A_FF1 - A_KCMP) // 2)
            stream(A_FF1, B_FF1, FF_TILES // 2)
            load_a(A_SKV)
            stream(A_SQ, None, (A_MRG - A_SQ) // 2)
            stream(A_MRG, B_MRG, KT // 2)
            stream(A_OUT, None, 2)
            load_a(A_ROUTE)
            sp.wait_ge(groups_ready, 1)
            for it in range(XITEMS):
                g = sp.value_load(item_group[0:1, it:it + 1], min_val=0, max_val=EGROUPS - 1)
                with sp.Fori(0, EPG) as i:
                    for u in range(2):
                        pa = sp.snap(g * (2 * EPG) + i * 2 + (A_MOE + u))
                        load_a(A_MOE + 2 * EPG * it + u, i, pa)
                        pb = sp.snap(g * (2 * EPG) + i * 2 + (B_MOE + u))
                        load_b(B_MOE + 2 * EPG * it + u, i, pb)
            load_a(A_PLE, 0, A_PLE - REPEATED)
            with sp.Fori(0, 2) as i:
                for u in range(2):
                    load_a(A_PG + u, i, A_PG - REPEATED + u + 2 * i)

        @block.tensor
        def _(pe):
            def three(out, w_hi, w_lo, x_hi, x_lo, first, last):
                pe.matmul(out, w_hi, x_hi, start=first, stop=False)
                pe.matmul(out, w_hi, x_lo, start=False, stop=False)
                return pe.matmul(out, w_lo, x_hi, start=False, stop=last)

            def product(out, s, col, pitch, width, x_hi, x_lo, kt=KT, k0=0, rows=P, first=True, last=True):
                for k in range(kt):
                    c = col + k * pitch
                    m = three(out, a_hi[s % 2][0:rows, c:c + width], a_lo[s % 2][0:rows, c:c + width],
                              x_hi(k), x_lo(k), first and k == 0, last and k == kt - 1)
                return m

            def hh(k):
                return hn_hi[:, k, :]

            def hl(k):
                return hn_lo[:, k, :]

            def tile_bank(s, j, n):
                if s >= 2 or s + j >= 2:
                    pe.wait_ge(tile_free, 2 * n - 3 + j)
                return bank[2 * (s % 2) + j]

            def linear(s, i=0, width=P):
                n = s + 2 * i
                pe.wait_ge(a_ready, n + 1)
                for j in range(2):
                    b = tile_bank(s, j, n)
                    product(b[0:width, :], s, j * width, 2 * width, width, hh, hl).then_inc(tile_ready, 1)

            def natural(s, j, col, pitch, width, i=0, inc=1):
                n = s + 2 * i
                b = tile_bank(s, j, n)
                for t in range(NT):
                    c = slice(t * P, (t + 1) * P)
                    for k in range(KT):
                        w = slice(col + k * pitch, col + k * pitch + width)
                        m = three(b[:, t * width:(t + 1) * width], hn_hi[:, k, c], hn_lo[:, k, c],
                                  a_hi[s % 2][:, w], a_lo[s % 2][:, w], k == 0, k == KT - 1)
                m.then_inc(tile_ready, inc)

            def norm_stats(q, ready, width=KT):
                ready(pe)
                for m in range(width):
                    pe.wait_ge(sq_ready, KT * q + m + 1)
                    pe.matmul(bank[4][:, :], ones, sq[:, m % 2, :], start=m == 0, stop=m == width - 1) \
                      .then_inc(stat_mm, 1)

            def down(sb_, e, i, x_hi, x_lo, rows):
                for hb in range(2):
                    s = sb_ + hb
                    n = s + 2 * i
                    pe.wait_ge(b_ready, n + 1)
                    for f in range(2):
                        if hb == 0:
                            pe.wait_ge(hid_ready, 2 * (e + i) + f + 1)
                        for m in range(4):
                            if f == 0:
                                pe.wait_ge(y_free, 4 * n + m - 3)
                            c = slice(f * 512 + m * P, f * 512 + (m + 1) * P)
                            mm = three(bank[4 + m][:, :], b_hi[s % 2][0:rows, c], b_lo[s % 2][0:rows, c],
                                       x_hi[0:rows, f, :], x_lo[0:rows, f, :], f == 0, f == 1)
                            if f == 1:
                                mm.then_inc(y_ready, 1)

            def rnn_pair(i, peeled):
                for u in range(2):
                    n = 2 * i + u
                    pe.wait_ge(a_ready, n + 1)
                    for j, done in ((0, xb_ready), (1, yb_ready)):
                        if not peeled:
                            pe.wait_ge(tile_free, 2 * n - 3 + j)
                        product(bank[2 * u + j][0:RNN_W, :], u, j * RNN_W, 2 * RNN_W, RNN_W, hh, hl) \
                            .then_inc(done, 1)
                    for j in range(2):
                        pe.wait_ge(xc_ready if j == 0 else yb_copied, n + 1)
                        product(bank[2 * u + j][0:RNN_W, :], u, 8 * 192 + j * RNN_W, 0, RNN_W,
                                lambda k: xc_hi[:, u, :], lambda k: xc_lo[:, u, :], kt=1, rows=RNN_W) \
                            .then_inc(tile_ready, 1)
                    if u == 0 and not peeled:
                        rnn_down(i)

            def rnn_down(i):
                for hb in range(2):
                    n = 2 * i - 2 + hb
                    pe.wait_ge(b_ready, n + 1)
                    for f in range(2):
                        if hb == 0:
                            pe.wait_ge(hid_ready, 2 * i - 2 + f + 1)
                        for m in range(4):
                            if f == 0 and hb:
                                pe.wait_ge(y_free, 4 * n + m - 3)
                            c = slice(f * 512 + m * P, f * 512 + (m + 1) * P)
                            mm = three(bank[4 + m][:, :], b_hi[hb][0:RNN_W, c], b_lo[hb][0:RNN_W, c],
                                       rhid_hi[0:RNN_W, f, :], rhid_lo[0:RNN_W, f, :], f == 0, f == 1)
                            if f == 1:
                                mm.then_inc(y_ready, 1)

            pe.wait_ge(consts, 16)
            norm_stats(N_MIX0, lambda e: None)
            pe.wait_ge(hn_ready, KT * (N_MIX0 + 1))
            rnn_pair(0, True)
            with pe.Fori(1, RNN_BLOCKS // 2) as i:
                rnn_pair(i, False)
            rnn_down(RNN_BLOCKS // 2)

            def ffn(sa, sb_, e, trips):
                with pe.Fori(0, trips) as i:
                    for f in range(2):
                        linear(sa + f, i)
                    down(sb_, e, i, hid_hi, hid_lo, P)

            def y_all(n_b):
                return lambda e: e.wait_ge(y_free, 4 * n_b)

            norm_stats(N_FFN0, y_all(B_FF0))
            pe.wait_ge(hn_ready, KT * (N_FFN0 + 1))
            ffn(A_FF0, B_FF0, E_FF0, FF_TILES // 2)

            norm_stats(N_KV, y_all(B_FF1))
            pe.wait_ge(hn_ready, KT * (N_KV + 1))
            linear(A_KCMP, width=DQK)
            linear(A_KCMP + 1, width=DQK)
            linear(A_VCMP)

            def rope_mm_(r, src):
                if r >= 2:
                    pe.wait_ge(rope_done, r - 1)
                pe.matmul(bank[4 + r % 2][0:DQK, :], rot, src, start=True, stop=True).then_inc(rope_mm, 1)

            for b in range(2):
                for p in range(2):
                    s = A_KSEL + 2 * b + p
                    linear(s, width=DQK)
                    for j in range(2):
                        pe.wait_ge(tile_free, 2 * s + j + 1)
                        rope_mm_(4 * b + 2 * p + j, kx[:, b, 2 * p + j, :])
            for b in range(2):
                s = A_VNAT + b
                pe.wait_ge(a_ready, s + 1)
                for j in range(2):
                    bk = tile_bank(s, j, s)
                    for t in range(2):
                        c = slice((2 * j + t) * P, (2 * j + t + 1) * P)
                        for k in range(KT):
                            w = slice(k * 256, (k + 1) * 256)
                            m = three(bk[:, t * 256:(t + 1) * 256], hn_hi[:, k, c], hn_lo[:, k, c],
                                      a_hi[s % 2][:, w], a_lo[s % 2][:, w], k == 0, k == KT - 1)
                    m.then_inc(tile_ready, 1)
            for b, (s0, rows) in enumerate(((A_W1K, DQK), (A_W1V, DV))):
                for p in range(4):
                    s = s0 + p
                    pe.wait_ge(a_ready, s + 1)
                    pe.wait_ge(xl_ready, 4 * b + p + 1)
                    if b == 1 and p == 0:
                        pe.wait_ge(chid_done, 1)
                    for m in range(2):
                        for l in range(8):
                            c = slice(l * 256 + m * P, l * 256 + (m + 1) * P)
                            mm = three(bank[6 + m][:, 0:124], a_hi[s % 2][0:rows, c], a_lo[s % 2][0:rows, c],
                                       xl_hi[0:rows, l, :], xl_lo[0:rows, l, :],
                                       p == 0 and l == 0, p == 3 and l == 7)
                    mm.then_inc(tile_ready, 2)
                pe.wait_ge(chid_done, b + 1)
                if b == 0:
                    for m in range(2):
                        mm = pe.matmul(bank[5][0:DQK, 0:124], smc("w2k", m * DQK, DQK), chid[:, m, :],
                                       start=m == 0, stop=m == 1)
                else:
                    pe.wait_ge(cmp_done, 1)
                    for g in range(GROUPS):
                        for m in range(2):
                            mm = pe.matmul(bank[5][0:NCMP, g * DV:(g + 1) * DV],
                                           chid[:, m, g * NCMP:(g + 1) * NCMP], smc("w2v", m * DV, DV),
                                           start=m == 0, stop=m == 1)
                mm.then_inc(cmp_w2, 1)

            norm_stats(N_MIX1, lambda e: e.wait_ge(cmp_done, 2))
            pe.wait_ge(hn_ready, KT * (N_MIX1 + 1))
            pe.wait_ge(a_ready, A_GATE + 1)
            natural(A_GATE, 0, 0, NGATE, NGATE, inc=2)
            with pe.Fori(0, HEADS // 4) as i:
                for u in range(2):
                    s = A_Q + u
                    linear(s, i, width=DQK)
                    for j in range(2):
                        v = 2 * u + j
                        pe.wait_ge(tile_free, 2 * (s + 2 * i) + j + 1)
                        pe.wait_ge(rope_done, 8 + 4 * i + v - 1)
                        pe.matmul(bank[4 + v % 2][0:DQK, :], rot, qb[:, v, 0, :], start=True, stop=True) \
                          .then_inc(rope_mm, 1)

            pe.wait_ge(rope_done, 8 + HEADS)
            pe.wait_ge(tile_free, 2 * A_WO)
            with pe.Fori(0, GROUPS) as g:
                def scores_c(u):
                    hd = HPG * g + u
                    pe.wait_ge(q_staged[u % 2], 32 * g + 16 * (u // 2) + 16)
                    pe.wait_ge(cpt_ready, 1 + hd)
                    for t in range(NT):
                        mm = pe.matmul(bank[6][:, t * NCMP:(t + 1) * NCMP], qs[:, u % 2, 0, t * P:(t + 1) * P],
                                       kct[:, ds(g * NCMP, NCMP)], start=True, stop=True)
                    mm.then_inc(csc_ready, 1)

                def scores(u, t):
                    hd = HPG * g + u
                    n = (t + 1) * P
                    pe.wait_ge(exp_done, 1 + 4 * hd + t - 1 if t >= 2 else 1 + 4 * hd)
                    for b in range(2):
                        bk = bank[2 * (t % 2) + b]
                        pe.matmul(bk[:, 0:n], qs[:, u % 2, 1, t * P:(t + 1) * P],
                                  kx[:, b, ds(g, 1), 0:n].rearrange("p a s -> p (a s)"), start=True, stop=False)
                        mm = pe.matmul(bk[:, t * P:n], masks[:, 0, :], masks[:, 1, :], start=False, stop=True)
                    mm.then_inc(sc_ready, 1)

                def turn(u, t):
                    x = 8 * (HPG * g + u) + 2 * t
                    pe.wait_ge(pm_ready, 1 + 4 * (HPG * g + u) + t + 1)
                    for b in range(2):
                        pe.wait_ge(pt_ready, 1 + x + b - 1 if t or b else 1 + x)
                        for j in range(t + 1):
                            mm = pe.transpose(bank[4 + b][:, j * P:(j + 1) * P],
                                              pm[:, t % 2, b, j * P:(j + 1) * P], ident)
                        mm.then_inc(tr_ready, 1)

                scores_c(0)
                scores(0, 0)
                scores(0, 1)
                for u in range(HPG):
                    hd = HPG * g + u
                    pe.wait_ge(cpm_ready, hd + 1)
                    for t in range(NT):
                        mm = pe.transpose(bank[6][0:NCMP, t * P:(t + 1) * P], pc[:, t, :], ident)
                    mm.then_inc(ctr_ready, 1)
                    for t in range(NT):
                        if t + 2 < NT:
                            scores(u, t + 2)
                        turn(u, t)
                    if u + 1 < HPG:
                        scores_c(u + 1)
                        scores(u + 1, 0)
                        scores(u + 1, 1)
                    r0 = DV * (u % 2)
                    if u == 0:
                        pe.wait_ge(v_staged, 3 * g + 3)
                    if u % 2 == 0:
                        pe.wait_ge(o_split, 1 + 2 * g + u // 2)
                    pe.wait_ge(pt_ready, 1 + 8 * hd + 8)
                    for b in range(2):
                        for j in range(NT):
                            pe.matmul(bank[7][r0:r0 + DV, j * P:S], vs[:, b, j, :], pt[:, b, j, j * P:S],
                                      start=b == 0 and j == 0, stop=False)
                    pe.matmul(bank[7][r0:r0 + DV, :], vcs[:, :], ptc[:, :], start=False, stop=True) \
                      .then_inc(o_ready, 1)

            pe.wait_ge(o_split, 1 + HEADS // 2)
            with pe.Fori(0, 2) as i:
                linear(A_WO, i)
                linear(A_WO + 1, i)

            norm_stats(N_FFN1, lambda e: None)
            pe.wait_ge(hn_ready, KT * (N_FFN1 + 1))
            ffn(A_FF1, B_FF1, E_FF1, FF_TILES // 2)
            norm_stats(N_FINAL, y_all(B_MRG))
            norm_stats(N_MIX2, lambda e: None)
            pe.wait_ge(hn_ready, KT * (N_MIX2 + 1))

            s = A_SKV
            pe.wait_ge(a_ready, s + 1)
            b = tile_bank(s, 0, s)
            product(b[:, :], s, 0, 2 * P, P, hh, hl).then_inc(tile_ready, 1)
            natural(s, 1, P, 2 * P, P)
            pe.wait_ge(qk_sq, 1)
            pe.matmul(bank[4][:, :], halves, sq[:, 0, :], start=True, stop=True).then_inc(qk_mm, 1)

            def query_w(m):
                s = A_SQ + m
                pe.wait_ge(a_ready, s + 1)
                b = tile_bank(s, 0, s)
                product(b[:, :], s, 0, 2 * P, P, hh, hl).then_inc(tile_ready, 2)
                pe.wait_ge(qk_sq, m + 2)
                pe.matmul(bank[1][:, :], halves, sq[:, m % 2, :], start=True, stop=True).then_inc(qk_mm, 1)

            def scores_w(m, half):
                r = slice(64 * half, 64 * half + 64)
                if m or half:
                    pe.wait_ge(w_mx, 2 * m + half)
                for (t, k0, w, c) in WIN:
                    mm = pe.matmul(bank[4 + c // S][:, c % S:c % S + w], qn[r, t * P:(t + 1) * P],
                                   sk[r, k0:k0 + w], start=True, stop=True)
                mm.then_inc(w_sc, 1)

            def out_w(m, half):
                r = slice(64 * half, 64 * half + 64)
                it = 2 * m + half
                pe.wait_ge(w_pm, it + 1)
                pe.wait_ge(w_pt, 1 + it)
                for j in range(7):
                    mm = pe.transpose(bank[6 + j // 4][:, j % 4 * P:(j % 4 + 1) * P],
                                      wp[:, half, j * P:(j + 1) * P], ident)
                mm.then_inc(w_tr, 1)
                pe.wait_ge(w_pt, 1 + it + 1)
                if half == 0:
                    pe.wait_ge(w_os, 1 + m)
                for (t, k0, w, c) in WIN:
                    for j in range(w // P):
                        mm = pe.matmul(bank[3][r, t * P:(t + 1) * P], sv[:, k0 // P + j, r],
                                       wpt[:, half, c + j * P:c + (j + 1) * P], start=j == 0, stop=j == w // P - 1)
                if half:
                    mm.then_inc(w_o, 1)

            query_w(0)
            for m in range(SWA_TILES):
                if m + 1 < SWA_TILES:
                    query_w(m + 1)
                pe.wait_ge(qk_norm, m + 2)
                scores_w(m, 0)
                scores_w(m, 1)
                out_w(m, 0)
                out_w(m, 1)

            pe.wait_ge(w_os, 1 + SWA_TILES)
            with pe.Fori(0, RET_H) as i:
                pe.wait_ge(a_ready, A_RET + 2 * i + 1)
                for j in range(2):
                    b = tile_bank(A_RET, j, A_RET + 2 * i)
                    product(b[:, :], A_RET, j * P, 2 * P, P, hh, hl).then_inc(tile_ready, 1)
                pe.wait_ge(a_ready, A_RET + 2 * i + 2)
                b = tile_bank(A_RET + 1, 0, A_RET + 1 + 2 * i)
                product(b[:, :], A_RET + 1, 0, 2 * P, P, hh, hl).then_inc(tile_ready, 1)
                natural(A_RET + 1, 1, P, 2 * P, P, i=i)
                pe.wait_ge(tile_free, 2 * (A_RET + 2 + 2 * i))

                def scores_r(j):
                    pe.wait_ge(r_dec, 1 + 4 * i + j - 1 if j >= 2 else 4 * i)
                    pe.matmul(bank[4 + j % 2][:, 0:S - j * P], rk[:, j * P:(j + 1) * P], rq[:, j * P:S],
                              start=True, stop=True).then_inc(r_sc, 1)

                def out_r(j):
                    pe.wait_ge(r_dec, 1 + 4 * i + j + 1)
                    if j == 0:
                        pe.wait_ge(r_y, 1 + i)
                    mm = pe.matmul(bank[6][:, j * P:S], rv[:, j * P:(j + 1) * P], srt[:, j % 2, 0:S - j * P],
                                   start=j == 0, stop=j == 3)
                    mm.then_inc(r_o, 1)

                scores_r(0)
                scores_r(1)
                out_r(0)
                scores_r(2)
                out_r(1)
                scores_r(3)
                out_r(2)
                out_r(3)
                pe.wait_ge(r_y, 1 + i + 1)
                pe.matmul(bank[7][:, :], ones, ry[:, :], start=True, stop=True).then_inc(r_mean, 1)
                pe.wait_ge(r_sq, i + 1)
                pe.matmul(bank[7][:, :], ones, sq[:, 0, :], start=True, stop=True).then_inc(r_var, 1)

            pe.wait_ge(r_split, RET_H)
            with pe.Fori(0, KT // 2) as i:
                for u in range(2):
                    linear(A_MRG + u, i)
                    s = B_MRG + u
                    n = s + 2 * i
                    pe.wait_ge(b_ready, n + 1)
                    pe.wait_ge(y_free, 4 * n - 4)
                    for j, (yh, yl) in enumerate(((yr_hi, yr_lo), (ys_hi, ys_lo))):
                        for k in range(4):
                            c = slice(j * 512 + k * P, j * 512 + (k + 1) * P)
                            mm = three(bank[4 + 2 * u + j][:, :], b_hi[s % 2][:, c], b_lo[s % 2][:, c],
                                       yh[:, k, :], yl[:, k, :], k == 0, k == 3)
                        mm.then_inc(y_ready, 2)

            pe.wait_ge(mg_ready, 1 + KT)
            with pe.Fori(0, 2) as i:
                for u in range(2):
                    s = A_OUT + u
                    n = s + 2 * i
                    pe.wait_ge(a_ready, n + 1)
                    for j in range(2):
                        b = tile_bank(s, j, n)
                        product(b[:, :], s, j * P, 2 * P, P, lambda k: mg_hi[:, k, :], lambda k: mg_lo[:, k, :]) \
                            .then_inc(tile_ready, 1)

            norm_stats(N_MOE, y_all(B_MOE))
            pe.wait_ge(hn_ready, KT * (N_MOE + 1))
            pe.wait_ge(a_ready, A_ROUTE + 1)
            natural(A_ROUTE, 0, 0, NROUTE, NROUTE, inc=2)

            def turn_tokens(c):
                t, f = c // 2, c % 2
                if c >= 4:
                    pe.wait_ge(nat_ready, c - 3)
                for k in range(4):
                    o = bank[4 + c % 4][:, k * P:(k + 1) * P]
                    pe.matmul(o, hn_hi[:, 4 * f + k, t * P:(t + 1) * P], ident_r[:, :], start=True, stop=False)
                    mm = pe.matmul(o, hn_lo[:, 4 * f + k, t * P:(t + 1) * P], ident_r[:, :],
                                   start=False, stop=True)
                mm.then_inc(nat_mm, 1)

            pe.wait_ge(ident_ready, 1)
            for c in range(4):
                turn_tokens(c)
            pe.wait_ge(marks_ready, 1)
            for t in range(NT + 1):
                for u in range(min(t + 1, NT)):
                    mm = pe.matmul(bank[3][:, t * EGROUPS:(t + 1) * EGROUPS], cnc("upto", P) if u == t else ones,
                                   rtg[:, 2, u, :], start=u == 0, stop=u == min(t, NT - 1))
            mm.then_inc(rank_mm, 1)
            for c in range(4, 8):
                turn_tokens(c)

            def side_bank(k):
                if k >= 2:
                    pe.wait_ge(side_free, k - 1)
                return bank[2 + k % 2]

            def gather(it):
                pe.wait_ge(sel_ready, it + 1)
                for c in range(KT // 2):
                    b = side_bank(GATHER[it] + c)
                    for f in range(2):
                        cols = slice((2 * c + f) * P, (2 * c + f + 1) * P)
                        for t in range(NT):
                            for part in (nat_hi, nat_lo):
                                mm = pe.matmul(b[:, f * XB:(f + 1) * XB], part[:, t, cols], sel[:, t, :],
                                               start=t == 0 and part is nat_hi, stop=t == NT - 1 and part is nat_lo)
                    mm.then_inc(side_mm, 1)
                b = side_bank(GATHER[it] + KT // 2)
                for t in range(NT):
                    for part in (w_hi, w_lo):
                        mm = pe.matmul(b[0:EPG, 0:XB], part[:, t, :], sel[:, t, :],
                                       start=t == 0 and part is w_hi, stop=t == NT - 1 and part is w_lo)
                mm.then_inc(side_mm, 1)

            def scatter(it):
                pe.wait_ge(sel_t_ready, it + 1)
                pe.wait_ge(xy_ready, 4 * it + 4)
                for m in range(KT):
                    b = side_bank(SCATTER[it] + m)
                    for u in range(XSUB):
                        for part in (xy_hi, xy_lo):
                            mm = pe.matmul(b[:, :], part[:, u, m * P:(m + 1) * P], sel_t[:, u, :],
                                           start=u == 0 and part is xy_hi, stop=u == XSUB - 1 and part is xy_lo)
                    mm.then_inc(side_mm, 1)

            def expert(it, i, first=False, last=False):
                x = slice((it % 2) * XB, (it % 2 + 1) * XB)
                for f in range(2):
                    s = A_MOE + 2 * EPG * it + f
                    n = s + 2 * i
                    pe.wait_ge(a_ready, n + 1)
                    for j in range(2):
                        pe.wait_ge(tile_free, 2 * n - 3 + j)
                        product(bank[s % 2][:, j * XB:(j + 1) * XB], s, j * P, 2 * P, P,
                                lambda k: hn_hi[:, k, x], lambda k: hn_lo[:, k, x]).then_inc(tile_ready, 1)
                for f in range(2):
                    pe.wait_ge(hid_ready, 2 * (E_MOE + EPG * it + i) + f + 1)
                    for hb in range(2):
                        s = B_MOE + 2 * EPG * it + hb
                        n = s + 2 * i
                        if f == 0:
                            pe.wait_ge(b_ready, n + 1)
                        for u in range(XSUB):
                            if first and f == 0 and it:
                                pe.wait_ge(xy_ready, 4 * it)
                            c = slice(u * P, (u + 1) * P)
                            mm = three(bank[4 + 2 * u + hb][:, :], xhid_hi[:, f, c], xhid_lo[:, f, c],
                                       b_hi[s % 2][:, f * 512:(f + 1) * 512], b_lo[s % 2][:, f * 512:(f + 1) * 512],
                                       first and f == 0, last and f == 1)
                            if f == 1:
                                mm.then_inc(y_ready, 2)

            pe.wait_ge(nat_ready, 2 * NT)
            gather(0)
            pe.wait_ge(wide_ready, 1)
            pe.wait_ge(side_free, GATHER[0] + KT // 2 + 1)
            for t in range(NT):
                mm = pe.matmul(bank[2][:, t * P:(t + 1) * P], slot_wide[:, t * P:(t + 1) * P], ident,
                               start=True, stop=True)
            mm.then_inc(rank_mm, 1)
            for it in range(XITEMS):
                pe.wait_ge(side_free, GATHER[it] + KT // 2)
                expert(it, 0, first=True)
                if it == 0:
                    pe.wait_ge(wide_ready, 2)
                else:
                    scatter(it - 1)
                if it + 1 < XITEMS:
                    gather(it + 1)
                with pe.Fori(1, EPG - 1) as i:
                    expert(it, i)
                expert(it, EPG - 1, last=True)
            scatter(XITEMS - 1)

            norm_stats(N_PLEG, lambda e: e.wait_ge(xy_ready, 4 * XITEMS))
            s = A_PLE
            pe.wait_ge(a_ready, s + 1)
            pe.wait_ge(p_ready, 1)
            for m in range(KT):
                b = bank[m % 2 + 2 * (s % 2)]
                if m >= 2:
                    pe.wait_ge(pg_done, m - 1)
                else:
                    tile_bank(s, m, s)
                mm = product(b[:, :], s, m * P, D, P, lambda k: ptr_hi[:, k, :], lambda k: ptr_lo[:, k, :], kt=2)
                mm.then_inc(ple_mm, 1)
            pe.wait_ge(pg_done, KT)
            pe.sem_inc(tile_ready, 2)
            norm_stats(N_PLE, lambda e: e.wait_ge(sd_ready, N_PLEG + 1))
            pe.wait_ge(hn_ready, KT * (N_PLEG + 1))
            for p in range(4):
                linear(A_PG + p)

        @block.scalar
        def _(act):
            step = Steps(act, act_step)

            def high_a(s, i=0):
                n = s + 2 * i
                act.wait_ge(a_loaded[s % 2], 16 * (s // 2 + i) + 16)
                if s >= 2 or not isinstance(i, int):
                    act.wait_ge(tile_ready, 2 * n - 2)
                act.activation(a_hi[s % 2][:, :], a_raw[s % 2][:, :], ACT.Copy).then_inc(a_rounded, 1)

            def high_b(s, i=0):
                n = s + 2 * i
                act.wait_ge(b_loaded[s % 2], 16 * (s // 2 + i) + 16)
                if s >= 1:
                    act.wait_ge(y_ready, 4 * n - 4)
                act.activation(b_hi[s % 2][:, :], b_raw[s % 2][:, :], ACT.Copy).then_inc(b_rounded, 1)

            def squares(q, ready):
                for m in range(KT):
                    ready(act, m)
                    if m >= 2:
                        act.wait_ge(stat_mm, KT * q + m - 1)
                    act.activation(sq[:, m % 2, :], h[:, m, :], ACT.Square).then_inc(sq_ready, 1)

            def root(q, n=KT):
                act.wait_ge(stat_mm, KT * (q + 1))
                if q:
                    act.wait_ge(dve_rstd, q)
                act.activation(sd[:, :], bank[4][:, :], ACT.Sqrt, bias=eps, scale=1.0 / D).then_inc(sd_ready, 1)

            def high_hn(q):
                for m in range(KT):
                    act.wait_ge(hn_scaled, KT * q + m + 1)
                    act.activation(hn_hi[:, m, :], tmp[:, m % 2, :], ACT.Copy).then_inc(hn_rounded, 1)

            act.dma_start(cn[:, :], const).then_inc(consts, 16)
            act.dma_start(h[:, :, :], x_t.rearrange("(k p) s -> p k s", p=P)).then_inc(x_loaded, 16)
            act.dma_start(sm[:, :], small).then_inc(params, 16)
            act.wait_ge(consts, 16)
            squares(N_MIX0, lambda e, m: e.wait_ge(x_loaded, 16))
            root(N_MIX0)
            high_a(A_RNN)
            high_hn(N_MIX0)

            act.wait_ge(params, 16)
            lam = smc("lam", 0, RNN_BLOCKS, RNN_W)
            step(act.activation(spt[:, 0, :], lam, ACT.Abs))
            act.activation(spt[:, 1, :], spt[:, 0, :], ACT.Exp, scale=-1.0).then_inc(sp_exp, 1)
            act.wait_ge(sp_one, 1)
            act.activation(spt[:, 3, :], spt[:, 2, :], ACT.Ln).then_inc(sp_ln, 1)
            act.wait_ge(sp_done, 1)

            def rnn_pair(i, peeled):
                for u in range(2):
                    n = 2 * i + u
                    high_a(A_RNN + 1 + u, i)
                    act.wait_ge(xc_done, n + 1)
                    act.activation(xc_hi[:, u, :], xc[:, u, :], ACT.Copy).then_inc(xc_rounded, 1)
                    for j, (dst, bias) in enumerate(((rg, "b_ra"), (ig, "b_ix"))):
                        act.wait_ge(tile_ready, 2 * n + j + 1)
                        act.activation(dst[:, u, :], bank[2 * u + j][0:RNN_W, :], ACT.Sigmoid,
                                       bias=sm[0:RNN_W, ds(SM[bias] + n, 1)]).then_inc(tile_free, 1)
                for u in range(2):
                    act.wait_ge(b_loaded[u], 16 * i + 16)
                    if not peeled:
                        act.wait_ge(y_ready, 8 * i - 4 + 4 * u)
                    act.activation(b_hi[u][:, :], b_raw[u][:, :], ACT.Copy).then_inc(b_rounded, 1)
                for u in range(2):
                    n = 2 * i + u
                    act.wait_ge(yb_copied, n + 1)
                    act.activation(gel[:, u, :], ybr[:, u, :], ACT.Gelu_apprx_tanh).then_inc(gelu_done, 1)
                act.wait_ge(tile_free, 4 * i + 4)
                for u in range(2):
                    n = 2 * i + u
                    act.activation(aa[:, u, :], rg[:, u, :], ACT.Exp, scale=spt[:, 7, ds(n, 1)]) \
                       .then_inc(decay_done, 1)
                    act.activation(pp[:, u, :], rg[:, u, :], ACT.Tanh, scale=spt[:, 6, ds(n, 1)]) \
                       .then_inc(decay_done, 1)
                for u in range(2):
                    n = 2 * i + u
                    act.wait_ge(m2_done, n + 1)
                    act.activation(mu[:, u, :], pp[:, u, :], ACT.Sqrt).then_inc(mult_done, 1)
                for u in range(2):
                    n = 2 * i + u
                    act.wait_ge(rec_done, n + 1)
                    if not peeled:
                        act.wait_ge(y_ready, 8 * i)
                    act.activation(rhid_hi[0:RNN_W, u, :], hs[:, u, :], ACT.Copy).then_inc(hid_rounded, 1)

            rnn_pair(0, True)
            with act.Fori(1, RNN_BLOCKS // 2) as i:
                rnn_pair(i, False)

            def ffn_pair(sa, sb_, e, i):
                for f in range(2):
                    n = sa + f + 2 * i
                    high_a(sa + f + 1, i)
                    high_b(sb_ + f, i)
                    act.wait_ge(tile_ready, 2 * n + 1)
                    act.activation(sg[:, f, :], bank[2 * ((sa + f) % 2)][:, :], ACT.Silu).then_inc(gate_done, 1)
                    act.wait_ge(tile_free, 2 * n + 2)
                    act.activation(hid_hi[:, f, :], hid[:, f, :], ACT.Copy).then_inc(hid_rounded, 1)

            def ffn(sa, sb_, e, trips):
                with act.Fori(0, trips) as i:
                    ffn_pair(sa, sb_, e, i)

            def y_is(nb):
                return lambda e, m: e.wait_ge(y_free, 4 * nb - KT + m + 1)

            squares(N_FFN0, y_is(B_FF0))
            root(N_FFN0)
            high_hn(N_FFN0)
            ffn(A_FF0, B_FF0, E_FF0, FF_TILES // 2)

            squares(N_KV, y_is(B_FF1))
            root(N_KV)
            high_hn(N_KV)
            for s in range(A_KCMP, A_W1K):
                high_a(s + 1)
            for b, rows in enumerate((DQK, DV)):
                for p in range(4):
                    act.wait_ge(xl_done, 4 * b + p + 1)
                    act.wait_ge(tile_ready, 2 * (A_W1K + 4 * b + p))
                    act.activation(xl_hi[0:rows, :, :], xl[0:rows, :, :], ACT.Copy).then_inc(xl_rounded, 1)
                    high_a(A_W1K + 4 * b + p + 1)
                act.wait_ge(tile_ready, 2 * (A_W1K + 4 * b + 4))
                if b == 1:
                    act.wait_ge(cmp_w2, 1)
                for m in range(2):
                    mm = act.activation(chid[:, m, :], bank[6 + m][:, 0:124], ACT.Gelu_apprx_tanh)
                mm.then_inc(chid_done, 1)

            squares(N_MIX1, lambda e, m: None)
            root(N_MIX1)
            high_hn(N_MIX1)
            high_a(A_GATE + 1)
            act.wait_ge(gates_in, 1)
            act.activation(gates[:, :, :], gates[:, :, :], ACT.Sigmoid).then_inc(gates_done, 1)
            with act.Fori(0, HEADS // 4) as i:
                for u in range(2):
                    high_a(A_Q + u + 1, i)

            with act.Fori(0, GROUPS) as g:
                for u in range(HPG):
                    hd = HPG * g + u

                    def expo(t):
                        n = (t + 1) * P
                        act.wait_ge(mx_done, 4 * hd + t + 1)
                        act.wait_ge(tr_ready, 1 + 8 * hd + 2 * t - 2 if t >= 2 else 1 + 8 * hd)
                        for b in range(2):
                            e = act.activation(pm[:, t % 2, b, 0:n], bank[2 * (t % 2) + b][:, 0:n], ACT.Exp,
                                               bias=ast[:, t % 2, b:b + 1], accum_out=ast[:, t % 2, 2 + b:3 + b])
                        e.then_inc(exp_done, 1)

                    act.wait_ge(csub_done, hd + 1)
                    act.activation(pc[:, :, :], pc[:, :, :], ACT.Exp).then_inc(cexp_done, 1)
                    expo(0)
                    expo(1)
                    act.wait_ge(ctr_ready, 1 + hd + 1)
                    act.wait_ge(o_ready, 1 + hd)
                    act.activation(ptc[:, :], bank[6][0:NCMP, :], ACT.Copy).then_inc(cpt_ready, 1)
                    for t in range(NT):
                        if t + 2 < NT:
                            expo(t + 2)
                        for b in range(2):
                            act.wait_ge(tr_ready, 1 + 8 * hd + 2 * t + b + 1)
                            act.activation(pt[:, b, 0:t + 1, t * P:(t + 1) * P],
                                           bank[4 + b][:, 0:(t + 1) * P].rearrange("p (j c) -> p j c", c=P),
                                           ACT.Copy).then_inc(pt_ready, 1)
                    if u % 2:
                        act.wait_ge(o_ready, 1 + hd + 1)
                        act.activation(hn_hi[:, ds(2 * g + u // 2, 1), :].rearrange("p a s -> p (a s)"),
                                       bank[7][:, :], ACT.Copy).then_inc(o_rounded, 1)

            for p in range(4):
                high_a(A_WO + p + 1)

            def tile_is(s):
                return lambda e, m: e.wait_ge(tile_free, 2 * s + m + 1)

            squares(N_FFN1, tile_is(A_WO))
            root(N_FFN1)
            high_hn(N_FFN1)
            ffn(A_FF1, B_FF1, E_FF1, FF_TILES // 2)
            squares(N_FINAL, y_is(B_MRG))
            root(N_FINAL)
            squares(N_MIX2, lambda e, m: e.wait_ge(hn_scaled, KT * N_FINAL + m + 1))
            root(N_MIX2)
            act.wait_ge(hn_rounded, KT * N_FINAL)
            act.sem_inc(hn_rounded, KT)
            high_hn(N_MIX2)

            high_a(A_SKV + 1)
            act.wait_ge(qk_raw, 1)
            act.activation(sq[:, 0, :], sk[:, :], ACT.Square).then_inc(qk_sq, 1)
            act.wait_ge(qk_mm, 1)
            act.activation(sd[:, :], bank[4][:, :], ACT.Sqrt, bias=eps, scale=1.0 / SWA_HD).then_inc(qk_sd, 1)

            def root_w(m):
                act.wait_ge(qk_raw, m + 2)
                act.activation(sq[:, m % 2, :], tmp[:, m % 2, :], ACT.Square).then_inc(qk_sq, 1)
                act.wait_ge(qk_mm, m + 2)
                act.wait_ge(qk_norm, m + 1)
                act.activation(sd[:, :], bank[1][:, :], ACT.Sqrt, bias=eps, scale=1.0 / SWA_HD).then_inc(qk_sd, 1)

            high_a(A_SQ + 1)
            root_w(0)
            for m in range(SWA_TILES):
                if m + 1 < SWA_TILES:
                    high_a(A_SQ + m + 2)
                    root_w(m + 1)
                for half in range(2):
                    act.wait_ge(w_mx, 2 * m + half + 1)
                    for k, (t, k0, w, c) in enumerate(WIN):
                        act.activation(wp[:, half, c:c + w], wp[:, half, c:c + w], ACT.Exp,
                                       bias=wst[:, half, 4 + k:5 + k], accum_out=wst[:, half, 8 + k:9 + k])
                    act.activation(wst[:, half, 12:16], wst[:, half, 4:8], ACT.Exp,
                                   bias=smc("sink", 2 * m + half)).then_inc(w_exp, 1)
                for half in range(2):
                    act.wait_ge(w_tr, 1 + 2 * m + half + 1)
                    act.activation(wpt[:, half, 0:S], bank[6][:, :], ACT.Copy)
                    act.activation(wpt[:, half, S:7 * P], bank[7][:, 0:3 * P], ACT.Copy).then_inc(w_pt, 1)
                act.wait_ge(w_o, m + 1)
                act.activation(ys_hi[:, m, :], bank[3][:, :], ACT.Copy).then_inc(w_or, 1)

            with act.Fori(0, RET_H) as i:
                high_a(A_RET + 1, i)
                act.wait_ge(tile_ready, 2 * (A_RET + 1 + 2 * i) + 1)
                act.wait_ge(r_g, 1 + i)
                act.activation(rgs[:, :], bank[2 * ((A_RET + 1) % 2)][:, :], ACT.Silu).then_inc(r_gate, 1)
                high_a(A_RET + 2, i)
                act.wait_ge(r_c, i + 1)
                act.activation(sq[:, 0, :], ryc[:, :], ACT.Square).then_inc(r_sq, 1)
                act.wait_ge(r_var, i + 1)
                act.activation(sd[:, :], bank[7][:, :], ACT.Sqrt, bias=eps, scale=1.0 / P).then_inc(r_sd, 1)
                act.wait_ge(r_g, 1 + i + 1)
                act.activation(yr_hi[:, ds(i, 1), :].rearrange("p a s -> p (a s)"), ryc[:, :], ACT.Copy) \
                   .then_inc(r_rounded, 1)

            act.wait_ge(r_split, RET_H)
            with act.Fori(0, KT // 2) as i:
                for u in range(2):
                    s = A_MRG + u
                    n = s + 2 * i
                    high_a(s + 1, i)
                    high_b(B_MRG + u, i)
                    act.wait_ge(mg_sum, 1 + 2 * i + u)
                    for j in range(2):
                        act.wait_ge(tile_ready, 2 * n + j + 1)
                        act.activation(sq[:, j, :], bank[2 * (s % 2) + j][:, :], ACT.Sigmoid).then_inc(mg_gate, 1)
                    act.wait_ge(mg_sum, 1 + 2 * i + u + 1)
                    act.activation(mg_hi[:, ds(2 * i + u, 1), :].rearrange("p a s -> p (a s)"), tmp[:, 0, :],
                                   ACT.Copy).then_inc(mg_rounded, 1)
            for p in range(4):
                high_a(A_OUT + p + 1)
            squares(N_MOE, tile_is(A_OUT))
            root(N_MOE)
            high_hn(N_MOE)

            def high_token(c):
                act.wait_ge(nat_mm, c + 1)
                act.activation(nat_hi[:, c // 2, (c % 2) * 512:(c % 2 + 1) * 512], bank[4 + c % 4][:, :], ACT.Copy) \
                   .then_inc(nat_rounded, 1)

            for c in range(4):
                high_token(c)
            act.wait_ge(rt_in, 1)
            act.activation(rtg[:, 1, :, :], rtg[:, 0, :, :], ACT.Exp)
            act.activation(rt[:, 5, :], rt[:, 4, :], ACT.Exp).then_inc(rt_exp, 1)
            for c in range(4, 8):
                high_token(c)
            high_a(A_MOE)
            high_a(A_MOE + 1)

            def high_gather(it):
                x = slice((it % 2) * XB, (it % 2 + 1) * XB)
                for c in range(KT // 2):
                    k = GATHER[it] + c
                    act.wait_ge(side_mm, k + 1)
                    act.activation(hn_hi[:, 2 * c:2 * c + 2, x],
                                   bank[2 + k % 2].rearrange("p (f x) -> p f x", f=2), ACT.Copy) \
                       .then_inc(x_rounded, 1)

            def expert(it, i):
                sa, sb_ = A_MOE + 2 * EPG * it, B_MOE + 2 * EPG * it
                for f in range(2):
                    high_b(sb_ + f, i)
                for f in range(2):
                    n = sa + f + 2 * i
                    act.wait_ge(tile_ready, 2 * n + 2)
                    act.activation(xsg[:, f, :], bank[(sa + f) % 2][:, 0:XB], ACT.Silu).then_inc(gate_done, 1)
                    act.wait_ge(tile_free, 2 * n + 2)
                    act.activation(xhid_hi[:, f, :], xhid[:, f, :], ACT.Copy).then_inc(hid_rounded, 1)
                    high_a(sa + f + 2, i)

            high_gather(0)
            for it in range(XITEMS):
                expert(it, 0)
                if it + 1 < XITEMS:
                    high_gather(it + 1)
                with act.Fori(1, EPG) as i:
                    expert(it, i)
                for hb in range(2):
                    act.wait_ge(y_ready, 4 * (B_MOE + 2 * EPG * (it + 1)) - 4 + 4 * hb)
                    for u in range(XSUB):
                        if it:
                            act.wait_ge(side_mm, SCATTER[it - 1] + KT)
                        act.activation(xy_hi[:, u, hb * 512:(hb + 1) * 512], bank[4 + 2 * u + hb][:, :], ACT.Copy) \
                           .then_inc(xy_rounded, 1)

            squares(N_PLEG, lambda e, m: e.wait_ge(h_added, KT * (XITEMS - 1) + m + 1))
            root(N_PLEG)
            act.wait_ge(p_loaded, 16)
            act.activation(ptr_hi[:, :, :], ptr[:, :, :], ACT.Copy).then_inc(p_rounded, 1)
            high_hn(N_PLEG)
            for m in range(KT):
                act.wait_ge(pg_done, m + 1)
                if m >= 2:
                    act.wait_ge(stat_mm, KT * N_PLE + m - 1)
                act.activation(sq[:, m % 2, :], ple[:, m, :], ACT.Square).then_inc(sq_ready, 1)
            root(N_PLE)
            for p in range(4):
                s = A_PG + p
                if p < 3:
                    high_a(s + 1)
                for j in range(2):
                    m = 2 * p + j
                    act.wait_ge(tile_ready, 2 * s + j + 1)
                    act.wait_ge(tile_free, 2 * s + j - 1)
                    act.activation(pgs[:, j, :], bank[2 * (s % 2) + j][:, :], ACT.Sigmoid).then_inc(out_done, 1)

        @block.vector
        def _(dve):
            step = Steps(dve, dve_step)
            V = dve

            def low_a(s, i=0):
                n = s + 2 * i
                V.wait_ge(a_rounded, n + 1)
                V.tensor_tensor(a_lo[s % 2][:, :], a_raw[s % 2][:, :], a_hi[s % 2][:, :], ALU.subtract) \
                 .then_inc(a_ready, 1)

            def low_b(s, i=0):
                n = s + 2 * i
                V.wait_ge(b_rounded, n + 1)
                V.tensor_tensor(b_lo[s % 2][:, :], b_raw[s % 2][:, :], b_hi[s % 2][:, :], ALU.subtract) \
                 .then_inc(b_ready, 1)

            def inverse_root(q):
                V.wait_ge(sd_ready, q + 1)
                V.reciprocal(rstd[:, :], sd[:, :]).then_inc(dve_rstd, 1)
                V.wait_ge(dve_rstd, q + 1)

            def normalise(q, gain, ready=None):
                inverse_root(q)
                if ready:
                    ready(V)

                def low(m):
                    V.wait_ge(hn_rounded, KT * q + m + 1)
                    V.tensor_tensor(hn_lo[:, m, :], tmp[:, m % 2, :], hn_hi[:, m, :], ALU.subtract) \
                     .then_inc(hn_ready, 1)

                for m in range(KT):
                    if m >= 2:
                        V.wait_ge(hn_ready, KT * q + m - 1)
                    V.scalar_tensor_tensor(tmp[:, m % 2, :], h[:, m, :], smc("gain", KT * gain + m), rstd[:, :],
                                           ALU.mult, ALU.mult).then_inc(hn_scaled, 1)
                    if m:
                        low(m - 1)
                low(KT - 1)

            low_a(A_RNN)
            V.wait_ge(consts, 16)
            V.tensor_copy(masks[:, 0, :], ident)
            V.tensor_copy(masks[:, 1, :], cnc("causal", P))
            V.wait_ge(params, 16)
            V.wait_ge(x_loaded, 16)
            normalise(N_MIX0, 0)

            V.wait_ge(sp_exp, 1)
            one, dif, zero = spt[:, 2, :], spt[:, 4, :], spt[:, 5, :]
            V.tensor_scalar(one, spt[:, 1, :], 1.0, None, ALU.add).then_inc(sp_one, 1)
            V.wait_ge(sp_one, 1)
            step(V.tensor_scalar(dif, one, -1.0, None, ALU.add))
            step(V.tensor_scalar(zero, dif, 0.0, None, ALU.is_equal))
            step(V.tensor_tensor(dif, dif, zero, ALU.add))
            step(V.reciprocal(dif, dif))
            V.wait_ge(sp_ln, 1)
            step(V.tensor_tensor(zero, zero, spt[:, 3, :], ALU.add))
            step(V.tensor_tensor(zero, zero, dif, ALU.mult))
            step(V.tensor_tensor(zero, zero, spt[:, 1, :], ALU.mult))
            step(V.tensor_scalar(dif, smc("lam", 0, RNN_BLOCKS, RNN_W), -1.0, 0.0, ALU.mult, ALU.max))
            step(V.tensor_tensor(dif, dif, zero, ALU.add))
            V.tensor_scalar(spt[:, 6, :], dif, 8.0, None, ALU.mult)
            V.tensor_scalar(spt[:, 7, :], dif, -8.0, None, ALU.mult).then_inc(sp_done, 1)

            def add_y(nb0):
                for m in range(KT):
                    V.wait_ge(y_ready, 4 * nb0 + m + 1)
                    V.tensor_tensor(h[:, m, :], h[:, m, :], bank[4 + m % 4][:, :], ALU.add).then_inc(y_free, 1)

            def rnn_pair(i, peeled):
                for u in range(2):
                    n = 2 * i + u
                    low_a(A_RNN + 1 + u, i)
                    V.wait_ge(xb_ready, n + 1)
                    if not peeled:
                        V.wait_ge(gx_done, n - 1)
                    ps = bank[2 * u][0:RNN_W, :]

                    def tap(k):
                        return sm[0:RNN_W, ds(SM["conv_w"] + 4 * n + k, 1)]

                    step(V.tensor_scalar(xc[:, u, :], ps, tap(3), sm[0:RNN_W, ds(SM["conv_b"] + n, 1)],
                                         ALU.mult, ALU.add))
                    for k in (2, 1, 0):
                        d = 3 - k
                        ins = V.scalar_tensor_tensor(xc[:, u, d:S], ps[:, 0:S - d], tap(k), xc[:, u, d:S],
                                                     ALU.mult, ALU.add)
                        if k:
                            step(ins)
                    ins.then_inc(xc_done, 1)
                    V.wait_ge(xc_rounded, n + 1)
                    V.tensor_tensor(xc_lo[:, u, :], xc[:, u, :], xc_hi[:, u, :], ALU.subtract).then_inc(xc_ready, 1)
                    V.wait_ge(yb_ready, n + 1)
                    if not peeled:
                        V.wait_ge(gelu_done, n - 1)
                    V.tensor_copy(ybr[:, u, :], bank[2 * u + 1][0:RNN_W, :]).then_inc(yb_copied, 1)
                    if u == 0 and not peeled:
                        add_y(2 * i - 2)
                for u in range(2):
                    V.wait_ge(b_rounded, 2 * i + u + 1)
                    V.tensor_tensor(b_lo[u][:, :], b_raw[u][:, :], b_hi[u][:, :], ALU.subtract).then_inc(b_ready, 1)
                for u in range(2):
                    n = 2 * i + u
                    V.wait_ge(asq_done, n + 1)
                    V.scalar_tensor_tensor(pp[:, u, :], mu[:, u, :], 1.0, pp[:, u, :], ALU.add, ALU.mult) \
                     .then_inc(m2_done, 1)
                for u in range(2):
                    n = 2 * i + u
                    V.wait_ge(bx_done, n + 1)
                    V.tensor_tensor_scan(hs[:, u, :], aa[:, u, :], gx[:, u, :], 0.0, ALU.mult, ALU.add) \
                     .then_inc(scan_done, 1)
                for u in range(2):
                    n = 2 * i + u
                    V.wait_ge(hid_rounded, n + 1)
                    V.tensor_tensor(rhid_lo[0:RNN_W, u, :], hs[:, u, :], rhid_hi[0:RNN_W, u, :], ALU.subtract) \
                     .then_inc(hid_ready, 1)

            rnn_pair(0, True)
            step.enter(0, 6)
            with V.Fori(1, RNN_BLOCKS // 2) as i:
                step.i = i - 1
                rnn_pair(i, False)
            step.leave(RNN_BLOCKS // 2 - 1)
            add_y(RNN_BLOCKS - 2)

            def ffn(sa, sb_, e, trips):
                with V.Fori(0, trips) as i:
                    for f in range(2):
                        n = sa + f + 2 * i
                        low_a(sa + f + 1, i)
                        low_b(sb_ + f, i)
                        V.wait_ge(gate_done, 2 * (e - E_FF0 + i) + f + 1)
                        V.wait_ge(tile_ready, 2 * n + 2)
                        V.tensor_tensor(hid[:, f, :], sg[:, f, :], bank[2 * ((sa + f) % 2) + 1][:, :], ALU.mult) \
                         .then_inc(tile_free, 2)
                        V.wait_ge(hid_rounded, 2 * (e + i) + f + 1)
                        V.tensor_tensor(hid_lo[:, f, :], hid[:, f, :], hid_hi[:, f, :], ALU.subtract) \
                         .then_inc(hid_ready, 1)
                    add_y(sb_ + 2 * i)

            normalise(N_FFN0, 1)
            ffn(A_FF0, B_FF0, E_FF0, FF_TILES // 2)

            normalise(N_KV, 2)

            def tile(s, j, n=None):
                V.wait_ge(tile_ready, 2 * (s if n is None else n) + j + 1)
                return bank[2 * (s % 2) + j]

            for p in range(2):
                low_a(A_KCMP + p + 1)
                for j in range(2):
                    b = tile(A_KCMP + p, j)
                    V.tensor_copy(kraw[:, 2 * p + j, :], b[0:DQK, :]).then_inc(tile_free, 1)
            low_a(A_VCMP + 1)
            for j in range(2):
                b = tile(A_VCMP, j)
                V.tensor_copy(vraw[:, 2 * j, :], b[0:DV, :])
                V.tensor_copy(vraw[:, 2 * j + 1, :], b[DV:P, :]).then_inc(tile_free, 1)
            V.wait_ge(rope_loaded, 16)

            def rotate(r, bk, x, out):
                V.wait_ge(rope_mm, r + 1)
                if r:
                    V.wait_ge(rope_done, r)
                step(V.tensor_tensor(rtmp[:, 0, :], bank[bk][0:DQK, :], cs[:, 1, :], ALU.mult))
                step(V.tensor_tensor(rtmp[:, 1, :], x, cs[:, 0, :], ALU.mult))
                V.tensor_tensor(out, rtmp[:, 0, :], rtmp[:, 1, :], ALU.add).then_inc(rope_done, 1)

            for b in range(2):
                for p in range(2):
                    s = A_KSEL + 2 * b + p
                    low_a(s + 1)
                    for j in range(2):
                        V.tensor_copy(kx[:, b, 2 * p + j, :], tile(s, j)[0:DQK, :]).then_inc(tile_free, 1)
                    for j in range(2):
                        r = 4 * b + 2 * p + j
                        rotate(r, 4 + r % 2, kx[:, b, 2 * p + j, :], kx[:, b, 2 * p + j, :])
            for b in range(2):
                s = A_VNAT + b
                low_a(s + 1)
                for j in range(2):
                    V.tensor_copy(vn[:, b, 2 * j:2 * j + 2, :],
                                  tile(s, j)[:, :].rearrange("p (t c) -> p t c", t=2)).then_inc(tile_free, 1)
            for b, (src, pos, rows) in enumerate(((kraw, "pos_k", DQK), (vraw, "pos_v", DV))):
                for p in range(4):
                    s = A_W1K + 4 * b + p
                    for l in range(8):
                        tap = 8 * p + l
                        ins = V.tensor_scalar(
                            xl[0:rows, l, :].rearrange("p (g c) -> p g c", g=GROUPS),
                            src[:, :, tap:tap + CSTRIDE * (NCMP - 1) + 1:CSTRIDE],
                            smc(pos, tap, 1, rows), None, ALU.add)
                    ins.then_inc(xl_done, 1)
                    V.wait_ge(xl_rounded, 4 * b + p + 1)
                    V.tensor_tensor(xl_lo[0:rows, :, :], xl[0:rows, :, :], xl_hi[0:rows, :, :], ALU.subtract) \
                     .then_inc(xl_ready, 1)
                    V.wait_ge(xl_ready, 4 * b + p + 1)
                    V.sem_inc(tile_free, 2)
                    low_a(s + 1)
                V.wait_ge(cmp_w2, b + 1)
                if b == 0:
                    V.tensor_copy(kct[:, :], bank[5][0:DQK, 0:124]).then_inc(cmp_done, 1)
                else:
                    V.tensor_copy(vcn[:, :, :], bank[5][0:NCMP, 0:GROUPS * DV]
                                  .rearrange("p (g c) -> p g c", g=GROUPS)).then_inc(cmp_done, 1)

            normalise(N_MIX1, 3)
            low_a(A_GATE + 1)
            V.wait_ge(tile_ready, 2 * A_GATE + 2)
            step(V.tensor_tensor(gates[:, :, :], bank[2 * (A_GATE % 2)][:, 0:NT * NGATE]
                                 .rearrange("p (t c) -> p t c", t=NT),
                                 smc("gate_b", 0, NT * NGATE).rearrange("p (t c) -> p t c", t=NT), ALU.add))
            V.sem_inc(gates_in, 1)
            V.sem_inc(tile_free, 2)
            step.enter(0, 8)
            with V.Fori(0, HEADS // 4) as i:
                step.i = i
                for u in range(2):
                    s = A_Q + u
                    n = s + 2 * i
                    low_a(s + 1, i)
                    for j in range(2):
                        v = 2 * u + j
                        b = tile(s, j, n)
                        V.wait_ge(q_free, 2 * i + u + 1)
                        V.tensor_scalar(qb[:, v, 0, :], b[0:DQK, :], DQK ** -0.5, None, ALU.mult) \
                         .then_inc(tile_free, 1)
                    V.wait_ge(tile_free, 2 * n + 2)
                    for j in range(2):
                        v = 2 * u + j
                        V.wait_ge(rope_mm, 8 + 4 * i + v + 1)
                        V.wait_ge(rope_done, 8 + 4 * i + v)
                        step(V.tensor_tensor(rtmp[:, 0, :], bank[4 + v % 2][0:DQK, :], cs[:, 1, :], ALU.mult))
                        step(V.tensor_tensor(rtmp[:, 1, :], qb[:, v, 0, :], cs[:, 0, :], ALU.mult))
                        V.tensor_tensor(qb[:, v, 1, :], rtmp[:, 0, :], rtmp[:, 1, :], ALU.add).then_inc(rope_done, 1)
            step.leave(HEADS // 4)

            V.wait_ge(gates_done, 1)
            step.enter(0, HPG * (8 + 4 * 2))
            with V.Fori(0, GROUPS) as g:
                step.i = g
                for u in range(HPG):
                    hd = HPG * g + u

                    def gate(t, b, n=1):
                        return gates[:, t:t + n, ds(3 * hd + b, 1)]

                    V.wait_ge(csc_ready, hd + 1)
                    V.wait_ge(ctr_ready, 1 + hd)
                    step(V.tensor_tensor(pc[:, :, :], bank[6][:, 0:124].rearrange("p (t c) -> p t c", t=NT),
                                         cnc("cmp_mask", 124).rearrange("p (t c) -> p t c", t=NT), ALU.add))
                    step(V.tensor_reduce(cst[:, 0, :], pc[:, :, :], AX_X, ALU.max))
                    step(V.tensor_scalar(cst[:, 1, :], cst[:, 0, :], -1e20, None, ALU.max))
                    V.tensor_tensor(pc[:, :, :], pc[:, :, :],
                                    cst[:, 1, :].rearrange("p (t o) -> p t o", o=1).to_broadcast([P, NT, NCMP]),
                                    ALU.subtract).then_inc(csub_done, 1)

                    def peak(t):
                        V.wait_ge(sc_ready, 4 * hd + t + 1)
                        V.wait_ge(pm_ready, 1 + 4 * hd + t - 1 if t >= 2 else 1 + 4 * hd)
                        V.tensor_reduce(ast[:, t % 2, 0:2], psum[:, 2 * (t % 2):2 * (t % 2) + 2, 0:(t + 1) * P],
                                        AX_X, ALU.max, negate=True).then_inc(mx_done, 1)

                    def weigh(t):
                        n = (t + 1) * P
                        V.wait_ge(exp_done, 1 + 4 * hd + t + 1)
                        step(V.reciprocal(ast[:, t % 2, 4:6], ast[:, t % 2, 2:4]))
                        step(V.tensor_tensor(ast[:, t % 2, 6:8], ast[:, t % 2, 4:6],
                                             gates[:, t:t + 1, ds(3 * hd + 1, 2)].rearrange("p a o -> p (a o)"),
                                             ALU.mult))
                        for b in range(2):
                            ins = V.tensor_scalar(pm[:, t % 2, b, 0:n], pm[:, t % 2, b, 0:n],
                                                  ast[:, t % 2, 6 + b:7 + b], None, ALU.mult)
                        ins.then_inc(pm_ready, 1)

                    peak(0)
                    peak(1)
                    V.wait_ge(cexp_done, hd + 1)
                    step(V.tensor_reduce(cst[:, 2, :], pc[:, :, :], AX_X, ALU.add))
                    step(V.tensor_scalar(cst[:, 2, :], cst[:, 2, :], 1e-30, None, ALU.max))
                    step(V.reciprocal(cst[:, 3, :], cst[:, 2, :]))
                    step(V.tensor_tensor(cst[:, 3, :], cst[:, 3, :],
                                         gate(0, 0, NT).rearrange("p a o -> p (a o)"), ALU.mult))
                    step(V.tensor_tensor(pc[:, :, :], pc[:, :, :],
                                    cst[:, 3, :].rearrange("p (t o) -> p t o", o=1).to_broadcast([P, NT, NCMP]),
                                    ALU.mult))
                    V.sem_inc(cpm_ready, 1)
                    for t in range(NT):
                        weigh(t)
                        if t + 2 < NT:
                            peak(t + 2)
                    if u % 2:
                        V.wait_ge(o_rounded, 2 * g + u // 2 + 1)
                        m = ds(2 * g + u // 2, 1)
                        V.tensor_tensor(hn_lo[:, m, :].rearrange("p a s -> p (a s)"), bank[7][:, :],
                                        hn_hi[:, m, :].rearrange("p a s -> p (a s)"), ALU.subtract) \
                         .then_inc(o_split, 1)
            step.leave(GROUPS)

            def add_tiles(s0):
                for p in range(4):
                    s = s0 + p
                    low_a(s + 1)
                    for j in range(2):
                        m = 2 * p + j
                        V.tensor_tensor(h[:, m, :], h[:, m, :], tile(s, j)[:, :], ALU.add).then_inc(tile_free, 1)

            add_tiles(A_WO)
            normalise(N_FFN1, 4)
            ffn(A_FF1, B_FF1, E_FF1, FF_TILES // 2)

            inverse_root(N_FINAL)
            for m in range(KT):
                V.scalar_tensor_tensor(h[:, m, :], h[:, m, :], smc("gain", KT * 5 + m), rstd[:, :],
                                       ALU.mult, ALU.mult).then_inc(hn_scaled, 1)
            V.wait_ge(hn_scaled, KT * (N_FINAL + 1))
            V.sem_inc(hn_ready, KT)
            normalise(N_MIX2, 6)

            low_a(A_SKV + 1)
            V.tensor_copy(sk[:, :], tile(A_SKV, 0)[:, :]).then_inc(qk_raw, 1)
            V.tensor_copy(sv[:, :, :], tile(A_SKV, 1)[:, :].rearrange("p (t c) -> p t c", t=NT)) \
             .then_inc(tile_free, 2)

            def qk_scale(dst, src, gain, k):
                V.wait_ge(qk_sd, k)
                step(V.reciprocal(rstd[:, :], sd[:, :]))
                V.scalar_tensor_tensor(dst, src, smc(gain), rstd[:, :], ALU.mult, ALU.mult).then_inc(qk_norm, 1)

            qk_scale(sk[:, :], sk[:, :], "k_g", 1)
            V.wait_ge(alibi_loaded, 16)

            def raw_w(m):
                s = A_SQ + m
                low_a(s + 1)
                V.wait_ge(tile_ready, 2 * s + 2)
                if m >= 2:
                    V.wait_ge(qk_norm, m)
                V.tensor_copy(tmp[:, m % 2, :], bank[2 * (s % 2)][:, :]).then_inc(tile_free, 2)
                V.wait_ge(tile_free, 2 * s + 2)
                V.sem_inc(qk_raw, 1)

            def scale_w(m):
                if m:
                    V.wait_ge(w_sc, 2 * m)
                qk_scale(qn[:, :], tmp[:, m % 2, :], "q_g", m + 2)

            def peak_w(m, half):
                it = 2 * m + half
                V.wait_ge(w_sc, it + 1)
                if m:
                    V.wait_ge(w_tr, 1 + it - 1)
                bias = al[:, it:it + 1, :]
                for (c, n, b) in ((0, 2, 4), (S, 1, 5)):
                    step(V.scalar_tensor_tensor(
                        wp[:, half, c:c + n * 2 * P].rearrange("p (n w) -> p n w", n=n),
                        bank[b][:, 0:n * 2 * P].rearrange("p (n w) -> p n w", n=n), SWA_HD ** -0.5,
                        bias.to_broadcast([P, n, 2 * P]), ALU.mult, ALU.add))
                step(V.scalar_tensor_tensor(wp[:, half, 6 * P:7 * P], bank[5][:, 2 * P:3 * P], SWA_HD ** -0.5,
                                            al[:, it, P:2 * P], ALU.mult, ALU.add))
                step(V.tensor_reduce(wst[:, half, 0:3], wp[:, half, 0:6 * P].rearrange("p (t w) -> p t w", t=3),
                                     AX_X, ALU.max))
                step(V.tensor_reduce(wst[:, half, 3:4], wp[:, half, 6 * P:7 * P], AX_X, ALU.max))
                V.tensor_scalar(wst[:, half, 4:8], wst[:, half, 0:4], smc("sink", it), -1.0,
                                ALU.max, ALU.mult).then_inc(w_mx, 1)

            def weigh_w(m, half):
                V.wait_ge(w_exp, 1 + 2 * m + half + 1)
                step(V.tensor_tensor(wst[:, half, 8:12], wst[:, half, 8:12], wst[:, half, 12:16], ALU.add))
                step(V.reciprocal(wst[:, half, 16:20], wst[:, half, 8:12]))
                for k, (t, k0, w, c) in enumerate(WIN):
                    ins = V.tensor_scalar(wp[:, half, c:c + w], wp[:, half, c:c + w],
                                          wst[:, half, 16 + k:17 + k], None, ALU.mult)
                ins.then_inc(w_pm, 1)

            raw_w(0)
            scale_w(0)
            raw_w(1)
            for m in range(SWA_TILES):
                peak_w(m, 0)
                peak_w(m, 1)
                weigh_w(m, 0)
                if m + 1 < SWA_TILES:
                    scale_w(m + 1)
                weigh_w(m, 1)
                if m + 2 < SWA_TILES:
                    raw_w(m + 2)
                V.wait_ge(w_or, m + 1)
                V.tensor_tensor(ys_lo[:, m, :], bank[3][:, :], ys_hi[:, m, :], ALU.subtract).then_inc(w_os, 1)

            V.wait_ge(decay_loaded, 16)
            step.enter(0, 3)
            with V.Fori(0, RET_H) as i:
                step.i = i
                low_a(A_RET + 1, i)
                V.tensor_copy(rq[:, :], tile(A_RET, 0, A_RET + 2 * i)[:, :]).then_inc(tile_free, 1)
                V.tensor_copy(rk[:, :], tile(A_RET, 1, A_RET + 2 * i)[:, :]).then_inc(tile_free, 1)
                low_a(A_RET + 2, i)
                b = tile(A_RET + 1, 1, A_RET + 1 + 2 * i)
                V.wait_ge(r_gate, i + 1)
                V.tensor_copy(rv[:, :], b[:, :]).then_inc(tile_free, 2)
                for j in range(4):
                    V.wait_ge(r_sc, 4 * i + j + 1)
                    V.wait_ge(r_o, 1 + 4 * i + j - 1 if j >= 2 else 4 * i)
                    V.tensor_tensor(srt[:, j % 2, 0:S - j * P], bank[4 + j % 2][:, 0:S - j * P],
                                    dk[:, ds(i, 1), 0:S - j * P].rearrange("p a s -> p (a s)"), ALU.mult) \
                     .then_inc(r_dec, 1)
                V.wait_ge(r_o, 1 + 4 * i + 4)
                V.tensor_copy(ry[:, :], bank[6][:, :]).then_inc(r_y, 1)
                V.wait_ge(r_mean, i + 1)
                V.wait_ge(r_rounded, 1 + i)
                V.scalar_tensor_tensor(ryc[:, :], bank[7][:, :], -1.0 / P, ry[:, :], ALU.mult, ALU.add) \
                 .then_inc(r_c, 1)
                V.wait_ge(r_sd, i + 1)
                step(V.reciprocal(rstd[:, :], sd[:, :]))
                step(V.scalar_tensor_tensor(ryc[:, :], ryc[:, :], sm[:, ds(SM["ret_g"] + i, 1)], rstd[:, :],
                                            ALU.mult, ALU.mult))
                V.scalar_tensor_tensor(ryc[:, :], ryc[:, :], sm[:, ds(SM["ret_b"] + i, 1)], rgs[:, :],
                                       ALU.add, ALU.mult).then_inc(r_g, 1)
                V.wait_ge(r_rounded, 1 + i + 1)
                step(V.tensor_tensor(yr_lo[:, ds(i, 1), :].rearrange("p a s -> p (a s)"), ryc[:, :],
                                     yr_hi[:, ds(i, 1), :].rearrange("p a s -> p (a s)"), ALU.subtract))
                V.sem_inc(r_split, 1)
            step.leave(RET_H)

            step.enter(0, 4)
            with V.Fori(0, KT // 2) as i:
                step.i = i
                for u in range(2):
                    s = A_MRG + u
                    n = s + 2 * i
                    nb = B_MRG + u + 2 * i
                    low_a(s + 1, i)
                    low_b(B_MRG + u, i)
                    V.wait_ge(mg_gate, 2 * (2 * i + u) + 2)
                    V.wait_ge(y_ready, 4 * nb + 2)
                    V.wait_ge(mg_ready, 1 + 2 * i + u)
                    step(V.tensor_tensor(tmp[:, 1, :], bank[4 + 2 * u][:, :], sq[:, 0, :], ALU.mult))
                    V.wait_ge(y_ready, 4 * nb + 4)
                    step(V.tensor_tensor(tmp[:, 0, :], bank[5 + 2 * u][:, :], sq[:, 1, :], ALU.mult))
                    V.sem_inc(tile_free, 2)
                    V.sem_inc(y_free, 4)
                    V.tensor_tensor(tmp[:, 0, :], tmp[:, 0, :], tmp[:, 1, :], ALU.add).then_inc(mg_sum, 1)
                    V.wait_ge(mg_rounded, 2 * i + u + 1)
                    V.tensor_tensor(mg_lo[:, ds(2 * i + u, 1), :].rearrange("p a s -> p (a s)"), tmp[:, 0, :],
                                    mg_hi[:, ds(2 * i + u, 1), :].rearrange("p a s -> p (a s)"), ALU.subtract) \
                     .then_inc(mg_ready, 1)
            step.leave(KT // 2)
            add_tiles(A_OUT)
            normalise(N_MOE, 7)

            V.tensor_copy(ident_r[:, :], ident).then_inc(ident_ready, 1)
            V.wait_ge(tile_ready, 2 * A_ROUTE + 2)
            step(V.tensor_tensor(logit[:, :, :], bank[2 * (A_ROUTE % 2)][:, 0:NT * NROUTE]
                                 .rearrange("p (t c) -> p t c", t=NT),
                                 smc("route_b", 0, NT * NROUTE).rearrange("p (t c) -> p t c", t=NT), ALU.add))
            V.sem_inc(tile_free, 2)

            def wide(x, n):
                return x.rearrange("p (t o) -> p t o", o=1).to_broadcast([P, NT, n])

            def best(dst, mark, x, prio, n, top):
                step(V.tensor_reduce(top, x, AX_X, ALU.max))
                step(V.tensor_tensor(mark, x, wide(top, n), ALU.is_ge))
                step(V.tensor_tensor(mark, mark, prio, ALU.mult))
                step(V.tensor_reduce(rt[:, 0, :], mark, AX_X, ALU.max))
                step(V.tensor_tensor(dst, mark, wide(rt[:, 0, :], n), ALU.is_equal))

            gl = logit[:, :, 0:EGROUPS]
            pg = cnc("prio_g", NT * EGROUPS).rearrange("p (t c) -> p t c", t=NT)
            pe_ = cnc("prio_e", NT * EPG).rearrange("p (t c) -> p t c", t=NT)
            best(rtg[:, 2, :, :], rtg[:, 3, :, :], gl, pg, EGROUPS, rt[:, 1, :])
            V.sem_inc(marks_ready, 1)

            def low_token(c):
                cols = slice((c % 2) * 512, (c % 2 + 1) * 512)
                V.wait_ge(nat_rounded, c + 1)
                V.tensor_tensor(nat_lo[:, c // 2, cols], bank[4 + c % 4][:, :], nat_hi[:, c // 2, cols], ALU.subtract) \
                 .then_inc(nat_ready, 1)

            for c in range(4):
                low_token(c)
            step(V.tensor_tensor(rtg[:, 0, :, :], gl, wide(rt[:, 1, :], EGROUPS), ALU.subtract))
            V.wait_ge(rank_mm, 1)
            step(V.tensor_copy(rank[:, :, :], bank[3][:, 0:NT * EGROUPS].rearrange("p (t g) -> p t g", t=NT)))
            step(V.tensor_copy(grp[:, 0, :], bank[3][:, NT * EGROUPS:(NT + 1) * EGROUPS]))
            step(V.tensor_scalar(grp[:, 1, :], grp[:, 0, :], 0.5, None, ALU.is_ge))
            step(V.tensor_scalar(grp[:, 2, :], grp[:, 0, :], XB + 0.5, None, ALU.is_ge))
            step(V.tensor_tensor(grp[:, 3, :], grp[:, 1, :], grp[:, 2, :], ALU.add))
            step(V.tensor_copy(grp[:, 4, :], grp[:, 3, :]))
            for g in range(1, EGROUPS):
                step(V.tensor_tensor(grp[:, 4, g:g + 1], grp[:, 4, g - 1:g], grp[:, 3, g:g + 1], ALU.add))
            for g in range(3):
                step(V.tensor_scalar(item[:, g, 0:XITEMS], cnc("iota", XITEMS), grp[:, 4, g:g + 1], None, ALU.is_ge))
            step(V.tensor_tensor(item[:, 0, 0:XITEMS], item[:, 0, 0:XITEMS], item[:, 1, 0:XITEMS], ALU.add))
            step(V.tensor_tensor(item[:, 0, 0:XITEMS], item[:, 0, 0:XITEMS], item[:, 2, 0:XITEMS], ALU.add))
            V.tensor_copy(item_group[:, 0:XITEMS], item[:, 0, 0:XITEMS]).then_inc(groups_ready, 1)
            step(V.tensor_tensor(grp[:, 5, :], grp[:, 4, :], grp[:, 3, :], ALU.subtract))
            step(V.tensor_scalar(grp[:, 6, :], grp[:, 5, :], float(XB), -1.0, ALU.mult, ALU.add))
            step(V.tensor_tensor(rank[:, :, :], rank[:, :, :],
                                 grp[:, 6:7, :].to_broadcast([P, NT, EGROUPS]), ALU.add))
            step(V.tensor_tensor(rank[:, :, :], rank[:, :, :], rtg[:, 2, :, :], ALU.mult))
            step(V.tensor_reduce(slot[:, :], rank[:, :, :], AX_X, ALU.add))
            for t in range(NT):
                ins = V.tensor_scalar(slot_wide[:, t * P:(t + 1) * P], ones, slot[:, t:t + 1], None, ALU.mult)
            ins.then_inc(wide_ready, 1)

            for g in range(EGROUPS):
                lg = logit[:, :, EGROUPS + g * EPG:EGROUPS + (g + 1) * EPG]
                mark = rtg[:, 2, :, g:g + 1].to_broadcast([P, NT, EPG])
                dst = rte[:, 0, :, :] if g == 0 else rte[:, 1, :, :]
                step(V.tensor_tensor(dst, lg, mark, ALU.mult))
                if g:
                    step(V.tensor_tensor(rte[:, 0, :, :], rte[:, 0, :, :], rte[:, 1, :, :], ALU.add))
            best(rte[:, 2, :, :], rte[:, 3, :, :], rte[:, 0, :, :], pe_, EPG, rt[:, 2, :])
            step(V.tensor_scalar(rte[:, 4, :, :], rte[:, 2, :, :], 2 * NEG, None, ALU.mult))
            step(V.tensor_tensor(rte[:, 4, :, :], rte[:, 4, :, :], rte[:, 0, :, :], ALU.add))
            best(rte[:, 5, :, :], rte[:, 6, :, :], rte[:, 4, :, :], pe_, EPG, rt[:, 3, :])
            step(V.tensor_tensor(rt[:, 4, :], rt[:, 3, :], rt[:, 2, :], ALU.subtract))
            V.sem_inc(rt_in, 1)
            V.wait_ge(rt_exp, 1)
            step(V.tensor_reduce(rt[:, 6, :], rtg[:, 1, :, :], AX_X, ALU.add))
            step(V.tensor_scalar(rt[:, 7, :], rt[:, 5, :], 1.0, None, ALU.add))
            step(V.tensor_tensor(rt[:, 8, :], rt[:, 6, :], rt[:, 7, :], ALU.mult))
            step(V.reciprocal(rt[:, 9, :], rt[:, 8, :]))
            step(V.tensor_tensor(rt[:, 10, :], rt[:, 9, :], rt[:, 5, :], ALU.mult))
            step(V.tensor_tensor(rte[:, 7, :, :], rte[:, 2, :, :], wide(rt[:, 9, :], EPG), ALU.mult))
            step(V.tensor_tensor(rte[:, 8, :, :], rte[:, 5, :, :], wide(rt[:, 10, :], EPG), ALU.mult))
            step(V.tensor_tensor(rte[:, 9, :, :], rte[:, 7, :, :], rte[:, 8, :, :], ALU.add))
            step(V.tensor_copy(w_hi[:, :, :], rte[:, 9, :, :]))
            step(V.tensor_tensor(w_lo[:, :, :], rte[:, 9, :, :], w_hi[:, :, :], ALU.subtract))

            def select(it):
                for t in range(NT):
                    ins = V.tensor_scalar(sel[:, t, :], cnc("iota", XB), slot[:, t:t + 1], -float(XB * it),
                                          ALU.subtract, ALU.is_equal)
                ins.then_inc(sel_ready, 1)

            def low_gather(it):
                x = slice((it % 2) * XB, (it % 2 + 1) * XB)
                for c in range(KT // 2):
                    k = GATHER[it] + c
                    V.wait_ge(x_rounded, KT // 2 * it + c + 1)
                    V.tensor_tensor(hn_lo[:, 2 * c:2 * c + 2, x], bank[2 + k % 2].rearrange("p (f x) -> p f x", f=2),
                                    hn_hi[:, 2 * c:2 * c + 2, x], ALU.subtract).then_inc(side_free, 1)
                k = GATHER[it] + KT // 2
                V.wait_ge(side_mm, k + 1)
                if it:
                    V.wait_ge(wslot_stored, 16 * it)
                V.tensor_copy(wslot[:, :], bank[2 + k % 2][0:EPG, 0:XB]).then_inc(wslot_done, 1)
                V.wait_ge(wslot_done, it + 1)
                V.sem_inc(side_free, 1)

            def select_t(it):
                if it:
                    V.wait_ge(side_mm, SCATTER[it - 1] + KT)
                for u in range(XSUB):
                    c = CN["slot_id"] + XSUB * it + u
                    ins = V.tensor_scalar(sel_t[:, u, :], slot_row[:, :], cn[:, c:c + 1], None, ALU.is_equal)
                ins.then_inc(sel_t_ready, 1)

            def add_block(it):
                for m in range(KT):
                    k = SCATTER[it] + m
                    V.wait_ge(side_mm, k + 1)
                    V.tensor_tensor(h[:, m, :], h[:, m, :], bank[2 + k % 2][:, :], ALU.add).then_inc(h_added, 1)
                    V.wait_ge(h_added, KT * it + m + 1)
                    V.sem_inc(side_free, 1)

            def expert(it, i):
                sa, sb_ = A_MOE + 2 * EPG * it, B_MOE + 2 * EPG * it
                for f in range(2):
                    low_b(sb_ + f, i)
                for f in range(2):
                    n = sa + f + 2 * i
                    V.wait_ge(gate_done, 2 * (E_MOE - E_FF0 + EPG * it + i) + f + 1)
                    if f == 0:
                        V.wait_ge(comb_loaded, 16 * (EPG * it + i) + 16)
                    step(V.tensor_tensor(xsg[:, f, :], xsg[:, f, :], xcomb, ALU.mult))
                    V.wait_ge(tile_ready, 2 * n + 2)
                    V.tensor_tensor(xhid[:, f, :], xsg[:, f, :], bank[(sa + f) % 2][:, XB:2 * XB], ALU.mult) \
                     .then_inc(tile_free, 2)
                    V.wait_ge(hid_rounded, 2 * (E_MOE + EPG * it + i) + f + 1)
                    V.tensor_tensor(xhid_lo[:, f, :], xhid[:, f, :], xhid_hi[:, f, :], ALU.subtract) \
                     .then_inc(hid_ready, 1)
                    low_a(sa + f + 2, i)

            select(0)
            for c in range(4, 8):
                low_token(c)
            low_a(A_MOE)
            low_gather(0)
            low_a(A_MOE + 1)
            V.wait_ge(rank_mm, 2)
            V.tensor_copy(slot_row[:, :], bank[2][:, :]).then_inc(wide_ready, 1)
            for it in range(XITEMS):
                if it:
                    select_t(it - 1)
                if it + 1 < XITEMS:
                    select(it + 1)
                expert(it, 0)
                if it:
                    add_block(it - 1)
                if it + 1 < XITEMS:
                    low_gather(it + 1)
                step.enter(1, 2)
                step.base -= 2
                with V.Fori(1, EPG) as i:
                    step.i = i
                    expert(it, i)
                step.leave(EPG)
                for hb in range(2):
                    for u in range(XSUB):
                        V.wait_ge(xy_rounded, 4 * it + XSUB * hb + u + 1)
                        V.tensor_tensor(xy_lo[:, u, hb * 512:(hb + 1) * 512], bank[4 + 2 * u + hb][:, :],
                                        xy_hi[:, u, hb * 512:(hb + 1) * 512], ALU.subtract).then_inc(xy_ready, 1)
            select_t(XITEMS - 1)
            add_block(XITEMS - 1)

            V.wait_ge(p_rounded, 1)
            V.tensor_tensor(ptr_lo[:, :, :], ptr[:, :, :], ptr_hi[:, :, :], ALU.subtract).then_inc(p_ready, 1)
            normalise(N_PLEG, 8)
            for m in range(KT):
                V.wait_ge(ple_mm, m + 1)
                V.tensor_copy(ple[:, m, :], bank[m % 2 + 2 * (A_PLE % 2)][:, :]).then_inc(pg_done, 1)
            V.wait_ge(pg_done, KT)
            V.sem_inc(tile_free, 2)
            inverse_root(N_PLE)
            for m in range(KT):
                ins = V.scalar_tensor_tensor(ple[:, m, :], ple[:, m, :], smc("gain", KT * 9 + m), rstd[:, :],
                                             ALU.mult, ALU.mult)
            step(ins)
            for p in range(4):
                s = A_PG + p
                if p < 3:
                    low_a(s + 1)
                for j in range(2):
                    m = 2 * p + j
                    V.wait_ge(out_done, m + 1)
                    step(V.tensor_tensor(ple[:, m, :], ple[:, m, :], pgs[:, j, :], ALU.mult))
                    V.tensor_tensor(h[:, m, :], h[:, m, :], ple[:, m, :], ALU.add).then_inc(tile_free, 1)

        @block.gpsimd
        def _(pool):
            def rnn_pair(i):
                for u in range(2):
                    n = 2 * i + u
                    pool.wait_ge(xc_done, n + 1)
                    pool.wait_ge(tile_free, 2 * n + 2)
                    pool.tensor_tensor(gx[:, u, :], ig[:, u, :], xc[:, u, :], ALU.mult).then_inc(gx_done, 1)
                for u in range(2):
                    n = 2 * i + u
                    pool.wait_ge(decay_done, 2 * n + 2)
                    pool.tensor_tensor(mu[:, u, :], aa[:, u, :], aa[:, u, :], ALU.mult).then_inc(asq_done, 1)
                for u in range(2):
                    n = 2 * i + u
                    pool.wait_ge(mult_done, n + 1)
                    pool.wait_ge(gx_done, n + 1)
                    pool.tensor_tensor(gx[:, u, :], gx[:, u, :], mu[:, u, :], ALU.mult).then_inc(bx_done, 1)
                for u in range(2):
                    n = 2 * i + u
                    pool.wait_ge(scan_done, n + 1)
                    pool.wait_ge(gelu_done, n + 1)
                    pool.tensor_tensor(hs[:, u, :], hs[:, u, :], gel[:, u, :], ALU.mult).then_inc(rec_done, 1)

            with pool.Fori(0, RNN_BLOCKS // 2) as i:
                rnn_pair(i)

            pool.wait_ge(hn_ready, KT * (N_KV + 1))
            pool.dma_start(cs[:, :, :], rope).then_inc(rope_loaded, 16)
            with pool.Fori(0, HEADS // 4) as i:
                for u in range(2):
                    pool.wait_ge(rope_done, 8 + 4 * i + 2 * u + 2)
                    pool.dma_start(q_dram[ds(4 * i + 2 * u, 2)].rearrange("a p n -> p a n"),
                                   qb[:, 2 * u:2 * u + 2, :, :].rearrange("p a b n -> p a (b n)")) \
                        .then_inc(q_stored[u], 16)
                    pool.wait_ge(q_stored[u], 16 * i + 16)
                    pool.sem_inc(q_free, 1)
            with pool.Fori(0, GROUPS) as g:
                pool.wait_ge(o_ready, 1 + HPG * g)
                for b in range(2):
                    pool.tensor_copy(vs[:, b, :, :], vn[:, b, :, ds(g * DV, DV)]).then_inc(v_staged, 1)
                pool.tensor_copy(vcs[:, :], vcn[:, ds(g, 1), :].rearrange("p a c -> p (a c)")).then_inc(v_staged, 1)
                for u in range(HPG):
                    if u >= 2:
                        pool.wait_ge(sc_ready, 4 * (HPG * g + u - 1))
                    pool.dma_start(qs[:, u % 2, :, :].rearrange("p b n -> p (b n)"),
                                   q_dram[ds(HPG * g + u, 1)].rearrange("a p n -> p (a n)")) \
                        .then_inc(q_staged[u % 2], 16)

            pool.wait_ge(hn_ready, KT * (N_MIX2 + 1))
            pool.dma_start(al[:, :, :], alibi).then_inc(alibi_loaded, 16)
            pool.wait_ge(w_os, 1 + SWA_TILES)
            pool.dma_start(dk[:, :, :], decay).then_inc(decay_loaded, 16)

            for it in range(XITEMS):
                pool.wait_ge(wslot_done, it + 1)
                pool.dma_start(c_dram[EPG * it:EPG * (it + 1), :], wslot[:, :]).then_inc(wslot_stored, 16)
                pool.wait_ge(wslot_stored, 16 * it + 16)
                with pool.Fori(0, EPG) as i:
                    pool.wait_ge(tile_free, 2 * (A_MOE + 2 * EPG * it + 2 * i))
                    pool.dma_start(xcomb, c_dram[ds(EPG * it + i, 1), :].to_broadcast([P, XB])) \
                        .then_inc(comb_loaded, 16)

            pool.wait_ge(h_added, KT * XITEMS)
            pool.dma_start(ptr[:, :, :], p_t.rearrange("(k p) s -> p k s", p=P)).then_inc(p_loaded, 16)
            out_v = out_t.rearrange("(k p) s -> p k s", p=P)
            for m in range(KT):
                pool.wait_ge(tile_free, 2 * A_PG + m + 1)
                pool.dma_start(out_v[:, m, :], h[:, m, :]).then_inc(stored, 16)
            pool.wait_ge(stored, 16 * KT)


def _pack_a(v):
    out = np.zeros((v.shape[0], P, WA), np.float32)
    out[:, :v.shape[1], :v.shape[2]] = v
    return out


def _cols(w, groups):
    k = w.shape[0] // P
    t = w.reshape(k, P, -1)
    return _pack_a(np.stack([np.concatenate([t[:, :, c] for c in g], 2).transpose(1, 0, 2).reshape(P, -1)
                             for g in groups]))


def _pairs(w, width, step=2):
    n = w.shape[1] // width
    return _cols(w, [[slice(i * width, (i + step) * width)] for i in range(0, n, step)])


def _down(w, rows):
    v = w.reshape(-1, 2, rows, 2, 512).transpose(0, 3, 2, 1, 4).reshape(-1, rows, WB)
    out = np.zeros((v.shape[0], P, WB), np.float32)
    out[:, :rows] = v
    return out


def _panels(x):
    a = []
    w_in = x["a_w_in"][0]
    gates = np.concatenate([x["a_w_ra"][0], x["a_w_ix"][0]], 2)
    rnn = _cols(w_in, [[slice(c * RNN_W, (c + 1) * RNN_W), slice(1536 + c * RNN_W, 1536 + (c + 1) * RNN_W)]
                       for c in range(RNN_BLOCKS)])
    rnn[:, :RNN_W, 1536:1728] = gates
    a.append(rnn)

    def ff(w):
        n = w.shape[1] // 2
        return _cols(w, [[slice(f * P, (f + 1) * P), slice(n + f * P, n + (f + 1) * P)] for f in range(n // P)])

    a.append(ff(x["ffn_w_gu"][0]))
    kc, vc, ks, vs, kw, vw = np.split(x["kv_w"], np.cumsum([384, 256, 384, 256, 384])[:5], 1)
    a += [_pairs(kc, DQK), _pairs(vc, P), _pairs(ks, DQK), _pairs(kw, DQK), _cols(vs, [[slice(0, 256)]]),
          _cols(vw, [[slice(0, 256)]])]
    for w, d in ((x["cmp_w1_k"], DQK), (x["cmp_w1_v"], DV)):
        a.append(_pack_a(w.reshape(4, 8, d, 256).transpose(0, 2, 1, 3).reshape(4, d, 2048)))
    w_q = x["b_w_q"][0]
    a += [_cols(w_q, [[slice(HEADS * DQK, HEADS * DQK + NGATE)]]), _pairs(w_q[:, :HEADS * DQK], DQK)]
    a.append(_pairs(x["b_w_o"][0], P))
    a.append(ff(x["ffn_w_gu"][1]))
    rq, rk, rv, rg, sq, sk, sv, gr, gs = np.split(
        x["w_in_2"][0], np.cumsum([512, 512, 512, 512, 512, 128, 128, 1024]), 1)
    order = np.concatenate([np.arange(64 * q, 64 * q + 64) for m in range(4) for q in (m, m + 4)])
    a.append(_cols(np.concatenate([sk, sv], 1), [[slice(0, 256)]]))
    sqp = np.zeros((D, 1024), np.float32)
    for m in range(4):
        sqp[:, m * 256:m * 256 + 128] = sq[:, order[m * 128:(m + 1) * 128]]
    a.append(_pairs(sqp, P))
    ret = np.concatenate([rq, rk, rg, rv], 1)
    a.append(_cols(ret, [[slice(o + i * P, o + (i + 1) * P), slice(o + 512 + i * P, o + 512 + (i + 1) * P)]
                         for i in range(RET_H) for o in (0, 1024)]))
    a.append(_cols(np.concatenate([gr, gs], 1), [[slice(m * P, (m + 1) * P), slice(D + m * P, D + (m + 1) * P)]
                                                 for m in range(KT)]))
    a.append(_pairs(x["w_out_2"][0], P))
    a.append(_cols(np.concatenate([x["w_router_group_2"][0], x["w_router_expert_2"][0]], 1),
                   [[slice(0, NROUTE)]]))
    eg, eu = x["w_exp_gate_2"][0], x["w_exp_up_2"][0]
    v = np.stack([eg.reshape(EXPERTS, KT, P, 2, P), eu.reshape(EXPERTS, KT, P, 2, P)], 4)
    a.append(v.transpose(0, 3, 2, 1, 4, 5).reshape(2 * EXPERTS, P, WA))
    a.append(_cols(x["w_ple_2"][0], [[slice(0, D)]]))
    a.append(_pairs(x["w_ple_gate_2"][0], P))
    w_a = np.concatenate(a)
    assert w_a.shape == (NA - REPEATED, P, WA), w_a.shape
    ret_o = x["w_ret_o_2"][0].reshape(4, P, KT, P).transpose(2, 1, 0, 3).reshape(KT, P, 512)
    swa_o = x["w_swa_o_2"][0][order].reshape(4, P, KT, P).transpose(2, 1, 0, 3).reshape(KT, P, 512)
    b = [_down(x["a_w_out"][0], RNN_W), _down(x["ffn_w_down"][0], P), _down(x["ffn_w_down"][1], P),
         np.concatenate([ret_o, swa_o], 2), _down(x["w_exp_down_2"][0].reshape(EXPERTS * EFF, D), P)]
    w_b = np.concatenate(b)
    assert w_b.shape == (NB - REPEATED, P, WB), w_b.shape
    return w_a, w_b


def _small(x):
    out = np.zeros((P, N_SMALL), np.float32)

    def put(name, v):
        out[:v.shape[0], SM[name]:SM[name] + v.shape[1]] = v

    gains = [x["norm_g"][0, 0], x["norm_g"][0, 1], x["kv_norm_g"], x["norm_g"][1, 0], x["norm_g"][1, 1],
             x["final_g"], x["mix_norm_g_2"][0], x["ffn_norm_g_2"][0], x["ple_gate_norm_g_2"][0],
             x["ple_norm_g_2"][0]]
    put("gain", np.concatenate([g.reshape(KT, P).T for g in gains], 1))
    put("conv_w", x["a_conv_w"][0].reshape(4, RNN_BLOCKS, RNN_W).transpose(2, 1, 0).reshape(RNN_W, -1))
    put("conv_b", x["a_conv_b"][0].reshape(RNN_BLOCKS, RNN_W).T)
    put("b_ra", x["a_b_ra"][0].T)
    put("b_ix", x["a_b_ix"][0].T)
    put("lam", x["a_lambda"][0].reshape(RNN_BLOCKS, RNN_W).T)
    put("pos_k", x["cmp_pos_k"].T)
    put("pos_v", x["cmp_pos_v"].T)
    put("gate_b", np.broadcast_to(np.tile(x["b_gate_bias"][0], NT), (P, NT * NGATE)))
    put("ret_g", x["ret_gn_g_2"][0].reshape(RET_H, P).T)
    put("ret_b", x["ret_gn_b_2"][0].reshape(RET_H, P).T)
    put("q_g", np.tile(x["q_norm_g_2"][0], 2)[:, None])
    put("k_g", np.tile(x["k_norm_g_2"][0], 2)[:, None])
    put("sink", np.broadcast_to(x["attn_sinks_2"][0].reshape(2, 4).T.reshape(-1), (P, SWA_H)))
    put("route_b", np.broadcast_to(np.tile(np.concatenate(
        [x["b_router_group_2"][0], x["b_router_expert_2"][0]]), NT), (P, NT * NROUTE)))
    put("w2k", x["cmp_w2_k"].reshape(2, P, DQK).transpose(1, 0, 2).reshape(P, -1))
    put("w2v", x["cmp_w2_v"].reshape(2, P, DV).transpose(1, 0, 2).reshape(P, -1))
    return out


def _constants():
    out = np.zeros((P, N_CONST), np.float32)

    def put(name, v):
        out[:v.shape[0], CN[name]:CN[name] + v.shape[1]] = v

    r = np.arange(P)
    put("eps", np.full((P, 1), EPS))
    put("ident", np.eye(P))
    put("ones", np.ones((P, P)))
    put("halves", (r[:, None] // 64 == r[None, :] // 64).astype(np.float32))
    rot = np.zeros((DQK, DQK))
    for k in range(12):
        rot[k + 12, k] = 1.0
        rot[k, k + 12] = 1.0
    put("rot", rot)
    put("causal", np.where(r[None, :] <= r[:, None], 0.0, NEG))
    t = np.arange(S).reshape(NT, P)
    c_end = np.arange(NCMP) * CSTRIDE + CBLOCK - 1
    put("cmp_mask", np.where(c_end[None, None, :] <= t[:, :, None], 0.0, NEG)
        .transpose(1, 0, 2).reshape(P, -1))
    put("prio_g", np.tile(EGROUPS - np.arange(EGROUPS), (P, NT)))
    put("prio_e", np.tile(EPG - np.arange(EPG), (P, NT)))
    put("upto", (r[:, None] <= r[None, :]).astype(np.float32))
    put("iota", np.tile(np.arange(XB), (P, 1)))
    put("slot_id", r[:, None] + P * np.arange(XITEMS * XSUB)[None, :])

    inv = np.float32(500000.0) ** (-np.arange(12, dtype=np.float32) * np.float32(2.0) / np.float32(24))
    ang = (np.arange(S, dtype=np.float32)[:, None] * inv[None, :].astype(np.float32)).astype(np.float64)
    rope = np.zeros((DQK, 2, S), np.float32)
    rope[:, 0] = 1.0
    rope[:12, 0] = rope[12:24, 0] = np.cos(ang).T
    rope[:12, 1] = -np.sin(ang).T
    rope[12:24, 1] = np.sin(ang).T

    c = np.arange(S)
    decay = np.zeros((P, RET_H, S))
    for i in range(RET_H):
        lg = np.log1p(-2.0 ** (-5.0 - i))
        d = c[None, :] - r[:, None]
        decay[:, i] = np.where(d >= 0, np.exp(np.maximum(d, 0) * lg), 0.0) * 128 ** -0.5
    alibi = np.zeros((P, SWA_H, 2 * P))
    rel = r[:, None] + P - np.arange(2 * P)[None, :]
    for m in range(4):
        for half in range(2):
            slope = 2.0 ** (-(m + 4 * half + 1.0))
            alibi[:, 2 * m + half] = np.where((rel >= 0) & (rel < P), -slope * rel, NEG)
    return out, rope, decay.astype(np.float32), alibi.astype(np.float32)


def kernel(**inputs):
    import concourse.bacc as bacc
    from concourse.bass_utils import run_bass_kernel_spmd

    x = {k: np.asarray(v) for k, v in inputs.items()}
    w_a, w_b = _panels(x)
    const, rope, decay, alibi = _constants()
    arrays = {
        "x_t": np.ascontiguousarray(x["x"][0].T), "p_t": np.ascontiguousarray(x["p_2"][0, 0].T),
        "w_a": w_a, "w_b": w_b, "small": _small(x), "const": const, "rope": rope, "decay": decay, "alibi": alibi,
    }
    nc = bacc.Bacc("TRN2", target_bir_lowering=False, num_devices=1)
    aps = [nc.dram_tensor(k, v.shape, F32, kind="ExternalInput").ap() for k, v in arrays.items()]
    out = nc.dram_tensor("out_t", (D, S), F32, kind="ExternalOutput").ap()
    build(nc, *aps, out)
    r = run_bass_kernel_spmd(nc, [arrays], core_ids=[0])
    return r.results[0]["out_t"].T[None]
```

```python
from contextlib import ExitStack

import numpy as np

import concourse.bass as bass
from concourse import mybir

F32 = mybir.dt.float32
F32R = mybir.dt.float32r
I32 = mybir.dt.int32
ALU = mybir.AluOpType
ACT = mybir.ActivationFunctionType
AX_X = mybir.AxisListType.X

P = 128
S = 512
D = 1024
KT = D // P
NT = S // P
EPS = 1e-6
NEG = -1e30

RNN_BLOCKS, RNN_W = 16, 96
FF_TILES = 2816 // P
HEADS, GROUPS, DQK, DV = 16, 4, 96, 64
HPG = HEADS // GROUPS
NCMP, CSTRIDE, CBLOCK = 31, 16, 32
NGATE = 3 * HEADS
RET_H = 4
SWA_H, SWA_HD, SWA_TILES = 8, 64, 4
EXPERTS, EGROUPS, EPG, EFF = 32, 4, 8, 256
NROUTE = EGROUPS + EXPERTS
XB = 256
XITEMS = S // XB + EGROUPS - 1
XSUB = XB // P

WA, WB = 2048, 1024

A_RNN = 0
A_FF0 = A_RNN + RNN_BLOCKS
A_KCMP = A_FF0 + FF_TILES
A_VCMP = A_KCMP + 2
A_KSEL = A_VCMP + 1
A_KWIN = A_KSEL + 2
A_VNAT = A_KWIN + 2
A_W1K = A_VNAT + 2
A_W1V = A_W1K + 4
A_GATE = A_W1V + 4
A_Q = A_GATE + 1
A_WO = A_Q + HEADS // 2
A_FF1 = A_WO + 4
A_SKV = A_FF1 + FF_TILES
A_SQ = A_SKV + 1
A_RET = A_SQ + SWA_TILES
A_MRG = A_RET + 2 * RET_H
A_OUT = A_MRG + KT
A_ROUTE = A_OUT + 4
A_MOE = A_ROUTE + 1
A_PLE = A_MOE + 2 * XITEMS * EPG
A_PG = A_PLE + 1
NA = A_PG + 4

B_RNN = 0
B_FF0 = B_RNN + RNN_BLOCKS
B_FF1 = B_FF0 + FF_TILES
B_MRG = B_FF1 + FF_TILES
B_MOE = B_MRG + KT
NB = B_MOE + 2 * XITEMS * EPG
REPEATED = 2 * (XITEMS * EPG - EXPERTS)

E_RNN = 0
E_FF0 = E_RNN + RNN_BLOCKS // 2
E_FF1 = E_FF0 + FF_TILES // 2
E_MOE = E_FF1 + FF_TILES // 2

(N_MIX0, N_FFN0, N_KV, N_MIX1, N_FFN1, N_FINAL, N_MIX2, N_MOE, N_PLE, N_PLEG) = range(10)

_SMALL = [("gain", 10 * KT), ("conv_w", 4 * RNN_BLOCKS), ("conv_b", RNN_BLOCKS), ("b_ra", RNN_BLOCKS),
          ("b_ix", RNN_BLOCKS), ("lam", RNN_BLOCKS), ("pos_k", CBLOCK), ("pos_v", CBLOCK),
          ("gate_b", NT * NGATE), ("ret_g", RET_H), ("ret_b", RET_H), ("q_g", 1), ("k_g", 1),
          ("sink", SWA_H), ("route_b", NT * NROUTE), ("w2k", 2 * DQK), ("w2v", 2 * DV)]
_CONST = [("eps", 1), ("ident", P), ("ones", P), ("halves", P), ("rot", DQK), ("causal", P),
          ("cmp_mask", NT * NCMP), ("prio_g", NT * EGROUPS), ("prio_e", NT * EPG),
          ("upto", P), ("iota", XB), ("slot_id", XITEMS * XSUB)]


def _columns(parts):
    at, out = 0, {}
    for name, n in parts:
        out[name] = at
        at += n
    return out, at


SM, N_SMALL = _columns(_SMALL)
CN, N_CONST = _columns(_CONST)


WIN = [(1, 0, 2 * P, 0), (2, P, 2 * P, 2 * P), (3, 2 * P, 2 * P, 4 * P), (0, 0, P, 6 * P)]


class Steps:

    def __init__(self, eng, sem):
        self.eng, self.sem = eng, sem
        self.base = self.count = self.per = 0
        self.i = 0

    def __call__(self, ins):
        ins.then_inc(self.sem, 1)
        self.count += 1
        self.eng.wait_ge(self.sem, self.base + self.per * self.i + self.count)

    def enter(self, i, per):
        self.base += self.count
        self.i, self.per, self.count = i, per, 0

    def leave(self, trips):
        assert self.count == self.per, f"the loop takes {self.count} steps"
        self.base += self.per * trips
        self.i = self.per = self.count = 0


def build(nc, x_t, p_t, w_a, w_b, small, const, rope, decay, alibi, out_t):
    ctx = ExitStack()
    with ctx:
        def sem(name):
            return ctx.enter_context(nc.semaphore(name))

        def sb(name, shape, dt=F32, stack=None):
            return (stack or ctx).enter_context(nc.sbuf_tensor(name, shape, dt))

        a_raw = [sb(f"a_raw{i}", [P, WA]) for i in range(2)]
        a_hi = [sb(f"a_hi{i}", [P, WA], F32R) for i in range(2)]
        a_lo = [sb(f"a_lo{i}", [P, WA], F32R) for i in range(2)]
        b_raw = [sb(f"b_raw{i}", [P, WB]) for i in range(2)]
        b_hi = [sb(f"b_hi{i}", [P, WB], F32R) for i in range(2)]
        b_lo = [sb(f"b_lo{i}", [P, WB], F32R) for i in range(2)]
        h = sb("h", [P, KT, S])
        hn_hi = sb("hn_hi", [P, KT, S], F32R)
        hn_lo = sb("hn_lo", [P, KT, S], F32R)
        tmp = sb("tmp", [P, 2, S])
        sq = sb("sq", [P, 2, S])
        sd = sb("sd", [P, S])
        rstd = sb("rstd", [P, S])
        warm = sb("warm", [P, 16])
        sm = sb("sm", [P, N_SMALL])
        cn = sb("cn", [P, N_CONST])
        psum = ctx.enter_context(nc.psum_tensor("psum", [P, 8, S], F32))
        bank = [psum[:, i, :] for i in range(8)]
        masks = sb("masks", [P, 2, P], mybir.dt.bfloat16)
        xsg, xhid, xcomb = tmp[:, :, 0:XB], tmp[:, :, XB:2 * XB], sq[:, 0, 0:XB]
        slot_row, slot_wide = sd, rstd

        def smc(name, k=0, n=1, rows=P):
            return sm[0:rows, SM[name] + k:SM[name] + k + n]

        def cnc(name, n, rows=P):
            return cn[0:rows, CN[name]:CN[name] + n]

        ident, ones = cnc("ident", P), cnc("ones", P)
        halves, rot = cnc("halves", P), cnc("rot", DQK, DQK)
        eps = cnc("eps", 1)

        with ExitStack() as st:
            rhid_hi = sb("rhid_hi", [P, 2, S], F32R, st)
            rhid_lo = sb("rhid_lo", [P, 2, S], F32R, st)
            xc, ybr, rg, ig, gx, aa, pp, mu, hs, gel = (
                sb(nm, [RNN_W, 2, S], F32, st) for nm in
                ("xc", "ybr", "rg", "ig", "gx", "aa", "pp", "mu", "hs", "gel"))
            xc_hi = sb("xc_hi", [RNN_W, 2, S], F32R, st)
            xc_lo = sb("xc_lo", [RNN_W, 2, S], F32R, st)
            spt = sb("spt", [RNN_W, 8, RNN_BLOCKS], F32, st)
        with ExitStack() as st:
            hid_hi = sb("hid_hi", [P, 2, S], F32R, st)
            hid_lo = sb("hid_lo", [P, 2, S], F32R, st)
            hid = sb("hid", [P, 2, S], F32, st)
            sg = sb("sg", [P, 2, S], F32, st)
        with ExitStack() as st:
            xhid_hi = sb("xhid_hi", [P, 2, XB], F32R, st)
            xhid_lo = sb("xhid_lo", [P, 2, XB], F32R, st)
            nat_hi = sb("nat_hi", [P, NT, D], F32R, st)
            nat_lo = sb("nat_lo", [P, NT, D], F32R, st)
            xy_hi = sb("xy_hi", [P, XSUB, D], F32R, st)
            xy_lo = sb("xy_lo", [P, XSUB, D], F32R, st)
            sel = sb("sel", [P, NT, XB], F32R, st)
            sel_t = sb("sel_t", [P, XSUB, S], F32R, st)
            ident_r = sb("ident_r", [P, P], F32R, st)
            w_hi = sb("w_hi", [P, NT, EPG], F32R, st)
            w_lo = sb("w_lo", [P, NT, EPG], F32R, st)
            grp = sb("grp", [P, 8, EGROUPS], F32, st)
            rank = sb("rank", [P, NT, EGROUPS], F32, st)
            slot = sb("slot", [P, NT], F32, st)
            item = sb("item", [P, 3, 8], F32, st)
            item_group = sb("item_group", [P, 8], I32, st)
            logit = sb("logit", [P, NT, NROUTE], F32, st)
            rt = sb("rt", [P, 24, NT], F32, st)
            rtg = sb("rtg", [P, 4, NT, EGROUPS], F32, st)
            rte = sb("rte", [P, 12, NT, EPG], F32, st)
            wslot = sb("wslot", [EPG, XB], F32, st)
        with ExitStack() as st:
            kx = sb("kx", [DQK, 2, GROUPS, S], F32, st)
            vn = sb("vn", [P, 2, NT, GROUPS * DV], F32, st)
            kct = sb("kct", [DQK, GROUPS * NCMP], F32, st)
            vcn = sb("vcn", [NCMP, GROUPS, DV], F32, st)
            gates = sb("gates", [P, NT, NGATE], F32, st)
            s1 = st.enter_context(ExitStack())
            cs = sb("cs", [DQK, 2, S], F32, s1)
            rtmp = sb("rtmp", [DQK, 2, S], F32, s1)
            with ExitStack() as s2:
                kraw = sb("kraw", [DQK, GROUPS, S], F32, s2)
                vraw = sb("vraw", [DV, GROUPS, S], F32, s2)
                xpos = sb("xpos", [DQK, GROUPS, S], F32, s2)
                hidn = sb("hidn", [P, 2 * P], F32, s2)
                chid = sb("chid", [P, 2, P], F32, s2)
            with ExitStack() as s2:
                qb = sb("qb", [DQK, 4, 2, S], F32, s2)
            s1.close()
            with ExitStack() as s2:
                pm = sb("pm", [P, 2, 2, S], F32, s2)
                pt = sb("pt", [P, 2, NT, S], F32, s2)
                qs = sb("qs", [DQK, 2, 2, S], F32, s2)
                vs = sb("vs", [P, 2, NT, DV], F32, s2)
                vcs = sb("vcs", [NCMP, DV], F32, s2)
                pc = sb("pc", [P, NT, NCMP], F32, s2)
                ptc = sb("ptc", [NCMP, S], F32, s2)
                ast = sb("ast", [P, 2, 8], F32, s2)
                cst = sb("cst", [P, 4, NT], F32, s2)
        with ExitStack() as st:
            ys_hi = sb("ys_hi", [P, SWA_TILES, S], F32R, st)
            ys_lo = sb("ys_lo", [P, SWA_TILES, S], F32R, st)
            yr_hi = sb("yr_hi", [P, RET_H, S], F32R, st)
            yr_lo = sb("yr_lo", [P, RET_H, S], F32R, st)
            with ExitStack() as s2:
                al = sb("al", [P, SWA_H, 2 * P], F32, s2)
                sk = sb("sk", [P, S], F32, s2)
                sv = sb("sv", [P, NT, P], F32, s2)
                qn = sb("qn", [P, S], F32, s2)
                wp = sb("wp", [P, 2, 7 * P], F32, s2)
                wpt = sb("wpt", [P, 2, 7 * P], F32, s2)
                wst = sb("wst", [P, 2, 20], F32, s2)
            with ExitStack() as s2:
                dk = sb("dk", [P, RET_H, S], F32, s2)
                rq = sb("rq", [P, S], F32, s2)
                rk = sb("rk", [P, S], F32, s2)
                rv = sb("rv", [P, S], F32, s2)
                rgs = sb("rgs", [P, S], F32, s2)
                srt = sb("srt", [P, 2, S], F32, s2)
                ry = sb("ry", [P, S], F32, s2)
                ryc = sb("ryc", [P, S], F32, s2)
            with ExitStack() as s2:
                mg_hi = sb("mg_hi", [P, KT, S], F32R, s2)
                mg_lo = sb("mg_lo", [P, KT, S], F32R, s2)
        with ExitStack() as st:
            sb("over_xhid", [P, 4, XB], F32, st)
            ptr = sb("ptr", [P, 2, S], F32, st)
            ptr_hi = sb("ptr_hi", [P, 2, S], F32R, st)
            ptr_lo = sb("ptr_lo", [P, 2, S], F32R, st)
            ple = sb("ple", [P, KT, S], F32, st)
            pgs = sb("pgs", [P, 2, S], F32, st)

        q_dram = nc.dram_tensor("q_scratch", (HEADS, DQK, 2 * S), F32, kind="Internal").ap()
        c_dram = nc.dram_tensor("combine_scratch", (XITEMS * EPG, XB), F32, kind="Internal").ap()

        a_loaded = [sem(f"a_loaded{i}") for i in range(2)]
        b_loaded = [sem(f"b_loaded{i}") for i in range(2)]
        a_rounded, a_ready = sem("a_rounded"), sem("a_ready")
        b_rounded, b_ready = sem("b_rounded"), sem("b_ready")
        tile_ready, tile_free = sem("tile_ready"), sem("tile_free")
        y_ready, y_free = sem("y_ready"), sem("y_free")
        gate_done, hid_rounded, hid_ready = sem("gate_done"), sem("hid_rounded"), sem("hid_ready")
        params, consts, x_loaded = sem("params"), sem("consts"), sem("x_loaded")
        sq_ready, stat_mm, sd_ready = sem("sq_ready"), sem("stat_mm"), sem("sd_ready")
        hn_scaled, hn_rounded, hn_ready = sem("hn_scaled"), sem("hn_rounded"), sem("hn_ready")
        dve_step, act_step, dve_rstd, ple_mm = sem("dve_step"), sem("act_step"), sem("rstd_done"), sem("ple_mm")
        sp_exp, sp_one, sp_ln, sp_done = sem("sp_exp"), sem("sp_one"), sem("sp_ln"), sem("sp_done")
        xb_ready, yb_ready, xc_done, xc_rounded = sem("xb_ready"), sem("yb_ready"), sem("xc_done"), sem("xc_rounded")
        xc_ready, yb_copied, gx_done = sem("xc_ready"), sem("yb_copied"), sem("gx_done")
        gelu_done, decay_done, asq_done = sem("gelu_done"), sem("decay_done"), sem("asq_done")
        m2_done, mult_done, bx_done, scan_done, rec_done = (
            sem("m2_done"), sem("mult_done"), sem("bx_done"), sem("scan_done"), sem("rec_done"))
        rope_mm, rope_done = sem("rope_mm"), sem("rope_done")
        xl_done, xl_rounded, xl_ready, hidn_done, hidn_turned, chid_done, cmp_w2, cmp_done = (
            sem("xl_done"), sem("xl_rounded"), sem("xl_ready"), sem("hidn_done"), sem("hidn_turned"), sem("chid_done"),
            sem("cmp_w2"), sem("cmp_done"))
        gates_in, gates_done, narrow_copied = sem("gates_in"), sem("gates_done"), sem("narrow_copied")
        v_copied, v_turned, r_v = sem("v_copied"), sem("v_turned"), sem("r_v")
        q_stored = [sem(f"q_stored{i}") for i in range(2)]
        q_staged = [sem(f"q_staged{i}") for i in range(2)]
        v_staged, q_free = sem("v_staged"), sem("q_free")
        sc_ready, mx_done, exp_done, pm_ready, tr_ready, pt_ready = (
            sem("sc_ready"), sem("mx_done"), sem("exp_done"), sem("pm_ready"), sem("tr_ready"), sem("pt_ready"))
        csc_ready, csub_done, cexp_done, cpm_ready, ctr_ready, cpt_ready = (
            sem("csc_ready"), sem("csub_done"), sem("cexp_done"), sem("cpm_ready"), sem("ctr_ready"), sem("cpt_ready"))
        o_ready, o_rounded, o_split = sem("o_ready"), sem("o_rounded"), sem("o_split")
        rope_loaded, alibi_loaded, decay_loaded, p_loaded = (
            sem("rope_loaded"), sem("alibi_loaded"), sem("decay_loaded"), sem("p_loaded"))
        qk_raw, qk_sq, qk_mm, qk_sd, qk_norm = (
            sem("qk_raw"), sem("qk_sq"), sem("qk_mm"), sem("qk_sd"), sem("qk_norm"))
        w_sc, w_mx, w_exp, w_pm, w_tr, w_pt, w_o, w_or, w_os = (
            sem("w_sc"), sem("w_mx"), sem("w_exp"), sem("w_pm"), sem("w_tr"), sem("w_pt"), sem("w_o"),
            sem("w_o_rounded"), sem("w_o_split"))
        r_gate, r_sc, r_dec, r_o, r_y, r_mean, r_c, r_sq, r_var, r_sd, r_g, r_rounded, r_split = (
            sem("r_gate"), sem("r_sc"), sem("r_dec"), sem("r_o"), sem("r_y"), sem("r_mean"),
            sem("r_c"), sem("r_sq"), sem("r_var"), sem("r_sd"), sem("r_g"), sem("r_rounded"), sem("r_split"))
        mg_gate, mg_sum, mg_rounded, mg_ready = sem("mg_gate"), sem("mg_sum"), sem("mg_rounded"), sem("mg_ready")
        rt_exp, rt_in, wslot_done, wslot_stored, comb_loaded = (
            sem("rt_exp"), sem("rt_in"), sem("wslot_done"), sem("wslot_stored"), sem("comb_loaded"))
        ident_ready, marks_ready, rank_mm, groups_ready, nat_mm, nat_rounded, nat_ready = (
            sem("ident_ready"), sem("marks_ready"), sem("rank_mm"), sem("groups_ready"), sem("nat_mm"),
            sem("nat_rounded"), sem("nat_ready"))
        sel_ready, sel_t_ready, wide_ready, side_mm, side_free, x_rounded, xy_rounded, xy_ready, h_added = (
            sem("sel_ready"), sem("sel_t_ready"), sem("wide_ready"), sem("side_mm"), sem("side_free"),
            sem("x_rounded"), sem("xy_rounded"), sem("xy_ready"), sem("h_added"))
        p_rounded, p_ready, pg_done, out_done, stored = (
            sem("p_rounded"), sem("p_ready"), sem("pg_done"), sem("out_done"), sem("stored"))

        EARLY = [mg_sum, o_ready, r_g,
                 tr_ready, ctr_ready, mg_ready, pm_ready, r_o, r_rounded, w_tr, cpt_ready,
                 exp_done, o_split, pt_ready, r_dec, r_y, w_exp, w_os, w_pt, q_free, q_free]
        GATHER, SCATTER, side = {}, {}, 0
        for it in range(-1, XITEMS + 1):
            if it >= 1:
                SCATTER[it - 1] = side
                side += KT
            if it + 1 < XITEMS:
                GATHER[it + 1] = side
                side += KT // 2 + 1
        block = ctx.enter_context(nc.Block())
        ds = bass.ds

        @block.sync
        def _(sp):
            for x in EARLY:
                sp.sem_inc(x, 1)

            def load_a(s, i=0, panel=None):
                n = s + 2 * i
                panel = n if panel is None else panel
                if s >= 2 or not isinstance(i, int):
                    sp.wait_ge(a_ready, n - 1)
                sp.dma_start(a_raw[s % 2][:, :], w_a[ds(panel, 1)].rearrange("a p n -> p (a n)")) \
                  .then_inc(a_loaded[s % 2], 16)

            def load_b(s, i=0, panel=None):
                n = s + 2 * i
                panel = n if panel is None else panel
                if s >= 2 or not isinstance(i, int):
                    sp.wait_ge(b_ready, n - 1)
                sp.dma_start(b_raw[s % 2][:, :], w_b[ds(panel, 1)].rearrange("a p n -> p (a n)")) \
                  .then_inc(b_loaded[s % 2], 16)

            def stream(a, b, trips):
                with sp.Fori(0, trips) as i:
                    for u in range(2):
                        if a is not None:
                            load_a(a + u, i)
                        if b is not None:
                            load_b(b + u, i)

            for s in range(4):
                load_a(A_RNN + s)
            for u in range(2):
                load_b(B_RNN + u)
            with sp.Fori(1, RNN_BLOCKS // 2 - 1) as i:
                for u in range(2):
                    load_a(A_RNN + 2 + u, i)
                for u in range(2):
                    load_b(B_RNN + u, i)
            for u in range(2):
                load_b(B_RNN + RNN_BLOCKS - 2 + u)
            stream(A_FF0, B_FF0, FF_TILES // 2)
            stream(A_KCMP, None, (A_FF1 - A_KCMP) // 2)
            stream(A_FF1, B_FF1, FF_TILES // 2)
            load_a(A_SKV)
            stream(A_SQ, None, (A_MRG - A_SQ) // 2)
            stream(A_MRG, B_MRG, KT // 2)
            stream(A_OUT, None, 2)
            load_a(A_ROUTE)
            sp.wait_ge(groups_ready, 1)
            for it in range(XITEMS):
                g = sp.value_load(item_group[0:1, it:it + 1], min_val=0, max_val=EGROUPS - 1)
                with sp.Fori(0, EPG) as i:
                    for u in range(2):
                        pa = sp.snap(g * (2 * EPG) + i * 2 + (A_MOE + u))
                        load_a(A_MOE + 2 * EPG * it + u, i, pa)
                        pb = sp.snap(g * (2 * EPG) + i * 2 + (B_MOE + u))
                        load_b(B_MOE + 2 * EPG * it + u, i, pb)
            load_a(A_PLE, 0, A_PLE - REPEATED)
            with sp.Fori(0, 2) as i:
                for u in range(2):
                    load_a(A_PG + u, i, A_PG - REPEATED + u + 2 * i)

        @block.tensor
        def _(pe):
            def three(out, w_hi, w_lo, x_hi, x_lo, first, last):
                pe.matmul(out, w_hi, x_hi, start=first, stop=False)
                pe.matmul(out, w_hi, x_lo, start=False, stop=False)
                return pe.matmul(out, w_lo, x_hi, start=False, stop=last)

            def product(out, s, col, pitch, width, x_hi, x_lo, kt=KT, k0=0, rows=P, first=True, last=True):
                for k in range(kt):
                    c = col + k * pitch
                    m = three(out, a_hi[s % 2][0:rows, c:c + width], a_lo[s % 2][0:rows, c:c + width],
                              x_hi(k), x_lo(k), first and k == 0, last and k == kt - 1)
                return m

            def hh(k):
                return hn_hi[:, k, :]

            def hl(k):
                return hn_lo[:, k, :]

            def tile_bank(s, j, n):
                if s >= 2 or s + j >= 2:
                    pe.wait_ge(tile_free, 2 * n - 3 + j)
                return bank[2 * (s % 2) + j]

            def linear(s, i=0, width=P):
                n = s + 2 * i
                pe.wait_ge(a_ready, n + 1)
                for j in range(2):
                    b = tile_bank(s, j, n)
                    product(b[0:width, :], s, j * width, 2 * width, width, hh, hl).then_inc(tile_ready, 1)

            def linear_first(s, q, i=0, width=P):
                n = s + 2 * i
                pe.wait_ge(a_ready, n + 1)
                b = [tile_bank(s, j, n)[0:width, :] for j in range(2)]
                for k in range(KT):
                    pe.wait_ge(hn_ready, KT * q + k + 1)
                    for j in range(2):
                        c = (2 * k + j) * width
                        mm = three(b[j], a_hi[s % 2][:, c:c + width], a_lo[s % 2][:, c:c + width], hh(k), hl(k),
                                   k == 0, k == KT - 1)
                        if k == KT - 1:
                            mm.then_inc(tile_ready, 1)

            def narrow(s, q, width):
                pe.wait_ge(a_ready, s + 1)
                b = tile_bank(s, 0, s)
                for k in range(KT):
                    pe.wait_ge(hn_ready, KT * q + k + 1)
                    mm = three(b[0:width, :], a_hi[s % 2][:, k * width:(k + 1) * width],
                               a_lo[s % 2][:, k * width:(k + 1) * width], hh(k), hl(k), k == 0, k == KT - 1)
                mm.then_inc(tile_ready, 1)

            def narrow_turned(s, c, width):
                b = tile_bank(s, 1, s)
                pe.wait_ge(narrow_copied, c)
                for t in range(NT):
                    mm = pe.transpose(b[:, t * width:(t + 1) * width], sd[0:width, t * P:(t + 1) * P],
                                      ident[0:width, 0:width])
                mm.then_inc(tile_ready, 1)

            def turn_v(b, src, c):
                pe.wait_ge(v_copied, c)
                for t in range(NT):
                    mm = pe.transpose(b[:, t * P:(t + 1) * P], src[:, t * P:(t + 1) * P], ident)
                mm.then_inc(v_turned, 1)

            def norm_stats(q, ready, width=KT):
                ready(pe)
                for m in range(width):
                    pe.wait_ge(sq_ready, KT * q + m + 1)
                    pe.matmul(bank[4][:, :], ones, sq[:, m % 2, :], start=m == 0, stop=m == width - 1) \
                      .then_inc(stat_mm, 1)

            def down(sb_, e, i, x_hi, x_lo, rows):
                for hb in range(2):
                    s = sb_ + hb
                    n = s + 2 * i
                    pe.wait_ge(b_ready, n + 1)
                    for f in range(2):
                        if hb == 0:
                            pe.wait_ge(hid_ready, 2 * (e + i) + f + 1)
                        for m in range(4):
                            if f == 0:
                                pe.wait_ge(y_free, 4 * n + m - 3)
                            c = slice(f * 512 + m * P, f * 512 + (m + 1) * P)
                            mm = three(bank[4 + m][:, :], b_hi[s % 2][0:rows, c], b_lo[s % 2][0:rows, c],
                                       x_hi[0:rows, f, :], x_lo[0:rows, f, :], f == 0, f == 1)
                            if f == 1:
                                mm.then_inc(y_ready, 1)

            def hh_first(k):
                pe.wait_ge(hn_ready, KT * N_MIX0 + k + 1)
                return hh(k)

            def rnn_pair(i, peeled):
                for u in range(2):
                    n = 2 * i + u
                    pe.wait_ge(a_ready, n + 1)
                    for j, done in ((0, xb_ready), (1, yb_ready)):
                        if not peeled:
                            pe.wait_ge(tile_free, 2 * n - 3 + j)
                        product(bank[2 * u + j][0:RNN_W, :], u, j * RNN_W, 2 * RNN_W, RNN_W,
                                hh_first if peeled and u == 0 and j == 0 else hh, hl).then_inc(done, 1)
                        if u == 1 and j == 0 and not peeled:
                            rnn_down(i)
                    for j in range(2):
                        pe.wait_ge(xc_ready if j == 0 else yb_copied, n + 1)
                        product(bank[2 * u + j][0:RNN_W, :], u, 8 * 192 + j * RNN_W, 0, RNN_W,
                                lambda k: xc_hi[:, u, :], lambda k: xc_lo[:, u, :], kt=1, rows=RNN_W) \
                            .then_inc(tile_ready, 1)

            def rnn_down(i):
                for hb in range(2):
                    n = 2 * i - 2 + hb
                    pe.wait_ge(b_ready, n + 1)
                    for f in range(2):
                        if hb == 0:
                            pe.wait_ge(hid_ready, 2 * i - 2 + f + 1)
                        for m in range(4):
                            if f == 0 and hb:
                                pe.wait_ge(y_free, 4 * n + m - 3)
                            c = slice(f * 512 + m * P, f * 512 + (m + 1) * P)
                            mm = three(bank[4 + m][:, :], b_hi[hb][0:RNN_W, c], b_lo[hb][0:RNN_W, c],
                                       rhid_hi[0:RNN_W, f, :], rhid_lo[0:RNN_W, f, :], f == 0, f == 1)
                            if f == 1:
                                mm.then_inc(y_ready, 1)

            pe.wait_ge(consts, 16)
            norm_stats(N_MIX0, lambda e: None)
            rnn_pair(0, True)
            with pe.Fori(1, RNN_BLOCKS // 2) as i:
                rnn_pair(i, False)
            rnn_down(RNN_BLOCKS // 2)

            def ffn(sa, sb_, e, trips, q):
                with pe.Fori(0, trips) as i:
                    linear_first(sa, q, i)
                    linear(sa + 1, i)
                    down(sb_, e, i, hid_hi, hid_lo, P)

            def y_all(n_b):
                return lambda e: e.wait_ge(y_free, 4 * n_b)

            norm_stats(N_FFN0, y_all(B_FF0))
            ffn(A_FF0, B_FF0, E_FF0, FF_TILES // 2, N_FFN0)

            norm_stats(N_KV, y_all(B_FF1))
            linear_first(A_KCMP, N_KV, width=DQK)
            linear(A_KCMP + 1, width=DQK)
            linear(A_VCMP)

            def rope_mm_(r, src):
                if r >= 2:
                    pe.wait_ge(rope_done, r - 1)
                pe.matmul(bank[4 + r % 2][0:DQK, :], rot, src, start=True, stop=True).then_inc(rope_mm, 1)

            for b in range(2):
                for p in range(2):
                    s = A_KSEL + 2 * b + p
                    linear(s, width=DQK)
                    for j in range(2):
                        pe.wait_ge(tile_free, 2 * s + j + 1)
                        rope_mm_(4 * b + 2 * p + j, kx[:, b, 2 * p + j, :])
            for b in range(2):
                s = A_VNAT + b
                pe.wait_ge(a_ready, s + 1)
                for j in range(2):
                    bk = tile_bank(s, j, s)
                    for t in range(2):
                        c = slice((2 * j + t) * P, (2 * j + t + 1) * P)
                        for k in range(KT):
                            w = slice(k * 256, (k + 1) * 256)
                            m = three(bk[:, t * 256:(t + 1) * 256], hn_hi[:, k, c], hn_lo[:, k, c],
                                      a_hi[s % 2][:, w], a_lo[s % 2][:, w], k == 0, k == KT - 1)
                    m.then_inc(tile_ready, 1)
            def compress(b, p):
                s, rows = (A_W1K, A_W1V)[b] + p, (DQK, DV)[b]
                pe.wait_ge(a_ready, s + 1)
                pe.wait_ge(xl_ready, 2 * b + p // 2 + 1)
                first = 0 if p >= 2 else GROUPS * S
                x_hi = hn_hi[0:rows, :, :].rearrange("p k s -> p (k s)")
                x_lo = hn_lo[0:rows, :, :].rearrange("p k s -> p (k s)")
                for l in range(8):
                    t0 = first + 8 * p + l
                    t = slice(t0, t0 + CSTRIDE * (P - 1) + 1, CSTRIDE)
                    c = slice(l * 256, (l + 1) * 256)
                    mm = three(bank[6 - 2 * b][:, 0:256], x_hi[:, t], x_lo[:, t],
                               a_hi[s % 2][0:rows, c], a_lo[s % 2][0:rows, c], p == 0 and l == 0, p == 3 and l == 7)
                mm.then_inc(tile_ready, 2)

            def turn_hidden(b):
                pe.wait_ge(hidn_done, b + 1)
                for m in range(2):
                    mm = pe.transpose(bank[7 - 2 * b][:, m * P:(m + 1) * P], hidn[:, m * P:(m + 1) * P], ident)
                mm.then_inc(hidn_turned, 1)

            for p in range(4):
                compress(0, p)
            pe.wait_ge(rope_done, 8)
            compress(1, 0)
            turn_hidden(0)
            compress(1, 1)
            pe.wait_ge(chid_done, 1)
            for m in range(2):
                mm = pe.matmul(bank[6][0:DQK, 0:P], smc("w2k", m * DQK, DQK), chid[:, m, :],
                               start=m == 0, stop=m == 1)
            mm.then_inc(cmp_w2, 1)
            compress(1, 2)
            compress(1, 3)

            pe.sem_inc(stat_mm, KT)
            narrow(A_GATE, N_MIX1, NGATE)
            turn_hidden(1)
            narrow_turned(A_GATE, 1, NGATE)
            pe.wait_ge(chid_done, 2)
            for g in range(GROUPS):
                for m in range(2):
                    mm = pe.matmul(bank[7][0:NCMP, g * DV:(g + 1) * DV], chid[:, m, g * 32:g * 32 + NCMP],
                                   smc("w2v", m * DV, DV), start=m == 0, stop=m == 1)
            mm.then_inc(cmp_w2, 1)
            with pe.Fori(0, HEADS // 4) as i:
                for u in range(2):
                    s = A_Q + u
                    linear(s, i, width=DQK)
                    for j in range(2):
                        v = 2 * u + j
                        pe.wait_ge(tile_free, 2 * (s + 2 * i) + j + 1)
                        pe.wait_ge(rope_done, 8 + 4 * i + v - 1)
                        pe.matmul(bank[4 + v % 2][0:DQK, :], rot, qb[:, v, 0, :], start=True, stop=True) \
                          .then_inc(rope_mm, 1)

            pe.wait_ge(rope_done, 8 + HEADS)
            pe.wait_ge(tile_free, 2 * A_WO)
            pe.wait_ge(cmp_done, 2)
            with pe.Fori(0, GROUPS) as g:
                def scores_c(u):
                    hd = HPG * g + u
                    pe.wait_ge(q_staged[u % 2], 32 * g + 16 * (u // 2) + 16)
                    pe.wait_ge(cpt_ready, 1 + hd)
                    for t in range(NT):
                        mm = pe.matmul(bank[6][:, t * NCMP:(t + 1) * NCMP], qs[:, u % 2, 0, t * P:(t + 1) * P],
                                       kct[:, ds(g * NCMP, NCMP)], start=True, stop=True)
                    mm.then_inc(csc_ready, 1)

                def scores(u, t):
                    hd = HPG * g + u
                    n = (t + 1) * P
                    pe.wait_ge(exp_done, 1 + 4 * hd + t - 1 if t >= 2 else 1 + 4 * hd)
                    for b in range(2):
                        bk = bank[2 * (t % 2) + b]
                        pe.matmul(bk[:, 0:n], qs[:, u % 2, 1, t * P:(t + 1) * P],
                                  kx[:, b, ds(g, 1), 0:n].rearrange("p a s -> p (a s)"), start=True, stop=False)
                        mm = pe.matmul(bk[:, t * P:n], masks[:, 0, :], masks[:, 1, :], start=False, stop=True)
                    mm.then_inc(sc_ready, 1)

                def turn(u, t):
                    x = 8 * (HPG * g + u) + 2 * t
                    pe.wait_ge(pm_ready, 1 + 4 * (HPG * g + u) + t + 1)
                    for b in range(2):
                        pe.wait_ge(pt_ready, 1 + x + b - 1 if t or b else 1 + x)
                        for j in range(t + 1):
                            mm = pe.transpose(bank[4 + b][:, j * P:(j + 1) * P],
                                              pm[:, t % 2, b, j * P:(j + 1) * P], ident)
                        mm.then_inc(tr_ready, 1)

                def outputs(u, t):
                    hd = HPG * g + u
                    r0 = DV * (u % 2)
                    if t == 0:
                        if u == 0:
                            pe.wait_ge(v_staged, 3 * g + 3)
                        if u % 2 == 0:
                            pe.wait_ge(o_split, 1 + 2 * g + u // 2)
                        pe.wait_ge(cpt_ready, 1 + hd + 1)
                    pe.wait_ge(pt_ready, 1 + 8 * hd + 2 * t + 2)
                    c = slice(t * P, (t + 1) * P)
                    o = bank[7][r0:r0 + DV, c]
                    for b in range(2):
                        for j in range(t + 1):
                            pe.matmul(o, vs[:, b, j, :], pt[:, b, j, c], start=b == 0 and j == 0, stop=False)
                    mm = pe.matmul(o, vcs[:, :], ptc[:, c], start=False, stop=True)
                    if t == NT - 1:
                        mm.then_inc(o_ready, 1)

                scores_c(0)
                scores(0, 0)
                scores(0, 1)
                for u in range(HPG):
                    hd = HPG * g + u
                    for t in range(NT):
                        if t + 2 < NT:
                            scores(u, t + 2)
                        turn(u, t)
                        if t == 1:
                            pe.wait_ge(cpm_ready, hd + 1)
                            for c in range(NT):
                                mm = pe.transpose(bank[6][0:NCMP, c * P:(c + 1) * P], pc[:, c, :], ident)
                            mm.then_inc(ctr_ready, 1)
                        if t == 2:
                            outputs(u, 0)
                            outputs(u, 1)
                    if u + 1 < HPG:
                        scores_c(u + 1)
                        scores(u + 1, 0)
                        scores(u + 1, 1)
                    outputs(u, 2)
                    outputs(u, 3)

            pe.wait_ge(o_split, 1 + HEADS // 2)
            with pe.Fori(0, 2) as i:
                linear(A_WO, i)
                linear(A_WO + 1, i)

            norm_stats(N_FFN1, lambda e: None)
            ffn(A_FF1, B_FF1, E_FF1, FF_TILES // 2, N_FFN1)
            norm_stats(N_FINAL, y_all(B_MRG))
            norm_stats(N_MIX2, lambda e: None)

            s = A_SKV
            pe.wait_ge(a_ready, s + 1)
            b = tile_bank(s, 0, s)

            def hh_split(k):
                pe.wait_ge(hn_ready, KT * N_MIX2 + k + 1)
                return hh(k)

            product(b[:, :], s, 0, 2 * P, P, hh_split, hl).then_inc(tile_ready, 1)
            b = tile_bank(s, 1, s)
            product(b[:, :], s, P, 2 * P, P, hh, hl).then_inc(tile_ready, 1)
            pe.wait_ge(qk_sq, 1)
            pe.matmul(bank[4][:, :], halves, sq[:, 0, :], start=True, stop=True).then_inc(qk_mm, 1)
            turn_v(b, tmp[:, 1, :], 1)

            def query_w(m):
                s = A_SQ + m
                pe.wait_ge(a_ready, s + 1)
                b = tile_bank(s, 0, s)
                product(b[:, :], s, 0, 2 * P, P, hh, hl).then_inc(tile_ready, 2)
                pe.wait_ge(qk_sq, m + 2)
                pe.matmul(bank[1][:, :], halves, sq[:, m % 2, :], start=True, stop=True).then_inc(qk_mm, 1)

            def scores_w(m, half):
                r = slice(64 * half, 64 * half + 64)
                if m or half:
                    pe.wait_ge(w_mx, 2 * m + half)
                for (t, k0, w, c) in WIN:
                    mm = pe.matmul(bank[4 + c // S][:, c % S:c % S + w], qn[r, t * P:(t + 1) * P],
                                   sk[r, k0:k0 + w], start=True, stop=True)
                mm.then_inc(w_sc, 1)

            def out_w(m, half):
                r = slice(64 * half, 64 * half + 64)
                it = 2 * m + half
                pe.wait_ge(w_pm, it + 1)
                pe.wait_ge(w_pt, 1 + it)
                for j in range(7):
                    mm = pe.transpose(bank[6 + j // 4][:, j % 4 * P:(j % 4 + 1) * P],
                                      wp[:, half, j * P:(j + 1) * P], ident)
                mm.then_inc(w_tr, 1)
                pe.wait_ge(w_pt, 1 + it + 1)
                if half == 0:
                    pe.wait_ge(w_os, 1 + m)
                for (t, k0, w, c) in WIN:
                    for j in range(w // P):
                        mm = pe.matmul(bank[3][r, t * P:(t + 1) * P], sv[:, k0 // P + j, r],
                                       wpt[:, half, c + j * P:c + (j + 1) * P], start=j == 0, stop=j == w // P - 1)
                if half:
                    mm.then_inc(w_o, 1)

            query_w(0)
            for m in range(SWA_TILES):
                if m + 1 < SWA_TILES:
                    query_w(m + 1)
                pe.wait_ge(qk_norm, m + 2)
                scores_w(m, 0)
                scores_w(m, 1)
                out_w(m, 0)
                out_w(m, 1)

            pe.wait_ge(w_os, 1 + SWA_TILES)
            with pe.Fori(0, RET_H) as i:
                pe.wait_ge(a_ready, A_RET + 2 * i + 1)
                for j in range(2):
                    b = tile_bank(A_RET, j, A_RET + 2 * i)
                    product(b[:, :], A_RET, j * P, 2 * P, P, hh, hl).then_inc(tile_ready, 1)
                pe.wait_ge(a_ready, A_RET + 2 * i + 2)
                for j in (1, 0):
                    b = tile_bank(A_RET + 1, j, A_RET + 1 + 2 * i)
                    product(b[:, :], A_RET + 1, j * P, 2 * P, P, hh, hl).then_inc(tile_ready, 1)
                pe.wait_ge(tile_free, 2 * (A_RET + 1 + 2 * i))

                def scores_r(j):
                    pe.wait_ge(r_dec, 1 + 4 * i + max(j - 1, 0))
                    pe.matmul(bank[4 + j % 2][:, 0:S - j * P], rk[:, j * P:(j + 1) * P], rq[:, j * P:S],
                              start=True, stop=True).then_inc(r_sc, 1)

                def out_r(j):
                    pe.wait_ge(r_dec, 1 + 4 * i + j + 1)
                    if j == 0:
                        pe.wait_ge(r_y, 1 + i)
                    mm = pe.matmul(bank[6][:, j * P:S], rv[:, j * P:(j + 1) * P], srt[:, j % 2, 0:S - j * P],
                                   start=j == 0, stop=j == 3)
                    mm.then_inc(r_o, 1)

                scores_r(0)
                scores_r(1)
                turn_v(bank[2 * ((A_RET + 1) % 2) + 1], tmp[:, 0, :], 2 + i)
                pe.wait_ge(r_v, i + 1)
                out_r(0)
                scores_r(2)
                out_r(1)
                scores_r(3)
                out_r(2)
                out_r(3)
                pe.wait_ge(r_y, 1 + i + 1)
                pe.matmul(bank[7][:, :], ones, ry[:, :], start=True, stop=True).then_inc(r_mean, 1)
                pe.wait_ge(r_sq, i + 1)
                pe.matmul(bank[7][:, :], ones, sq[:, 0, :], start=True, stop=True).then_inc(r_var, 1)

            pe.wait_ge(r_split, RET_H)
            with pe.Fori(0, KT // 2) as i:
                for u in range(2):
                    linear(A_MRG + u, i)
                    s = B_MRG + u
                    n = s + 2 * i
                    pe.wait_ge(b_ready, n + 1)
                    pe.wait_ge(y_free, 4 * n - 4)
                    for j, (yh, yl) in enumerate(((yr_hi, yr_lo), (ys_hi, ys_lo))):
                        for k in range(4):
                            c = slice(j * 512 + k * P, j * 512 + (k + 1) * P)
                            mm = three(bank[4 + 2 * u + j][:, :], b_hi[s % 2][:, c], b_lo[s % 2][:, c],
                                       yh[:, k, :], yl[:, k, :], k == 0, k == 3)
                        mm.then_inc(y_ready, 2)

            pe.wait_ge(mg_ready, 1 + KT)
            with pe.Fori(0, 2) as i:
                for u in range(2):
                    s = A_OUT + u
                    n = s + 2 * i
                    pe.wait_ge(a_ready, n + 1)
                    for j in range(2):
                        b = tile_bank(s, j, n)
                        product(b[:, :], s, j * P, 2 * P, P, lambda k: mg_hi[:, k, :], lambda k: mg_lo[:, k, :]) \
                            .then_inc(tile_ready, 1)

            norm_stats(N_MOE, y_all(B_MOE))
            narrow(A_ROUTE, N_MOE, NROUTE)
            narrow_turned(A_ROUTE, 2, NROUTE)

            def turn_tokens(c):
                t, f = c // 2, c % 2
                if c >= 4:
                    pe.wait_ge(nat_ready, c - 3)
                for k in range(4):
                    o = bank[4 + c % 4][:, k * P:(k + 1) * P]
                    pe.matmul(o, hn_hi[:, 4 * f + k, t * P:(t + 1) * P], ident_r[:, :], start=True, stop=False)
                    mm = pe.matmul(o, hn_lo[:, 4 * f + k, t * P:(t + 1) * P], ident_r[:, :],
                                   start=False, stop=True)
                mm.then_inc(nat_mm, 1)

            pe.wait_ge(ident_ready, 1)
            for c in range(4):
                turn_tokens(c)
            pe.wait_ge(marks_ready, 1)
            for t in range(NT + 1):
                for u in range(min(t + 1, NT)):
                    mm = pe.matmul(bank[3][:, t * EGROUPS:(t + 1) * EGROUPS], cnc("upto", P) if u == t else ones,
                                   rtg[:, 2, u, :], start=u == 0, stop=u == min(t, NT - 1))
            mm.then_inc(rank_mm, 1)
            for c in range(4, 8):
                turn_tokens(c)

            def side_bank(k):
                if k >= 2:
                    pe.wait_ge(side_free, k - 1)
                return bank[2 + k % 2]

            def gather(it):
                pe.wait_ge(sel_ready, it + 1)
                for c in range(KT // 2):
                    b = side_bank(GATHER[it] + c)
                    for f in range(2):
                        cols = slice((2 * c + f) * P, (2 * c + f + 1) * P)
                        for t in range(NT):
                            for part in (nat_hi, nat_lo):
                                mm = pe.matmul(b[:, f * XB:(f + 1) * XB], part[:, t, cols], sel[:, t, :],
                                               start=t == 0 and part is nat_hi, stop=t == NT - 1 and part is nat_lo)
                    mm.then_inc(side_mm, 1)
                b = side_bank(GATHER[it] + KT // 2)
                for t in range(NT):
                    for part in (w_hi, w_lo):
                        mm = pe.matmul(b[0:EPG, 0:XB], part[:, t, :], sel[:, t, :],
                                       start=t == 0 and part is w_hi, stop=t == NT - 1 and part is w_lo)
                mm.then_inc(side_mm, 1)

            def scatter(it):
                pe.wait_ge(sel_t_ready, it + 1)
                pe.wait_ge(xy_ready, 4 * it + 4)
                for m in range(KT):
                    b = side_bank(SCATTER[it] + m)
                    for u in range(XSUB):
                        for part in (xy_hi, xy_lo):
                            mm = pe.matmul(b[:, :], part[:, u, m * P:(m + 1) * P], sel_t[:, u, :],
                                           start=u == 0 and part is xy_hi, stop=u == XSUB - 1 and part is xy_lo)
                    mm.then_inc(side_mm, 1)

            def expert(it, i, first=False, last=False):
                x = slice((it % 2) * XB, (it % 2 + 1) * XB)
                for f in range(2):
                    s = A_MOE + 2 * EPG * it + f
                    n = s + 2 * i
                    pe.wait_ge(a_ready, n + 1)
                    for j in range(2):
                        pe.wait_ge(tile_free, 2 * n - 3 + j)
                        product(bank[s % 2][:, j * XB:(j + 1) * XB], s, j * P, 2 * P, P,
                                lambda k: hn_hi[:, k, x], lambda k: hn_lo[:, k, x]).then_inc(tile_ready, 1)
                for f in range(2):
                    pe.wait_ge(hid_ready, 2 * (E_MOE + EPG * it + i) + f + 1)
                    for hb in range(2):
                        s = B_MOE + 2 * EPG * it + hb
                        n = s + 2 * i
                        if f == 0:
                            pe.wait_ge(b_ready, n + 1)
                        for u in range(XSUB):
                            if first and f == 0 and it:
                                pe.wait_ge(xy_ready, 4 * it)
                            c = slice(u * P, (u + 1) * P)
                            mm = three(bank[4 + 2 * u + hb][:, :], xhid_hi[:, f, c], xhid_lo[:, f, c],
                                       b_hi[s % 2][:, f * 512:(f + 1) * 512], b_lo[s % 2][:, f * 512:(f + 1) * 512],
                                       first and f == 0, last and f == 1)
                            if f == 1:
                                mm.then_inc(y_ready, 2)

            pe.wait_ge(nat_ready, 2 * NT)
            gather(0)
            pe.wait_ge(wide_ready, 1)
            pe.wait_ge(side_free, GATHER[0] + KT // 2 + 1)
            for t in range(NT):
                mm = pe.matmul(bank[2][:, t * P:(t + 1) * P], slot_wide[:, t * P:(t + 1) * P], ident,
                               start=True, stop=True)
            mm.then_inc(rank_mm, 1)
            for it in range(XITEMS):
                pe.wait_ge(side_free, GATHER[it] + KT // 2)
                expert(it, 0, first=True)
                if it == 0:
                    pe.wait_ge(wide_ready, 2)
                else:
                    scatter(it - 1)
                if it + 1 < XITEMS:
                    gather(it + 1)
                with pe.Fori(1, EPG - 1) as i:
                    expert(it, i)
                expert(it, EPG - 1, last=True)
            scatter(XITEMS - 1)

            s = A_PLE
            pe.wait_ge(a_ready, s + 1)
            pe.wait_ge(p_ready, 1)
            for m in range(KT):
                if m >= 2:
                    pe.wait_ge(pg_done, m - 1)
                mm = product(bank[5 + m % 2][:, :], s, m * P, D, P, lambda k: ptr_hi[:, k, :],
                             lambda k: ptr_lo[:, k, :], kt=2)
                mm.then_inc(ple_mm, 1)
            pe.wait_ge(pg_done, KT)
            pe.sem_inc(tile_ready, 2)
            norm_stats(N_PLE, lambda e: None)
            norm_stats(N_PLEG, lambda e: e.wait_ge(sd_ready, N_PLE + 1))
            linear_first(A_PG, N_PLEG)
            for p in range(1, 4):
                linear(A_PG + p)

        @block.scalar
        def _(act):
            step = Steps(act, act_step)

            def high_a(s, i=0):
                n = s + 2 * i
                act.wait_ge(a_loaded[s % 2], 16 * (s // 2 + i) + 16)
                if s >= 2 or not isinstance(i, int):
                    act.wait_ge(tile_ready, 2 * n - 2)
                act.activation(a_hi[s % 2][:, :], a_raw[s % 2][:, :], ACT.Copy).then_inc(a_rounded, 1)

            def high_b(s, i=0):
                n = s + 2 * i
                act.wait_ge(b_loaded[s % 2], 16 * (s // 2 + i) + 16)
                if s >= 1:
                    act.wait_ge(y_ready, 4 * n - 4)
                act.activation(b_hi[s % 2][:, :], b_raw[s % 2][:, :], ACT.Copy).then_inc(b_rounded, 1)

            def squares(q, ready):
                act.activation(warm[:, q:q + 1], eps, ACT.Sqrt)
                for m in range(KT):
                    ready(act, m)
                    if m >= 2:
                        act.wait_ge(stat_mm, KT * q + m - 1)
                    act.activation(sq[:, m % 2, :], h[:, m, :], ACT.Square).then_inc(sq_ready, 1)

            def root(q, n=KT):
                act.wait_ge(stat_mm, KT * (q + 1))
                if q:
                    act.wait_ge(dve_rstd, q)
                act.activation(sd[:, :], bank[4][:, :], ACT.Sqrt, bias=eps, scale=1.0 / D).then_inc(sd_ready, 1)

            def high_hn(q):
                for m in range(KT):
                    act.wait_ge(hn_scaled, KT * q + m + 1)
                    act.activation(hn_hi[:, m, :], tmp[:, m % 2, :], ACT.Copy).then_inc(hn_rounded, 1)

            act.dma_start(cn[:, :], const).then_inc(consts, 16)
            act.dma_start(h[:, :, :], x_t.rearrange("(k p) s -> p k s", p=P)).then_inc(x_loaded, 16)
            act.dma_start(sm[:, :], small).then_inc(params, 16)
            act.wait_ge(consts, 16)
            squares(N_MIX0, lambda e, m: e.wait_ge(x_loaded, 16))
            root(N_MIX0)
            high_a(A_RNN)
            high_hn(N_MIX0)

            act.wait_ge(params, 16)
            lam = smc("lam", 0, RNN_BLOCKS, RNN_W)
            step(act.activation(spt[:, 0, :], lam, ACT.Abs))
            act.activation(spt[:, 1, :], spt[:, 0, :], ACT.Exp, scale=-1.0).then_inc(sp_exp, 1)
            act.wait_ge(sp_one, 1)
            act.activation(spt[:, 3, :], spt[:, 2, :], ACT.Ln).then_inc(sp_ln, 1)
            act.wait_ge(sp_done, 1)

            def decays(u, i):
                n = 2 * i + u
                act.wait_ge(tile_free, 2 * n + 2)
                act.activation(aa[:, u, :], rg[:, u, :], ACT.Exp, scale=spt[:, 7, ds(n, 1)]).then_inc(decay_done, 1)
                act.activation(pp[:, u, :], rg[:, u, :], ACT.Tanh, scale=spt[:, 6, ds(n, 1)]).then_inc(decay_done, 1)

            def multiplier(u, i):
                act.wait_ge(m2_done, 2 * i + u + 1)
                act.activation(mu[:, u, :], pp[:, u, :], ACT.Sqrt).then_inc(mult_done, 1)

            def branch(u, i):
                act.wait_ge(yb_copied, 2 * i + u + 1)
                act.activation(gel[:, u, :], ybr[:, u, :], ACT.Gelu_apprx_tanh).then_inc(gelu_done, 1)

            def high_rnn(u, i, used=None):
                act.wait_ge(rec_done, 2 * i + u + 1)
                if used is not None:
                    act.wait_ge(y_ready, used)
                act.activation(rhid_hi[0:RNN_W, u, :], hs[:, u, :], ACT.Copy).then_inc(hid_rounded, 1)

            def high_rnn_b(i):
                for u in range(2):
                    act.wait_ge(b_loaded[u], 16 * i)
                    act.activation(b_hi[u][:, :], b_raw[u][:, :], ACT.Copy).then_inc(b_rounded, 1)

            def channel(u, i, last=None, peeled=False):
                n = 2 * i + u
                high_a(A_RNN + 1 + u, i)
                if last:
                    decays(*last)
                    multiplier(*last)
                act.wait_ge(xc_done, n + 1)
                act.activation(xc_hi[:, u, :], xc[:, u, :], ACT.Copy).then_inc(xc_rounded, 1)
                if last:
                    branch(*last)
                if u == 0 and not peeled:
                    high_rnn_b(i)
                if last:
                    high_rnn(*last, used=8 * i if u and not peeled else None)
                for j, (dst, bias) in enumerate(((rg, "b_ra"), (ig, "b_ix"))):
                    act.wait_ge(tile_ready, 2 * n + j + 1)
                    act.activation(dst[:, u, :], bank[2 * u + j][0:RNN_W, :], ACT.Sigmoid,
                                   bias=sm[0:RNN_W, ds(SM[bias] + n, 1)]).then_inc(tile_free, 1)

            channel(0, 0, peeled=True)
            channel(1, 0, (0, 0), peeled=True)
            with act.Fori(1, RNN_BLOCKS // 2) as i:
                channel(0, i, (1, i - 1))
                channel(1, i, (0, i))
            last = (1, RNN_BLOCKS // 2 - 1)
            decays(*last)
            high_rnn_b(RNN_BLOCKS // 2)
            multiplier(*last)
            branch(*last)
            high_rnn(*last)

            def ffn_pair(sa, sb_, e, i):
                for f in range(2):
                    n = sa + f + 2 * i
                    high_a(sa + f + 1, i)
                    high_b(sb_ + f, i)
                    act.wait_ge(tile_ready, 2 * n + 1)
                    act.activation(sg[:, f, :], bank[2 * ((sa + f) % 2)][:, :], ACT.Silu).then_inc(gate_done, 1)
                    act.wait_ge(tile_free, 2 * n + 2)
                    act.activation(hid_hi[:, f, :], hid[:, f, :], ACT.Copy).then_inc(hid_rounded, 1)

            def ffn(sa, sb_, e, trips):
                with act.Fori(0, trips) as i:
                    ffn_pair(sa, sb_, e, i)

            def y_is(nb):
                return lambda e, m: e.wait_ge(y_free, 4 * nb - KT + m + 1)

            squares(N_FFN0, y_is(B_FF0))
            root(N_FFN0)
            high_hn(N_FFN0)
            ffn(A_FF0, B_FF0, E_FF0, FF_TILES // 2)

            squares(N_KV, y_is(B_FF1))
            root(N_KV)
            high_hn(N_KV)
            for s in range(A_KCMP, A_W1K):
                high_a(s + 1)
            def high_pos(ph):
                act.wait_ge(xl_done, ph + 1)
                rows, half = (DQK, DV)[ph // 2], 4 - 4 * (ph % 2)
                act.activation(hn_hi[0:rows, half:half + 4, :], xpos[0:rows, :, :], ACT.Copy).then_inc(xl_rounded, 1)

            def gelu_hidden(b):
                act.wait_ge(tile_ready, 2 * (A_W1K + 4 * b + 4))
                if b == 1:
                    act.wait_ge(hidn_turned, 1)
                act.activation(hidn[:, :], bank[6 - 2 * b][:, 0:256], ACT.Gelu_apprx_tanh).then_inc(hidn_done, 1)

            def copy_hidden(b):
                act.wait_ge(hidn_turned, b + 1)
                if b == 1:
                    act.wait_ge(cmp_w2, 1)
                act.activation(chid[:, :, :], bank[7 - 2 * b][:, 0:256].rearrange("p (m c) -> p m c", m=2), ACT.Copy) \
                   .then_inc(chid_done, 1)

            high_pos(0)
            for ph in range(4):
                high_a(A_W1K + 2 * ph + 1)
                if ph < 3:
                    high_pos(ph + 1)
                if ph == 2:
                    gelu_hidden(0)
                high_a(A_W1K + 2 * ph + 2)
                if ph == 2:
                    copy_hidden(0)
            gelu_hidden(1)
            act.sem_inc(sq_ready, KT)
            act.sem_inc(sd_ready, 1)
            high_hn(N_MIX1)
            copy_hidden(1)
            high_a(A_GATE + 1)
            act.wait_ge(gates_in, 1)
            act.activation(gates[:, :, :], gates[:, :, :], ACT.Sigmoid).then_inc(gates_done, 1)
            with act.Fori(0, HEADS // 4) as i:
                for u in range(2):
                    high_a(A_Q + u + 1, i)

            for u in range(2):
                act.wait_ge(q_stored[u], 16 * (HEADS // 4))
            with act.Fori(0, GROUPS) as g:
                def high_out(pair):
                    act.wait_ge(o_ready, 1 + HPG * g + 2 * pair + 2)
                    act.activation(hn_hi[:, ds(2 * g + pair, 1), :].rearrange("p a s -> p (a s)"),
                                   bank[7][:, :], ACT.Copy).then_inc(o_rounded, 1)

                for u in range(HPG):
                    hd = HPG * g + u

                    def expo(t):
                        n = (t + 1) * P
                        act.wait_ge(mx_done, 4 * hd + t + 1)
                        act.wait_ge(tr_ready, 1 + 8 * hd + 2 * t - 2 if t >= 2 else 1 + 8 * hd)
                        for b in range(2):
                            e = act.activation(pm[:, t % 2, b, 0:n], bank[2 * (t % 2) + b][:, 0:n], ACT.Exp,
                                               bias=ast[:, t % 2, b:b + 1], accum_out=ast[:, t % 2, 2 + b:3 + b])
                        e.then_inc(exp_done, 1)

                    expo(0)
                    expo(1)
                    if u == 2:
                        high_out(0)
                    act.wait_ge(csub_done, hd + 1)
                    act.activation(pc[:, :, :], pc[:, :, :], ACT.Exp).then_inc(cexp_done, 1)
                    for t in range(NT):
                        if t + 2 < NT:
                            expo(t + 2)
                        for b in range(2):
                            act.wait_ge(tr_ready, 1 + 8 * hd + 2 * t + b + 1)
                            act.activation(pt[:, b, 0:t + 1, t * P:(t + 1) * P],
                                           bank[4 + b][:, 0:(t + 1) * P].rearrange("p (j c) -> p j c", c=P),
                                           ACT.Copy).then_inc(pt_ready, 1)
                        if t == 1:
                            act.wait_ge(ctr_ready, 1 + hd + 1)
                            act.wait_ge(o_ready, 1 + hd)
                            act.activation(ptc[:, :], bank[6][0:NCMP, :], ACT.Copy).then_inc(cpt_ready, 1)
                    if u == HPG - 1:
                        high_out(1)

            for p in range(4):
                high_a(A_WO + p + 1)

            def tile_is(s):
                return lambda e, m: e.wait_ge(tile_free, 2 * s + m + 1)

            squares(N_FFN1, tile_is(A_WO))
            root(N_FFN1)
            high_hn(N_FFN1)
            ffn(A_FF1, B_FF1, E_FF1, FF_TILES // 2)
            squares(N_FINAL, y_is(B_MRG))
            root(N_FINAL)
            squares(N_MIX2, lambda e, m: e.wait_ge(hn_scaled, KT * N_FINAL + m + 1))
            root(N_MIX2)
            act.wait_ge(hn_rounded, KT * N_FINAL)
            act.sem_inc(hn_rounded, KT)
            high_hn(N_MIX2)

            high_a(A_SKV + 1)
            act.wait_ge(qk_raw, 1)
            act.activation(sq[:, 0, :], sk[:, :], ACT.Square).then_inc(qk_sq, 1)
            act.wait_ge(qk_mm, 1)
            act.activation(sd[:, :], bank[4][:, :], ACT.Sqrt, bias=eps, scale=1.0 / SWA_HD).then_inc(qk_sd, 1)

            def root_w(m):
                act.wait_ge(qk_raw, m + 2)
                act.activation(sq[:, m % 2, :], tmp[:, m % 2, :], ACT.Square).then_inc(qk_sq, 1)
                act.wait_ge(qk_mm, m + 2)
                act.wait_ge(qk_norm, m + 1)
                act.activation(sd[:, :], bank[1][:, :], ACT.Sqrt, bias=eps, scale=1.0 / SWA_HD).then_inc(qk_sd, 1)

            high_a(A_SQ + 1)
            root_w(0)
            for m in range(SWA_TILES):
                if m + 1 < SWA_TILES:
                    high_a(A_SQ + m + 2)
                    root_w(m + 1)
                for half in range(2):
                    act.wait_ge(w_mx, 2 * m + half + 1)
                    for k, (t, k0, w, c) in enumerate(WIN):
                        act.activation(wp[:, half, c:c + w], wp[:, half, c:c + w], ACT.Exp,
                                       bias=wst[:, half, 4 + k:5 + k], accum_out=wst[:, half, 8 + k:9 + k])
                    act.activation(wst[:, half, 12:16], wst[:, half, 4:8], ACT.Exp,
                                   bias=smc("sink", 2 * m + half)).then_inc(w_exp, 1)
                for half in range(2):
                    act.wait_ge(w_tr, 1 + 2 * m + half + 1)
                    act.activation(wpt[:, half, 0:S], bank[6][:, :], ACT.Copy)
                    act.activation(wpt[:, half, S:7 * P], bank[7][:, 0:3 * P], ACT.Copy).then_inc(w_pt, 1)
                act.wait_ge(w_o, m + 1)
                act.activation(ys_hi[:, m, :], bank[3][:, :], ACT.Copy).then_inc(w_or, 1)

            with act.Fori(0, RET_H) as i:
                high_a(A_RET + 1, i)
                act.wait_ge(tile_ready, 2 * (A_RET + 1 + 2 * i) + 2)
                act.wait_ge(r_g, 1 + i)
                act.activation(rgs[:, :], bank[2 * ((A_RET + 1) % 2)][:, :], ACT.Silu).then_inc(r_gate, 1)
                high_a(A_RET + 2, i)
                act.wait_ge(r_c, i + 1)
                act.activation(sq[:, 0, :], ryc[:, :], ACT.Square).then_inc(r_sq, 1)
                act.wait_ge(r_var, i + 1)
                act.activation(sd[:, :], bank[7][:, :], ACT.Sqrt, bias=eps, scale=1.0 / P).then_inc(r_sd, 1)
                act.wait_ge(r_g, 1 + i + 1)
                act.activation(yr_hi[:, ds(i, 1), :].rearrange("p a s -> p (a s)"), ryc[:, :], ACT.Copy) \
                   .then_inc(r_rounded, 1)

            act.wait_ge(r_split, RET_H)
            with act.Fori(0, KT // 2) as i:
                for u in range(2):
                    s = A_MRG + u
                    n = s + 2 * i
                    high_a(s + 1, i)
                    high_b(B_MRG + u, i)
                    act.wait_ge(mg_sum, 1 + 2 * i + u)
                    for j in range(2):
                        act.wait_ge(tile_ready, 2 * n + j + 1)
                        act.activation(sq[:, j, :], bank[2 * (s % 2) + j][:, :], ACT.Sigmoid).then_inc(mg_gate, 1)
                    act.wait_ge(mg_sum, 1 + 2 * i + u + 1)
                    act.activation(mg_hi[:, ds(2 * i + u, 1), :].rearrange("p a s -> p (a s)"), tmp[:, 0, :],
                                   ACT.Copy).then_inc(mg_rounded, 1)
            for p in range(4):
                high_a(A_OUT + p + 1)
            squares(N_MOE, tile_is(A_OUT))
            root(N_MOE)
            high_hn(N_MOE)

            def high_token(c):
                act.wait_ge(nat_mm, c + 1)
                act.activation(nat_hi[:, c // 2, (c % 2) * 512:(c % 2 + 1) * 512], bank[4 + c % 4][:, :], ACT.Copy) \
                   .then_inc(nat_rounded, 1)

            for c in range(4):
                high_token(c)
            act.wait_ge(rt_in, 1)
            act.activation(rtg[:, 1, :, :], rtg[:, 0, :, :], ACT.Exp)
            act.activation(rt[:, 5, :], rt[:, 4, :], ACT.Exp).then_inc(rt_exp, 1)
            for c in range(4, 8):
                high_token(c)
            high_a(A_MOE)
            high_a(A_MOE + 1)

            def high_gather(it):
                x = slice((it % 2) * XB, (it % 2 + 1) * XB)
                for c in range(KT // 2):
                    k = GATHER[it] + c
                    act.wait_ge(side_mm, k + 1)
                    act.activation(hn_hi[:, 2 * c:2 * c + 2, x],
                                   bank[2 + k % 2].rearrange("p (f x) -> p f x", f=2), ACT.Copy) \
                       .then_inc(x_rounded, 1)

            def expert(it, i):
                sa, sb_ = A_MOE + 2 * EPG * it, B_MOE + 2 * EPG * it
                for f in range(2):
                    high_b(sb_ + f, i)
                for f in range(2):
                    n = sa + f + 2 * i
                    act.wait_ge(tile_ready, 2 * n + 2)
                    act.activation(xsg[:, f, :], bank[(sa + f) % 2][:, 0:XB], ACT.Silu).then_inc(gate_done, 1)
                    act.wait_ge(tile_free, 2 * n + 2)
                    act.activation(xhid_hi[:, f, :], xhid[:, f, :], ACT.Copy).then_inc(hid_rounded, 1)
                    high_a(sa + f + 2, i)

            high_gather(0)
            for it in range(XITEMS):
                expert(it, 0)
                if it + 1 < XITEMS:
                    high_gather(it + 1)
                else:
                    act.wait_ge(p_loaded, 16)
                    act.activation(ptr_hi[:, :, :], ptr[:, :, :], ACT.Copy).then_inc(p_rounded, 1)
                with act.Fori(1, EPG) as i:
                    expert(it, i)
                for hb in range(2):
                    act.wait_ge(y_ready, 4 * (B_MOE + 2 * EPG * (it + 1)) - 4 + 4 * hb)
                    for u in range(XSUB):
                        if it:
                            act.wait_ge(side_mm, SCATTER[it - 1] + KT)
                        act.activation(xy_hi[:, u, hb * 512:(hb + 1) * 512], bank[4 + 2 * u + hb][:, :], ACT.Copy) \
                           .then_inc(xy_rounded, 1)

            for m in range(KT):
                act.wait_ge(pg_done, m + 1)
                if m >= 2:
                    act.wait_ge(stat_mm, KT * N_PLE + m - 1)
                act.activation(sq[:, m % 2, :], ple[:, m, :], ACT.Square).then_inc(sq_ready, 1)
            root(N_PLE)
            squares(N_PLEG, lambda e, m: e.wait_ge(h_added, KT * (XITEMS - 1) + m + 1))
            root(N_PLEG)
            act.wait_ge(hn_rounded, KT * N_PLE)
            act.sem_inc(hn_rounded, KT)
            high_hn(N_PLEG)
            for p in range(4):
                s = A_PG + p
                if p < 3:
                    high_a(s + 1)
                for j in range(2):
                    m = 2 * p + j
                    act.wait_ge(tile_ready, 2 * s + j + 1)
                    act.wait_ge(tile_free, 2 * s + j - 1)
                    act.activation(pgs[:, j, :], bank[2 * (s % 2) + j][:, :], ACT.Sigmoid).then_inc(out_done, 1)

        @block.vector
        def _(dve):
            step = Steps(dve, dve_step)
            V = dve

            def low_a(s, i=0):
                n = s + 2 * i
                V.wait_ge(a_rounded, n + 1)
                V.tensor_tensor(a_lo[s % 2][:, :], a_raw[s % 2][:, :], a_hi[s % 2][:, :], ALU.subtract) \
                 .then_inc(a_ready, 1)

            def low_b(s, i=0):
                n = s + 2 * i
                V.wait_ge(b_rounded, n + 1)
                V.tensor_tensor(b_lo[s % 2][:, :], b_raw[s % 2][:, :], b_hi[s % 2][:, :], ALU.subtract) \
                 .then_inc(b_ready, 1)

            def inverse_root(q):
                V.wait_ge(sd_ready, q + 1)
                V.reciprocal(rstd[:, :], sd[:, :]).then_inc(dve_rstd, 1)
                V.wait_ge(dve_rstd, q + 1)

            def normalise(q, gain, root=True):
                if root:
                    inverse_root(q)

                def low(m):
                    V.wait_ge(hn_rounded, KT * q + m + 1)
                    V.tensor_tensor(hn_lo[:, m, :], tmp[:, m % 2, :], hn_hi[:, m, :], ALU.subtract) \
                     .then_inc(hn_ready, 1)

                for m in range(KT):
                    if m >= 2:
                        V.wait_ge(hn_ready, KT * q + m - 1)
                    V.scalar_tensor_tensor(tmp[:, m % 2, :], h[:, m, :], smc("gain", KT * gain + m), rstd[:, :],
                                           ALU.mult, ALU.mult).then_inc(hn_scaled, 1)
                    if m:
                        low(m - 1)
                low(KT - 1)

            low_a(A_RNN)
            V.wait_ge(consts, 16)
            V.tensor_copy(masks[:, 0, :], ident)
            V.tensor_copy(masks[:, 1, :], cnc("causal", P))
            V.wait_ge(params, 16)
            V.wait_ge(x_loaded, 16)
            normalise(N_MIX0, 0)

            V.wait_ge(sp_exp, 1)
            one, dif, zero = spt[:, 2, :], spt[:, 4, :], spt[:, 5, :]
            V.tensor_scalar(one, spt[:, 1, :], 1.0, None, ALU.add).then_inc(sp_one, 1)
            V.wait_ge(sp_one, 1)
            step(V.tensor_scalar(dif, one, -1.0, None, ALU.add))
            step(V.tensor_scalar(zero, dif, 0.0, None, ALU.is_equal))
            step(V.tensor_tensor(dif, dif, zero, ALU.add))
            step(V.reciprocal(dif, dif))
            V.wait_ge(sp_ln, 1)
            step(V.tensor_tensor(zero, zero, spt[:, 3, :], ALU.add))
            step(V.tensor_tensor(zero, zero, dif, ALU.mult))
            step(V.tensor_tensor(zero, zero, spt[:, 1, :], ALU.mult))
            step(V.tensor_scalar(dif, smc("lam", 0, RNN_BLOCKS, RNN_W), -1.0, 0.0, ALU.mult, ALU.max))
            step(V.tensor_tensor(dif, dif, zero, ALU.add))
            V.tensor_scalar(spt[:, 6, :], dif, 8.0, None, ALU.mult)
            V.tensor_scalar(spt[:, 7, :], dif, -8.0, None, ALU.mult).then_inc(sp_done, 1)

            def add_y(nb0):
                for m in range(KT):
                    V.wait_ge(y_ready, 4 * nb0 + m + 1)
                    V.tensor_tensor(h[:, m, :], h[:, m, :], bank[4 + m % 4][:, :], ALU.add).then_inc(y_free, 1)

            def one_minus_square(u, i):
                V.wait_ge(asq_done, 2 * i + u + 1)
                V.scalar_tensor_tensor(pp[:, u, :], mu[:, u, :], 1.0, pp[:, u, :], ALU.add, ALU.mult) \
                 .then_inc(m2_done, 1)

            def scan(u, i):
                V.wait_ge(bx_done, 2 * i + u + 1)
                V.tensor_tensor_scan(hs[:, u, :], aa[:, u, :], gx[:, u, :], 0.0, ALU.mult, ALU.add) \
                 .then_inc(scan_done, 1)

            def low_rnn(u, i):
                V.wait_ge(hid_rounded, 2 * i + u + 1)
                V.tensor_tensor(rhid_lo[0:RNN_W, u, :], hs[:, u, :], rhid_hi[0:RNN_W, u, :], ALU.subtract) \
                 .then_inc(hid_ready, 1)

            def low_rnn_b(i):
                for u in range(2):
                    V.wait_ge(b_rounded, 2 * i - 2 + u + 1)
                    V.tensor_tensor(b_lo[u][:, :], b_raw[u][:, :], b_hi[u][:, :], ALU.subtract).then_inc(b_ready, 1)

            def channel(u, i, last=None, peeled=False):
                n = 2 * i + u
                low_a(A_RNN + 1 + u, i)
                if last:
                    one_minus_square(*last)
                if u and not peeled:
                    add_y(2 * i - 2)
                V.wait_ge(xb_ready, n + 1)
                if not peeled:
                    V.wait_ge(gx_done, n - 1)
                ps = bank[2 * u][0:RNN_W, :]

                def tap(k):
                    return sm[0:RNN_W, ds(SM["conv_w"] + 4 * n + k, 1)]

                step(V.tensor_scalar(xc[:, u, :], ps, tap(3), sm[0:RNN_W, ds(SM["conv_b"] + n, 1)],
                                     ALU.mult, ALU.add))
                for k in (2, 1, 0):
                    d = 3 - k
                    ins = V.scalar_tensor_tensor(xc[:, u, d:S], ps[:, 0:S - d], tap(k), xc[:, u, d:S],
                                                 ALU.mult, ALU.add)
                    if k:
                        step(ins)
                ins.then_inc(xc_done, 1)
                V.wait_ge(xc_rounded, n + 1)
                V.tensor_tensor(xc_lo[:, u, :], xc[:, u, :], xc_hi[:, u, :], ALU.subtract).then_inc(xc_ready, 1)
                if last:
                    scan(*last)
                V.wait_ge(yb_ready, n + 1)
                if not peeled:
                    V.wait_ge(gelu_done, n - 1)
                V.tensor_copy(ybr[:, u, :], bank[2 * u + 1][0:RNN_W, :]).then_inc(yb_copied, 1)
                if u == 0 and not peeled:
                    low_rnn_b(i)
                if last:
                    low_rnn(*last)

            channel(0, 0, peeled=True)
            channel(1, 0, (0, 0), peeled=True)
            step.enter(0, 6)
            with V.Fori(1, RNN_BLOCKS // 2) as i:
                step.i = i - 1
                channel(0, i, (1, i - 1))
                channel(1, i, (0, i))
            step.leave(RNN_BLOCKS // 2 - 1)
            last = (1, RNN_BLOCKS // 2 - 1)
            one_minus_square(*last)
            low_rnn_b(RNN_BLOCKS // 2)
            scan(*last)
            low_rnn(*last)
            add_y(RNN_BLOCKS - 2)

            def ffn(sa, sb_, e, trips):
                with V.Fori(0, trips) as i:
                    for f in range(2):
                        n = sa + f + 2 * i
                        low_a(sa + f + 1, i)
                        low_b(sb_ + f, i)
                        V.wait_ge(gate_done, 2 * (e - E_FF0 + i) + f + 1)
                        V.wait_ge(tile_ready, 2 * n + 2)
                        V.tensor_tensor(hid[:, f, :], sg[:, f, :], bank[2 * ((sa + f) % 2) + 1][:, :], ALU.mult) \
                         .then_inc(tile_free, 2)
                        V.wait_ge(hid_rounded, 2 * (e + i) + f + 1)
                        V.tensor_tensor(hid_lo[:, f, :], hid[:, f, :], hid_hi[:, f, :], ALU.subtract) \
                         .then_inc(hid_ready, 1)
                    add_y(sb_ + 2 * i)

            normalise(N_FFN0, 1)
            ffn(A_FF0, B_FF0, E_FF0, FF_TILES // 2)

            normalise(N_KV, 2)

            def tile(s, j, n=None):
                V.wait_ge(tile_ready, 2 * (s if n is None else n) + j + 1)
                return bank[2 * (s % 2) + j]

            for p in range(2):
                low_a(A_KCMP + p + 1)
                for j in range(2):
                    b = tile(A_KCMP + p, j)
                    V.tensor_copy(kraw[:, 2 * p + j, :], b[0:DQK, :]).then_inc(tile_free, 1)
            low_a(A_VCMP + 1)
            for j in range(2):
                b = tile(A_VCMP, j)
                V.tensor_copy(vraw[:, 2 * j, :], b[0:DV, :])
                V.tensor_copy(vraw[:, 2 * j + 1, :], b[DV:P, :]).then_inc(tile_free, 1)
            V.wait_ge(rope_loaded, 16)

            def rotate(r, bk, x, out):
                V.wait_ge(rope_mm, r + 1)
                if r:
                    V.wait_ge(rope_done, r)
                step(V.tensor_tensor(rtmp[:, 0, :], bank[bk][0:DQK, :], cs[:, 1, :], ALU.mult))
                step(V.tensor_tensor(rtmp[:, 1, :], x, cs[:, 0, :], ALU.mult))
                V.tensor_tensor(out, rtmp[:, 0, :], rtmp[:, 1, :], ALU.add).then_inc(rope_done, 1)

            for b in range(2):
                for p in range(2):
                    s = A_KSEL + 2 * b + p
                    low_a(s + 1)
                    for j in range(2):
                        V.tensor_copy(kx[:, b, 2 * p + j, :], tile(s, j)[0:DQK, :]).then_inc(tile_free, 1)
                    for j in range(2):
                        r = 4 * b + 2 * p + j
                        rotate(r, 4 + r % 2, kx[:, b, 2 * p + j, :], kx[:, b, 2 * p + j, :])
            for b in range(2):
                s = A_VNAT + b
                low_a(s + 1)
                for j in range(2):
                    V.tensor_copy(vn[:, b, 2 * j:2 * j + 2, :],
                                  tile(s, j)[:, :].rearrange("p (t c) -> p t c", t=2)).then_inc(tile_free, 1)
            def low_pos(ph):
                rows, half = (DQK, DV)[ph // 2], 4 - 4 * (ph % 2)
                V.wait_ge(xl_rounded, ph + 1)
                V.tensor_tensor(hn_lo[0:rows, half:half + 4, :], xpos[0:rows, :, :], hn_hi[0:rows, half:half + 4, :],
                                ALU.subtract).then_inc(xl_ready, 1)

            def add_pos(ph):
                src, pos, rows = ((kraw, "pos_k", DQK), (vraw, "pos_v", DV))[ph // 2]
                V.wait_ge(tile_ready, 2 * (A_W1K + (0, 0, 4, 4)[ph]))
                if ph:
                    V.wait_ge(xl_ready, ph)
                v = smc(pos, CSTRIDE * (ph % 2), CSTRIDE, rows).rearrange("p (o l) -> p o l", o=1)
                V.tensor_tensor(xpos[0:rows, :, :].rearrange("p g (c l) -> p (g c) l", l=CSTRIDE),
                                src[:, :, :].rearrange("p g (c l) -> p (g c) l", l=CSTRIDE),
                                v.to_broadcast([rows, GROUPS * S // CSTRIDE, CSTRIDE]), ALU.add).then_inc(xl_done, 1)

            def keep_k():
                V.wait_ge(cmp_w2, 1)
                V.tensor_copy(kct[:, :].rearrange("p (g c) -> p g c", g=GROUPS),
                              bank[6][0:DQK, 0:P].rearrange("p (g c) -> p g c", g=GROUPS)[:, :, 0:NCMP]) \
                 .then_inc(cmp_done, 1)

            add_pos(0)
            low_pos(0)
            for ph in range(4):
                low_a(A_W1K + 2 * ph + 1)
                if ph < 3:
                    add_pos(ph + 1)
                    low_pos(ph + 1)
                low_a(A_W1K + 2 * ph + 2)
            keep_k()
            V.sem_inc(tile_free, 16)

            def copy_narrow(s, width):
                V.wait_ge(tile_ready, 2 * s + 1)
                V.tensor_copy(sd[0:width, :], bank[2 * (s % 2)][0:width, :]).then_inc(narrow_copied, 1)

            V.sem_inc(dve_rstd, 1)
            normalise(N_MIX1, 3, root=False)
            low_a(A_GATE + 1)
            copy_narrow(A_GATE, NGATE)
            V.wait_ge(cmp_w2, 2)
            V.tensor_copy(vcn[:, :, :], bank[7][0:NCMP, 0:GROUPS * DV]
                          .rearrange("p (g c) -> p g c", g=GROUPS)).then_inc(cmp_done, 1)
            V.wait_ge(tile_ready, 2 * A_GATE + 2)
            step(V.tensor_tensor(gates[:, :, :], bank[2 * (A_GATE % 2) + 1][:, 0:NT * NGATE]
                                 .rearrange("p (t c) -> p t c", t=NT),
                                 smc("gate_b", 0, NT * NGATE).rearrange("p (t c) -> p t c", t=NT), ALU.add))
            V.sem_inc(gates_in, 1)
            V.sem_inc(tile_free, 2)
            step.enter(0, 8)
            with V.Fori(0, HEADS // 4) as i:
                step.i = i
                for u in range(2):
                    s = A_Q + u
                    n = s + 2 * i
                    low_a(s + 1, i)
                    for j in range(2):
                        v = 2 * u + j
                        b = tile(s, j, n)
                        V.wait_ge(q_free, 2 * i + u + 1)
                        V.tensor_scalar(qb[:, v, 0, :], b[0:DQK, :], DQK ** -0.5, None, ALU.mult) \
                         .then_inc(tile_free, 1)
                    V.wait_ge(tile_free, 2 * n + 2)
                    for j in range(2):
                        v = 2 * u + j
                        V.wait_ge(rope_mm, 8 + 4 * i + v + 1)
                        V.wait_ge(rope_done, 8 + 4 * i + v)
                        step(V.tensor_tensor(rtmp[:, 0, :], bank[4 + v % 2][0:DQK, :], cs[:, 1, :], ALU.mult))
                        step(V.tensor_tensor(rtmp[:, 1, :], qb[:, v, 0, :], cs[:, 0, :], ALU.mult))
                        V.tensor_tensor(qb[:, v, 1, :], rtmp[:, 0, :], rtmp[:, 1, :], ALU.add).then_inc(rope_done, 1)
            step.leave(HEADS // 4)

            V.wait_ge(gates_done, 1)
            step.enter(0, HPG * (8 + 4 * 2))
            with V.Fori(0, GROUPS) as g:
                step.i = g

                def low_out(pair):
                    V.wait_ge(o_rounded, 2 * g + pair + 1)
                    m = ds(2 * g + pair, 1)
                    V.tensor_tensor(hn_lo[:, m, :].rearrange("p a s -> p (a s)"), bank[7][:, :],
                                    hn_hi[:, m, :].rearrange("p a s -> p (a s)"), ALU.subtract) \
                     .then_inc(o_split, 1)

                for u in range(HPG):
                    hd = HPG * g + u

                    def gate(t, b, n=1):
                        return gates[:, t:t + n, ds(3 * hd + b, 1)]

                    def peak(t):
                        V.wait_ge(sc_ready, 4 * hd + t + 1)
                        V.wait_ge(pm_ready, 1 + 4 * hd + t - 1 if t >= 2 else 1 + 4 * hd)
                        V.tensor_reduce(ast[:, t % 2, 0:2], psum[:, 2 * (t % 2):2 * (t % 2) + 2, 0:(t + 1) * P],
                                        AX_X, ALU.max, negate=True).then_inc(mx_done, 1)

                    def weigh(t):
                        n = (t + 1) * P
                        V.wait_ge(exp_done, 1 + 4 * hd + t + 1)
                        step(V.reciprocal(ast[:, t % 2, 4:6], ast[:, t % 2, 2:4]))
                        step(V.tensor_tensor(ast[:, t % 2, 6:8], ast[:, t % 2, 4:6],
                                             gates[:, t:t + 1, ds(3 * hd + 1, 2)].rearrange("p a o -> p (a o)"),
                                             ALU.mult))
                        for b in range(2):
                            ins = V.tensor_scalar(pm[:, t % 2, b, 0:n], pm[:, t % 2, b, 0:n],
                                                  ast[:, t % 2, 6 + b:7 + b], None, ALU.mult)
                        ins.then_inc(pm_ready, 1)

                    peak(0)
                    peak(1)
                    V.wait_ge(csc_ready, hd + 1)
                    V.wait_ge(ctr_ready, 1 + hd)
                    step(V.tensor_tensor(pc[:, :, :], bank[6][:, 0:124].rearrange("p (t c) -> p t c", t=NT),
                                         cnc("cmp_mask", 124).rearrange("p (t c) -> p t c", t=NT), ALU.add))
                    step(V.tensor_reduce(cst[:, 0, :], pc[:, :, :], AX_X, ALU.max))
                    step(V.tensor_scalar(cst[:, 1, :], cst[:, 0, :], -1e20, None, ALU.max))
                    V.tensor_tensor(pc[:, :, :], pc[:, :, :],
                                    cst[:, 1, :].rearrange("p (t o) -> p t o", o=1).to_broadcast([P, NT, NCMP]),
                                    ALU.subtract).then_inc(csub_done, 1)

                    weigh(0)
                    peak(2)
                    if u == 2:
                        low_out(0)
                    V.wait_ge(cexp_done, hd + 1)
                    step(V.tensor_reduce(cst[:, 2, :], pc[:, :, :], AX_X, ALU.add))
                    step(V.tensor_scalar(cst[:, 2, :], cst[:, 2, :], 1e-30, None, ALU.max))
                    step(V.reciprocal(cst[:, 3, :], cst[:, 2, :]))
                    step(V.tensor_tensor(cst[:, 3, :], cst[:, 3, :],
                                         gate(0, 0, NT).rearrange("p a o -> p (a o)"), ALU.mult))
                    step(V.tensor_tensor(pc[:, :, :], pc[:, :, :],
                                    cst[:, 3, :].rearrange("p (t o) -> p t o", o=1).to_broadcast([P, NT, NCMP]),
                                    ALU.mult))
                    V.sem_inc(cpm_ready, 1)
                    for t in range(1, NT):
                        weigh(t)
                        if t + 2 < NT:
                            peak(t + 2)
                    if u == HPG - 1:
                        low_out(1)
            step.leave(GROUPS)

            def add_tiles(s0):
                for p in range(4):
                    s = s0 + p
                    low_a(s + 1)
                    for j in range(2):
                        m = 2 * p + j
                        V.tensor_tensor(h[:, m, :], h[:, m, :], tile(s, j)[:, :], ALU.add).then_inc(tile_free, 1)

            add_tiles(A_WO)
            normalise(N_FFN1, 4)
            ffn(A_FF1, B_FF1, E_FF1, FF_TILES // 2)

            inverse_root(N_FINAL)
            for m in range(KT):
                V.scalar_tensor_tensor(h[:, m, :], h[:, m, :], smc("gain", KT * 5 + m), rstd[:, :],
                                       ALU.mult, ALU.mult).then_inc(hn_scaled, 1)
            V.wait_ge(hn_scaled, KT * (N_FINAL + 1))
            V.sem_inc(hn_ready, KT)
            normalise(N_MIX2, 6)

            low_a(A_SKV + 1)
            V.tensor_copy(sk[:, :], tile(A_SKV, 0)[:, :]).then_inc(qk_raw, 1)
            V.tensor_copy(tmp[:, 1, :], tile(A_SKV, 1)[:, :]).then_inc(v_copied, 1)

            def qk_scale(dst, src, gain, k):
                V.wait_ge(qk_sd, k)
                step(V.reciprocal(rstd[:, :], sd[:, :]))
                V.scalar_tensor_tensor(dst, src, smc(gain), rstd[:, :], ALU.mult, ALU.mult).then_inc(qk_norm, 1)

            qk_scale(sk[:, :], sk[:, :], "k_g", 1)
            V.wait_ge(v_turned, 1)
            V.tensor_copy(sv[:, :, :], tile(A_SKV, 1)[:, :].rearrange("p (t c) -> p t c", t=NT)) \
             .then_inc(tile_free, 2)
            V.wait_ge(alibi_loaded, 16)

            def raw_w(m):
                s = A_SQ + m
                low_a(s + 1)
                V.wait_ge(tile_ready, 2 * s + 2)
                if m >= 2:
                    V.wait_ge(qk_norm, m)
                V.tensor_copy(tmp[:, m % 2, :], bank[2 * (s % 2)][:, :]).then_inc(tile_free, 2)
                V.wait_ge(tile_free, 2 * s + 2)
                V.sem_inc(qk_raw, 1)

            def scale_w(m):
                if m:
                    V.wait_ge(w_sc, 2 * m)
                qk_scale(qn[:, :], tmp[:, m % 2, :], "q_g", m + 2)

            def peak_w(m, half):
                it = 2 * m + half
                V.wait_ge(w_sc, it + 1)
                if m:
                    V.wait_ge(w_tr, 1 + it - 1)
                bias = al[:, it:it + 1, :]
                for (c, n, b) in ((0, 2, 4), (S, 1, 5)):
                    step(V.scalar_tensor_tensor(
                        wp[:, half, c:c + n * 2 * P].rearrange("p (n w) -> p n w", n=n),
                        bank[b][:, 0:n * 2 * P].rearrange("p (n w) -> p n w", n=n), SWA_HD ** -0.5,
                        bias.to_broadcast([P, n, 2 * P]), ALU.mult, ALU.add))
                step(V.scalar_tensor_tensor(wp[:, half, 6 * P:7 * P], bank[5][:, 2 * P:3 * P], SWA_HD ** -0.5,
                                            al[:, it, P:2 * P], ALU.mult, ALU.add))
                step(V.tensor_reduce(wst[:, half, 0:3], wp[:, half, 0:6 * P].rearrange("p (t w) -> p t w", t=3),
                                     AX_X, ALU.max))
                step(V.tensor_reduce(wst[:, half, 3:4], wp[:, half, 6 * P:7 * P], AX_X, ALU.max))
                V.tensor_scalar(wst[:, half, 4:8], wst[:, half, 0:4], smc("sink", it), -1.0,
                                ALU.max, ALU.mult).then_inc(w_mx, 1)

            def weigh_w(m, half):
                V.wait_ge(w_exp, 1 + 2 * m + half + 1)
                step(V.tensor_tensor(wst[:, half, 8:12], wst[:, half, 8:12], wst[:, half, 12:16], ALU.add))
                step(V.reciprocal(wst[:, half, 16:20], wst[:, half, 8:12]))
                for k, (t, k0, w, c) in enumerate(WIN):
                    ins = V.tensor_scalar(wp[:, half, c:c + w], wp[:, half, c:c + w],
                                          wst[:, half, 16 + k:17 + k], None, ALU.mult)
                ins.then_inc(w_pm, 1)

            raw_w(0)
            scale_w(0)
            raw_w(1)
            for m in range(SWA_TILES):
                peak_w(m, 0)
                peak_w(m, 1)
                weigh_w(m, 0)
                if m + 1 < SWA_TILES:
                    scale_w(m + 1)
                weigh_w(m, 1)
                if m + 2 < SWA_TILES:
                    raw_w(m + 2)
                V.wait_ge(w_or, m + 1)
                V.tensor_tensor(ys_lo[:, m, :], bank[3][:, :], ys_hi[:, m, :], ALU.subtract).then_inc(w_os, 1)

            V.wait_ge(decay_loaded, 16)
            step.enter(0, 3)
            with V.Fori(0, RET_H) as i:
                step.i = i
                low_a(A_RET + 1, i)
                V.tensor_copy(rq[:, :], tile(A_RET, 0, A_RET + 2 * i)[:, :]).then_inc(tile_free, 1)
                V.tensor_copy(rk[:, :], tile(A_RET, 1, A_RET + 2 * i)[:, :]).then_inc(tile_free, 1)
                V.wait_ge(tile_ready, 2 * (A_RET + 1 + 2 * i) + 1)
                b = bank[2 * ((A_RET + 1) % 2) + 1]
                V.tensor_copy(tmp[:, 0, :], b[:, :]).then_inc(v_copied, 1)
                V.wait_ge(v_turned, 2 + i)
                V.tensor_copy(rv[:, :], b[:, :]).then_inc(r_v, 1)
                for j in range(4):
                    V.wait_ge(r_sc, 4 * i + j + 1)
                    V.wait_ge(r_o, 1 + 4 * i + max(j - 1, 0))
                    V.tensor_tensor(srt[:, j % 2, 0:S - j * P], bank[4 + j % 2][:, 0:S - j * P],
                                    dk[:, ds(i, 1), 0:S - j * P].rearrange("p a s -> p (a s)"), ALU.mult) \
                     .then_inc(r_dec, 1)
                V.wait_ge(r_o, 1 + 4 * i + 4)
                V.tensor_copy(ry[:, :], bank[6][:, :]).then_inc(r_y, 1)
                V.wait_ge(r_mean, i + 1)
                V.wait_ge(r_rounded, 1 + i)
                V.scalar_tensor_tensor(ryc[:, :], bank[7][:, :], -1.0 / P, ry[:, :], ALU.mult, ALU.add) \
                 .then_inc(r_c, 1)
                V.wait_ge(r_v, i + 1)
                V.wait_ge(r_gate, i + 1)
                V.sem_inc(tile_free, 2)
                low_a(A_RET + 2, i)
                V.wait_ge(r_sd, i + 1)
                step(V.reciprocal(rstd[:, :], sd[:, :]))
                step(V.scalar_tensor_tensor(ryc[:, :], ryc[:, :], sm[:, ds(SM["ret_g"] + i, 1)], rstd[:, :],
                                            ALU.mult, ALU.mult))
                V.scalar_tensor_tensor(ryc[:, :], ryc[:, :], sm[:, ds(SM["ret_b"] + i, 1)], rgs[:, :],
                                       ALU.add, ALU.mult).then_inc(r_g, 1)
                V.wait_ge(r_rounded, 1 + i + 1)
                step(V.tensor_tensor(yr_lo[:, ds(i, 1), :].rearrange("p a s -> p (a s)"), ryc[:, :],
                                     yr_hi[:, ds(i, 1), :].rearrange("p a s -> p (a s)"), ALU.subtract))
                V.sem_inc(r_split, 1)
            step.leave(RET_H)

            step.enter(0, 4)
            with V.Fori(0, KT // 2) as i:
                step.i = i
                for u in range(2):
                    s = A_MRG + u
                    n = s + 2 * i
                    nb = B_MRG + u + 2 * i
                    low_a(s + 1, i)
                    low_b(B_MRG + u, i)
                    V.wait_ge(mg_gate, 2 * (2 * i + u) + 2)
                    V.wait_ge(y_ready, 4 * nb + 2)
                    V.wait_ge(mg_ready, 1 + 2 * i + u)
                    step(V.tensor_tensor(tmp[:, 1, :], bank[4 + 2 * u][:, :], sq[:, 0, :], ALU.mult))
                    V.wait_ge(y_ready, 4 * nb + 4)
                    step(V.tensor_tensor(tmp[:, 0, :], bank[5 + 2 * u][:, :], sq[:, 1, :], ALU.mult))
                    V.sem_inc(tile_free, 2)
                    V.sem_inc(y_free, 4)
                    V.tensor_tensor(tmp[:, 0, :], tmp[:, 0, :], tmp[:, 1, :], ALU.add).then_inc(mg_sum, 1)
                    V.wait_ge(mg_rounded, 2 * i + u + 1)
                    V.tensor_tensor(mg_lo[:, ds(2 * i + u, 1), :].rearrange("p a s -> p (a s)"), tmp[:, 0, :],
                                    mg_hi[:, ds(2 * i + u, 1), :].rearrange("p a s -> p (a s)"), ALU.subtract) \
                     .then_inc(mg_ready, 1)
            step.leave(KT // 2)
            add_tiles(A_OUT)
            normalise(N_MOE, 7)

            V.tensor_copy(ident_r[:, :], ident).then_inc(ident_ready, 1)
            copy_narrow(A_ROUTE, NROUTE)
            V.wait_ge(tile_ready, 2 * A_ROUTE + 2)
            step(V.tensor_tensor(logit[:, :, :], bank[2 * (A_ROUTE % 2) + 1][:, 0:NT * NROUTE]
                                 .rearrange("p (t c) -> p t c", t=NT),
                                 smc("route_b", 0, NT * NROUTE).rearrange("p (t c) -> p t c", t=NT), ALU.add))
            V.sem_inc(tile_free, 2)

            def wide(x, n):
                return x.rearrange("p (t o) -> p t o", o=1).to_broadcast([P, NT, n])

            def best(dst, mark, x, prio, n, top):
                step(V.tensor_reduce(top, x, AX_X, ALU.max))
                step(V.tensor_tensor(mark, x, wide(top, n), ALU.is_ge))
                step(V.tensor_tensor(mark, mark, prio, ALU.mult))
                step(V.tensor_reduce(rt[:, 0, :], mark, AX_X, ALU.max))
                step(V.tensor_tensor(dst, mark, wide(rt[:, 0, :], n), ALU.is_equal))

            gl = logit[:, :, 0:EGROUPS]
            pg = cnc("prio_g", NT * EGROUPS).rearrange("p (t c) -> p t c", t=NT)
            pe_ = cnc("prio_e", NT * EPG).rearrange("p (t c) -> p t c", t=NT)
            best(rtg[:, 2, :, :], rtg[:, 3, :, :], gl, pg, EGROUPS, rt[:, 1, :])
            V.sem_inc(marks_ready, 1)

            def low_token(c):
                cols = slice((c % 2) * 512, (c % 2 + 1) * 512)
                V.wait_ge(nat_rounded, c + 1)
                V.tensor_tensor(nat_lo[:, c // 2, cols], bank[4 + c % 4][:, :], nat_hi[:, c // 2, cols], ALU.subtract) \
                 .then_inc(nat_ready, 1)

            for c in range(4):
                low_token(c)
            step(V.tensor_tensor(rtg[:, 0, :, :], gl, wide(rt[:, 1, :], EGROUPS), ALU.subtract))
            V.wait_ge(rank_mm, 1)
            step(V.tensor_copy(rank[:, :, :], bank[3][:, 0:NT * EGROUPS].rearrange("p (t g) -> p t g", t=NT)))
            step(V.tensor_copy(grp[:, 0, :], bank[3][:, NT * EGROUPS:(NT + 1) * EGROUPS]))
            step(V.tensor_scalar(grp[:, 1, :], grp[:, 0, :], 0.5, None, ALU.is_ge))
            step(V.tensor_scalar(grp[:, 2, :], grp[:, 0, :], XB + 0.5, None, ALU.is_ge))
            step(V.tensor_tensor(grp[:, 3, :], grp[:, 1, :], grp[:, 2, :], ALU.add))
            step(V.tensor_copy(grp[:, 4, :], grp[:, 3, :]))
            for g in range(1, EGROUPS):
                step(V.tensor_tensor(grp[:, 4, g:g + 1], grp[:, 4, g - 1:g], grp[:, 3, g:g + 1], ALU.add))
            for g in range(3):
                step(V.tensor_scalar(item[:, g, 0:XITEMS], cnc("iota", XITEMS), grp[:, 4, g:g + 1], None, ALU.is_ge))
            step(V.tensor_tensor(item[:, 0, 0:XITEMS], item[:, 0, 0:XITEMS], item[:, 1, 0:XITEMS], ALU.add))
            step(V.tensor_tensor(item[:, 0, 0:XITEMS], item[:, 0, 0:XITEMS], item[:, 2, 0:XITEMS], ALU.add))
            V.tensor_copy(item_group[:, 0:XITEMS], item[:, 0, 0:XITEMS]).then_inc(groups_ready, 1)
            step(V.tensor_tensor(grp[:, 5, :], grp[:, 4, :], grp[:, 3, :], ALU.subtract))
            step(V.tensor_scalar(grp[:, 6, :], grp[:, 5, :], float(XB), -1.0, ALU.mult, ALU.add))
            step(V.tensor_tensor(rank[:, :, :], rank[:, :, :],
                                 grp[:, 6:7, :].to_broadcast([P, NT, EGROUPS]), ALU.add))
            step(V.tensor_tensor(rank[:, :, :], rank[:, :, :], rtg[:, 2, :, :], ALU.mult))
            step(V.tensor_reduce(slot[:, :], rank[:, :, :], AX_X, ALU.add))
            for t in range(NT):
                ins = V.tensor_scalar(slot_wide[:, t * P:(t + 1) * P], ones, slot[:, t:t + 1], None, ALU.mult)
            ins.then_inc(wide_ready, 1)

            for g in range(EGROUPS):
                lg = logit[:, :, EGROUPS + g * EPG:EGROUPS + (g + 1) * EPG]
                mark = rtg[:, 2, :, g:g + 1].to_broadcast([P, NT, EPG])
                dst = rte[:, 0, :, :] if g == 0 else rte[:, 1, :, :]
                step(V.tensor_tensor(dst, lg, mark, ALU.mult))
                if g:
                    step(V.tensor_tensor(rte[:, 0, :, :], rte[:, 0, :, :], rte[:, 1, :, :], ALU.add))
            best(rte[:, 2, :, :], rte[:, 3, :, :], rte[:, 0, :, :], pe_, EPG, rt[:, 2, :])
            step(V.tensor_scalar(rte[:, 4, :, :], rte[:, 2, :, :], 2 * NEG, None, ALU.mult))
            step(V.tensor_tensor(rte[:, 4, :, :], rte[:, 4, :, :], rte[:, 0, :, :], ALU.add))
            best(rte[:, 5, :, :], rte[:, 6, :, :], rte[:, 4, :, :], pe_, EPG, rt[:, 3, :])
            step(V.tensor_tensor(rt[:, 4, :], rt[:, 3, :], rt[:, 2, :], ALU.subtract))
            V.sem_inc(rt_in, 1)
            V.wait_ge(rt_exp, 1)
            step(V.tensor_reduce(rt[:, 6, :], rtg[:, 1, :, :], AX_X, ALU.add))
            step(V.tensor_scalar(rt[:, 7, :], rt[:, 5, :], 1.0, None, ALU.add))
            step(V.tensor_tensor(rt[:, 8, :], rt[:, 6, :], rt[:, 7, :], ALU.mult))
            step(V.reciprocal(rt[:, 9, :], rt[:, 8, :]))
            step(V.tensor_tensor(rt[:, 10, :], rt[:, 9, :], rt[:, 5, :], ALU.mult))
            step(V.tensor_tensor(rte[:, 7, :, :], rte[:, 2, :, :], wide(rt[:, 9, :], EPG), ALU.mult))
            step(V.tensor_tensor(rte[:, 8, :, :], rte[:, 5, :, :], wide(rt[:, 10, :], EPG), ALU.mult))
            step(V.tensor_tensor(rte[:, 9, :, :], rte[:, 7, :, :], rte[:, 8, :, :], ALU.add))
            step(V.tensor_copy(w_hi[:, :, :], rte[:, 9, :, :]))
            step(V.tensor_tensor(w_lo[:, :, :], rte[:, 9, :, :], w_hi[:, :, :], ALU.subtract))

            def select(it):
                for t in range(NT):
                    ins = V.tensor_scalar(sel[:, t, :], cnc("iota", XB), slot[:, t:t + 1], -float(XB * it),
                                          ALU.subtract, ALU.is_equal)
                ins.then_inc(sel_ready, 1)

            def low_gather(it):
                x = slice((it % 2) * XB, (it % 2 + 1) * XB)
                for c in range(KT // 2):
                    k = GATHER[it] + c
                    V.wait_ge(x_rounded, KT // 2 * it + c + 1)
                    V.tensor_tensor(hn_lo[:, 2 * c:2 * c + 2, x], bank[2 + k % 2].rearrange("p (f x) -> p f x", f=2),
                                    hn_hi[:, 2 * c:2 * c + 2, x], ALU.subtract).then_inc(side_free, 1)
                k = GATHER[it] + KT // 2
                V.wait_ge(side_mm, k + 1)
                if it:
                    V.wait_ge(wslot_stored, 16 * it)
                V.tensor_copy(wslot[:, :], bank[2 + k % 2][0:EPG, 0:XB]).then_inc(wslot_done, 1)
                V.wait_ge(wslot_done, it + 1)
                V.sem_inc(side_free, 1)

            def select_t(it):
                if it:
                    V.wait_ge(side_mm, SCATTER[it - 1] + KT)
                for u in range(XSUB):
                    c = CN["slot_id"] + XSUB * it + u
                    ins = V.tensor_scalar(sel_t[:, u, :], slot_row[:, :], cn[:, c:c + 1], None, ALU.is_equal)
                ins.then_inc(sel_t_ready, 1)

            def add_block(it):
                for m in range(KT):
                    k = SCATTER[it] + m
                    V.wait_ge(side_mm, k + 1)
                    V.tensor_tensor(h[:, m, :], h[:, m, :], bank[2 + k % 2][:, :], ALU.add).then_inc(h_added, 1)
                    V.wait_ge(h_added, KT * it + m + 1)
                    V.sem_inc(side_free, 1)

            def expert(it, i):
                sa, sb_ = A_MOE + 2 * EPG * it, B_MOE + 2 * EPG * it
                for f in range(2):
                    low_b(sb_ + f, i)
                for f in range(2):
                    n = sa + f + 2 * i
                    V.wait_ge(gate_done, 2 * (E_MOE - E_FF0 + EPG * it + i) + f + 1)
                    if f == 0:
                        V.wait_ge(comb_loaded, 16 * (EPG * it + i) + 16)
                    step(V.tensor_tensor(xsg[:, f, :], xsg[:, f, :], xcomb, ALU.mult))
                    V.wait_ge(tile_ready, 2 * n + 2)
                    V.tensor_tensor(xhid[:, f, :], xsg[:, f, :], bank[(sa + f) % 2][:, XB:2 * XB], ALU.mult) \
                     .then_inc(tile_free, 2)
                    V.wait_ge(hid_rounded, 2 * (E_MOE + EPG * it + i) + f + 1)
                    V.tensor_tensor(xhid_lo[:, f, :], xhid[:, f, :], xhid_hi[:, f, :], ALU.subtract) \
                     .then_inc(hid_ready, 1)
                    low_a(sa + f + 2, i)

            select(0)
            for c in range(4, 8):
                low_token(c)
            low_a(A_MOE)
            low_gather(0)
            low_a(A_MOE + 1)
            V.wait_ge(rank_mm, 2)
            V.tensor_copy(slot_row[:, :], bank[2][:, :]).then_inc(wide_ready, 1)
            for it in range(XITEMS):
                if it:
                    select_t(it - 1)
                if it + 1 < XITEMS:
                    select(it + 1)
                expert(it, 0)
                if it:
                    add_block(it - 1)
                if it + 1 < XITEMS:
                    low_gather(it + 1)
                else:
                    V.wait_ge(p_rounded, 1)
                    V.tensor_tensor(ptr_lo[:, :, :], ptr[:, :, :], ptr_hi[:, :, :], ALU.subtract).then_inc(p_ready, 1)
                step.enter(1, 2)
                step.base -= 2
                with V.Fori(1, EPG) as i:
                    step.i = i
                    expert(it, i)
                step.leave(EPG)
                for hb in range(2):
                    for u in range(XSUB):
                        V.wait_ge(xy_rounded, 4 * it + XSUB * hb + u + 1)
                        V.tensor_tensor(xy_lo[:, u, hb * 512:(hb + 1) * 512], bank[4 + 2 * u + hb][:, :],
                                        xy_hi[:, u, hb * 512:(hb + 1) * 512], ALU.subtract).then_inc(xy_ready, 1)
            select_t(XITEMS - 1)
            add_block(XITEMS - 1)

            for m in range(KT):
                V.wait_ge(ple_mm, m + 1)
                V.tensor_copy(ple[:, m, :], bank[5 + m % 2][:, :]).then_inc(pg_done, 1)
            V.wait_ge(pg_done, KT)
            V.sem_inc(tile_free, 2)
            inverse_root(N_PLE)
            for m in range(KT):
                ins = V.scalar_tensor_tensor(ple[:, m, :], ple[:, m, :], smc("gain", KT * 9 + m), rstd[:, :],
                                             ALU.mult, ALU.mult)
            step(ins)
            V.sem_inc(hn_scaled, KT)
            V.sem_inc(hn_ready, KT)
            normalise(N_PLEG, 8)
            for p in range(4):
                s = A_PG + p
                if p < 3:
                    low_a(s + 1)
                for j in range(2):
                    m = 2 * p + j
                    V.wait_ge(out_done, m + 1)
                    step(V.tensor_tensor(ple[:, m, :], ple[:, m, :], pgs[:, j, :], ALU.mult))
                    V.tensor_tensor(h[:, m, :], h[:, m, :], ple[:, m, :], ALU.add).then_inc(tile_free, 1)

        @block.gpsimd
        def _(pool):
            with pool.Fori(0, RNN_BLOCKS // 2) as i:
                for u in range(2):
                    n = 2 * i + u
                    pool.wait_ge(xc_done, n + 1)
                    pool.wait_ge(tile_free, 2 * n + 2)
                    pool.tensor_tensor(gx[:, u, :], ig[:, u, :], xc[:, u, :], ALU.mult).then_inc(gx_done, 1)
                    pool.wait_ge(decay_done, 2 * n + 2)
                    pool.tensor_tensor(mu[:, u, :], aa[:, u, :], aa[:, u, :], ALU.mult).then_inc(asq_done, 1)
                    pool.wait_ge(mult_done, n + 1)
                    pool.wait_ge(gx_done, n + 1)
                    pool.tensor_tensor(gx[:, u, :], gx[:, u, :], mu[:, u, :], ALU.mult).then_inc(bx_done, 1)
                    pool.wait_ge(scan_done, n + 1)
                    pool.wait_ge(gelu_done, n + 1)
                    pool.tensor_tensor(hs[:, u, :], hs[:, u, :], gel[:, u, :], ALU.mult).then_inc(rec_done, 1)

            pool.wait_ge(hn_ready, KT * (N_KV + 1))
            pool.dma_start(cs[:, :, :], rope).then_inc(rope_loaded, 16)
            def store_q(i):
                for u in range(2):
                    pool.wait_ge(rope_done, 8 + 4 * i + 2 * u + 2)
                    pool.dma_start(q_dram[ds(4 * i + 2 * u, 2)].rearrange("a p n -> p a n"),
                                   qb[:, 2 * u:2 * u + 2, :, :].rearrange("p a b n -> p a (b n)")) \
                        .then_inc(q_stored[u], 16)
                    pool.wait_ge(q_stored[u], 16 * i + 16)
                    pool.sem_inc(q_free, 1)
            def stage_q(u, g, wait=True):
                if wait:
                    pool.wait_ge(sc_ready, 4 * (HPG * g + u - 1))
                pool.dma_start(qs[:, u % 2, :, :].rearrange("p b n -> p (b n)"),
                               q_dram[ds(HPG * g + u, 1)].rearrange("a p n -> p (a n)")) \
                    .then_inc(q_staged[u % 2], 16)

            def stage_v(g):
                pool.wait_ge(o_ready, 1 + HPG * g)
                for b in range(2):
                    pool.tensor_copy(vs[:, b, :, :], vn[:, b, :, ds(g * DV, DV)]).then_inc(v_staged, 1)
                pool.tensor_copy(vcs[:, :], vcn[:, ds(g, 1), :].rearrange("p a c -> p (a c)")).then_inc(v_staged, 1)

            with pool.Fori(0, HEADS // 4 - 1) as i:
                store_q(i)
            stage_q(0, 0, wait=False)
            stage_q(1, 0, wait=False)
            store_q(HEADS // 4 - 1)
            with pool.Fori(0, GROUPS - 1) as g:
                stage_v(g)
                for u in range(2, HPG + 2):
                    stage_q(u, g)
            stage_v(GROUPS - 1)
            for u in range(2, HPG):
                stage_q(u, GROUPS - 1)

            pool.wait_ge(hn_ready, KT * (N_MIX2 + 1))
            pool.dma_start(al[:, :, :], alibi).then_inc(alibi_loaded, 16)
            pool.wait_ge(w_os, 1 + SWA_TILES)
            pool.dma_start(dk[:, :, :], decay).then_inc(decay_loaded, 16)

            for it in range(XITEMS):
                if it == XITEMS - 1:
                    pool.wait_ge(side_free, GATHER[it] + KT // 2 + 1)
                    pool.dma_start(ptr[:, :, :], p_t.rearrange("(k p) s -> p k s", p=P)).then_inc(p_loaded, 16)
                pool.wait_ge(wslot_done, it + 1)
                pool.dma_start(c_dram[EPG * it:EPG * (it + 1), :], wslot[:, :]).then_inc(wslot_stored, 16)
                pool.wait_ge(wslot_stored, 16 * it + 16)
                with pool.Fori(0, EPG) as i:
                    pool.wait_ge(tile_free, 2 * (A_MOE + 2 * EPG * it + 2 * i))
                    pool.dma_start(xcomb, c_dram[ds(EPG * it + i, 1), :].to_broadcast([P, XB])) \
                        .then_inc(comb_loaded, 16)

            out_v = out_t.rearrange("(k p) s -> p k s", p=P)
            for m in range(KT):
                pool.wait_ge(tile_free, 2 * A_PG + m + 1)
                pool.dma_start(out_v[:, m, :], h[:, m, :]).then_inc(stored, 16)
            pool.wait_ge(stored, 16 * KT)


def _pack_a(v):
    out = np.zeros((v.shape[0], P, WA), np.float32)
    out[:, :v.shape[1], :v.shape[2]] = v
    return out


def _cols(w, groups):
    k = w.shape[0] // P
    t = w.reshape(k, P, -1)
    return _pack_a(np.stack([np.concatenate([t[:, :, c] for c in g], 2).transpose(1, 0, 2).reshape(P, -1)
                             for g in groups]))


def _pairs(w, width, step=2):
    n = w.shape[1] // width
    return _cols(w, [[slice(i * width, (i + step) * width)] for i in range(0, n, step)])


def _down(w, rows):
    v = w.reshape(-1, 2, rows, 2, 512).transpose(0, 3, 2, 1, 4).reshape(-1, rows, WB)
    out = np.zeros((v.shape[0], P, WB), np.float32)
    out[:, :rows] = v
    return out


def _panels(x):
    a = []
    w_in = x["a_w_in"][0]
    gates = np.concatenate([x["a_w_ra"][0], x["a_w_ix"][0]], 2)
    rnn = _cols(w_in, [[slice(c * RNN_W, (c + 1) * RNN_W), slice(1536 + c * RNN_W, 1536 + (c + 1) * RNN_W)]
                       for c in range(RNN_BLOCKS)])
    rnn[:, :RNN_W, 1536:1728] = gates
    a.append(rnn)

    def ff(w):
        n = w.shape[1] // 2
        return _cols(w, [[slice(f * P, (f + 1) * P), slice(n + f * P, n + (f + 1) * P)] for f in range(n // P)])

    a.append(ff(x["ffn_w_gu"][0]))
    kc, vc, ks, vs, kw, vw = np.split(x["kv_w"], np.cumsum([384, 256, 384, 256, 384])[:5], 1)
    a += [_pairs(kc, DQK), _pairs(vc, P), _pairs(ks, DQK), _pairs(kw, DQK), _cols(vs, [[slice(0, 256)]]),
          _cols(vw, [[slice(0, 256)]])]
    for w, d in ((x["cmp_w1_k"], DQK), (x["cmp_w1_v"], DV)):
        a.append(_pack_a(w.reshape(4, 8, d, 256).transpose(0, 2, 1, 3).reshape(4, d, 2048)))
    w_q = x["b_w_q"][0]
    a += [_cols(w_q, [[slice(HEADS * DQK, HEADS * DQK + NGATE)]]), _pairs(w_q[:, :HEADS * DQK], DQK)]
    a.append(_pairs(x["b_w_o"][0], P))
    a.append(ff(x["ffn_w_gu"][1]))
    rq, rk, rv, rg, sq, sk, sv, gr, gs = np.split(
        x["w_in_2"][0], np.cumsum([512, 512, 512, 512, 512, 128, 128, 1024]), 1)
    order = np.concatenate([np.arange(64 * q, 64 * q + 64) for m in range(4) for q in (m, m + 4)])
    a.append(_cols(np.concatenate([sk, sv], 1), [[slice(0, 256)]]))
    sqp = np.zeros((D, 1024), np.float32)
    for m in range(4):
        sqp[:, m * 256:m * 256 + 128] = sq[:, order[m * 128:(m + 1) * 128]]
    a.append(_pairs(sqp, P))
    ret = np.concatenate([rq, rk, rg, rv], 1)
    a.append(_cols(ret, [[slice(o + i * P, o + (i + 1) * P), slice(o + 512 + i * P, o + 512 + (i + 1) * P)]
                         for i in range(RET_H) for o in (0, 1024)]))
    a.append(_cols(np.concatenate([gr, gs], 1), [[slice(m * P, (m + 1) * P), slice(D + m * P, D + (m + 1) * P)]
                                                 for m in range(KT)]))
    a.append(_pairs(x["w_out_2"][0], P))
    a.append(_cols(np.concatenate([x["w_router_group_2"][0], x["w_router_expert_2"][0]], 1),
                   [[slice(0, NROUTE)]]))
    eg, eu = x["w_exp_gate_2"][0], x["w_exp_up_2"][0]
    v = np.stack([eg.reshape(EXPERTS, KT, P, 2, P), eu.reshape(EXPERTS, KT, P, 2, P)], 4)
    a.append(v.transpose(0, 3, 2, 1, 4, 5).reshape(2 * EXPERTS, P, WA))
    a.append(_cols(x["w_ple_2"][0], [[slice(0, D)]]))
    a.append(_pairs(x["w_ple_gate_2"][0], P))
    w_a = np.concatenate(a)
    assert w_a.shape == (NA - REPEATED, P, WA), w_a.shape
    ret_o = x["w_ret_o_2"][0].reshape(4, P, KT, P).transpose(2, 1, 0, 3).reshape(KT, P, 512)
    swa_o = x["w_swa_o_2"][0][order].reshape(4, P, KT, P).transpose(2, 1, 0, 3).reshape(KT, P, 512)
    b = [_down(x["a_w_out"][0], RNN_W), _down(x["ffn_w_down"][0], P), _down(x["ffn_w_down"][1], P),
         np.concatenate([ret_o, swa_o], 2), _down(x["w_exp_down_2"][0].reshape(EXPERTS * EFF, D), P)]
    w_b = np.concatenate(b)
    assert w_b.shape == (NB - REPEATED, P, WB), w_b.shape
    return w_a, w_b


def _small(x):
    out = np.zeros((P, N_SMALL), np.float32)

    def put(name, v):
        out[:v.shape[0], SM[name]:SM[name] + v.shape[1]] = v

    gains = [x["norm_g"][0, 0], x["norm_g"][0, 1], x["kv_norm_g"], x["norm_g"][1, 0], x["norm_g"][1, 1],
             x["final_g"], x["mix_norm_g_2"][0], x["ffn_norm_g_2"][0], x["ple_gate_norm_g_2"][0],
             x["ple_norm_g_2"][0]]
    put("gain", np.concatenate([g.reshape(KT, P).T for g in gains], 1))
    put("conv_w", x["a_conv_w"][0].reshape(4, RNN_BLOCKS, RNN_W).transpose(2, 1, 0).reshape(RNN_W, -1))
    put("conv_b", x["a_conv_b"][0].reshape(RNN_BLOCKS, RNN_W).T)
    put("b_ra", x["a_b_ra"][0].T)
    put("b_ix", x["a_b_ix"][0].T)
    put("lam", x["a_lambda"][0].reshape(RNN_BLOCKS, RNN_W).T)
    put("pos_k", x["cmp_pos_k"].T)
    put("pos_v", x["cmp_pos_v"].T)
    put("gate_b", np.broadcast_to(np.tile(x["b_gate_bias"][0], NT), (P, NT * NGATE)))
    put("ret_g", x["ret_gn_g_2"][0].reshape(RET_H, P).T)
    put("ret_b", x["ret_gn_b_2"][0].reshape(RET_H, P).T)
    put("q_g", np.tile(x["q_norm_g_2"][0], 2)[:, None])
    put("k_g", np.tile(x["k_norm_g_2"][0], 2)[:, None])
    put("sink", np.broadcast_to(x["attn_sinks_2"][0].reshape(2, 4).T.reshape(-1), (P, SWA_H)))
    put("route_b", np.broadcast_to(np.tile(np.concatenate(
        [x["b_router_group_2"][0], x["b_router_expert_2"][0]]), NT), (P, NT * NROUTE)))
    put("w2k", x["cmp_w2_k"].reshape(2, P, DQK).transpose(1, 0, 2).reshape(P, -1))
    put("w2v", x["cmp_w2_v"].reshape(2, P, DV).transpose(1, 0, 2).reshape(P, -1))
    return out


def _constants():
    out = np.zeros((P, N_CONST), np.float32)

    def put(name, v):
        out[:v.shape[0], CN[name]:CN[name] + v.shape[1]] = v

    r = np.arange(P)
    put("eps", np.full((P, 1), EPS))
    put("ident", np.eye(P))
    put("ones", np.ones((P, P)))
    put("halves", (r[:, None] // 64 == r[None, :] // 64).astype(np.float32))
    rot = np.zeros((DQK, DQK))
    for k in range(12):
        rot[k + 12, k] = 1.0
        rot[k, k + 12] = 1.0
    put("rot", rot)
    put("causal", np.where(r[None, :] <= r[:, None], 0.0, NEG))
    t = np.arange(S).reshape(NT, P)
    c_end = np.arange(NCMP) * CSTRIDE + CBLOCK - 1
    put("cmp_mask", np.where(c_end[None, None, :] <= t[:, :, None], 0.0, NEG)
        .transpose(1, 0, 2).reshape(P, -1))
    put("prio_g", np.tile(EGROUPS - np.arange(EGROUPS), (P, NT)))
    put("prio_e", np.tile(EPG - np.arange(EPG), (P, NT)))
    put("upto", (r[:, None] <= r[None, :]).astype(np.float32))
    put("iota", np.tile(np.arange(XB), (P, 1)))
    put("slot_id", r[:, None] + P * np.arange(XITEMS * XSUB)[None, :])

    inv = np.float32(500000.0) ** (-np.arange(12, dtype=np.float32) * np.float32(2.0) / np.float32(24))
    ang = (np.arange(S, dtype=np.float32)[:, None] * inv[None, :].astype(np.float32)).astype(np.float64)
    rope = np.zeros((DQK, 2, S), np.float32)
    rope[:, 0] = 1.0
    rope[:12, 0] = rope[12:24, 0] = np.cos(ang).T
    rope[:12, 1] = -np.sin(ang).T
    rope[12:24, 1] = np.sin(ang).T

    c = np.arange(S)
    decay = np.zeros((P, RET_H, S))
    for i in range(RET_H):
        lg = np.log1p(-2.0 ** (-5.0 - i))
        d = c[None, :] - r[:, None]
        decay[:, i] = np.where(d >= 0, np.exp(np.maximum(d, 0) * lg), 0.0) * 128 ** -0.5
    alibi = np.zeros((P, SWA_H, 2 * P))
    rel = r[:, None] + P - np.arange(2 * P)[None, :]
    for m in range(4):
        for half in range(2):
            slope = 2.0 ** (-(m + 4 * half + 1.0))
            alibi[:, 2 * m + half] = np.where((rel >= 0) & (rel < P), -slope * rel, NEG)
    return out, rope, decay.astype(np.float32), alibi.astype(np.float32)


def kernel(**inputs):
    import concourse.bacc as bacc
    from concourse.bass_utils import run_bass_kernel_spmd

    x = {k: np.asarray(v) for k, v in inputs.items()}
    w_a, w_b = _panels(x)
    const, rope, decay, alibi = _constants()
    arrays = {
        "x_t": np.ascontiguousarray(x["x"][0].T), "p_t": np.ascontiguousarray(x["p_2"][0, 0].T),
        "w_a": w_a, "w_b": w_b, "small": _small(x), "const": const, "rope": rope, "decay": decay, "alibi": alibi,
    }
    nc = bacc.Bacc("TRN2", target_bir_lowering=False, num_devices=1)
    aps = [nc.dram_tensor(k, v.shape, F32, kind="ExternalInput").ap() for k, v in arrays.items()]
    out = nc.dram_tensor("out_t", (D, S), F32, kind="ExternalOutput").ap()
    build(nc, *aps, out)
    r = run_bass_kernel_spmd(nc, [arrays], core_ids=[0])
    return r.results[0]["out_t"].T[None]
```
